# Optimizing a Trainium2 kernel written in Bass

```python
import math
import jax, jax.numpy as jnp
from jax import lax
import numpy as np
import jax
import jax.numpy as jnp

D_MODEL = 1024
BATCH = 1
SEQ = 256
DEPTH = 2

D_FF = 2816
EPS = 1e-6
FOURIER_GROUPS = 8
FOURIER_GROUP_DIM = 128
FOURIER_WIDTH = FOURIER_GROUPS * FOURIER_GROUP_DIM
DIL_PAIRS = ((128, 1), (512, 4), (2048, 16))
DIL_HEADS_PER_GROUP = 2
DIL_HEAD_DIM = 64
DIL_HEADS = DIL_HEADS_PER_GROUP * len(DIL_PAIRS)
DIL_WIDTH = DIL_HEADS * DIL_HEAD_DIM
DIL_OUT_WIDTH = DIL_HEADS_PER_GROUP * DIL_HEAD_DIM
DIFF_HEADS = 4
DIFF_HEAD_DIM = 64
DIFF_QK_WIDTH = DIFF_HEADS * 2 * DIFF_HEAD_DIM
DIFF_V_DIM = 2 * DIFF_HEAD_DIM
DIFF_V_WIDTH = DIFF_HEADS * DIFF_V_DIM
SUBLN_EPS = 1e-5
Q_BLOCK = 128
IN_WIDTH = FOURIER_WIDTH + 3 * DIL_WIDTH + 2 * DIFF_QK_WIDTH + DIFF_V_WIDTH
N_BRANCHES = 3
NUM_BUCKETS = 32
MAX_DISTANCE = 1024
N_BIAS_HEADS = DIL_HEADS + DIFF_HEADS
NEG_INF = -1e30


def rmsnorm(x, g, eps=EPS):
    xf = x.astype(jnp.float32)
    y = xf * lax.rsqrt(jnp.mean(xf * xf, axis=-1, keepdims=True) + eps)
    return (y * g.astype(jnp.float32)).astype(x.dtype)

def swiglu(h, w_gate, w_up, w_down):
    return (jax.nn.silu(h @ w_gate) * (h @ w_up)) @ w_down

def rel_bucket(rel):
    half = NUM_BUCKETS // 2
    max_exact = half // 2
    ret = jnp.where(rel > 0, half, 0)
    n = jnp.abs(rel)
    nf = jnp.maximum(n, 1).astype(jnp.float32)
    large = max_exact + (jnp.log(nf / max_exact) / math.log(MAX_DISTANCE / max_exact)
                         * (half - max_exact)).astype(jnp.int32)
    large = jnp.minimum(large, half - 1)
    return ret + jnp.where(n < max_exact, n, large)

def fourier_mix(a):
    Bsz, S, _ = a.shape
    ag = a.astype(jnp.float32).reshape(Bsz, S, FOURIER_GROUPS, FOURIER_GROUP_DIM)
    y = jnp.fft.fftn(ag, axes=(1, 3), norm="ortho").real
    return y.reshape(Bsz, S, FOURIER_WIDTH).astype(a.dtype)

def dilated_window_attention(q, k, v, bias_cols, window, dil):
    Bsz, S, H, dh = q.shape
    radius = window // (2 * dil)
    blk = radius
    L = S // dil
    nb = -(-L // blk)
    Lp = nb * blk

    def to_sub(t):
        t = t.reshape(Bsz, L, dil, H, dh).transpose(0, 2, 3, 1, 4)
        return jnp.pad(t, ((0, 0), (0, 0), (0, 0), (0, Lp - L), (0, 0)))

    def windows(t):
        tp = jnp.pad(to_sub(t), ((0, 0), (0, 0), (0, 0), (blk, blk), (0, 0)))
        tp = tp.reshape(Bsz, dil, H, nb + 2, blk, dh)
        return jnp.concatenate([tp[:, :, :, :-2], tp[:, :, :, 1:-1], tp[:, :, :, 2:]], axis=4)

    qs = to_sub(q).reshape(Bsz, dil, H, nb, blk, dh).astype(jnp.float32)
    kw = windows(k).astype(jnp.float32)
    vw = windows(v).astype(jnp.float32)

    i = jnp.arange(blk)[:, None]
    m = jnp.arange(3 * blk)[None, :]
    rel_t = m - blk - i
    bias = bias_cols[rel_bucket(rel_t * dil)].astype(jnp.float32)
    bias = jnp.transpose(bias, (2, 0, 1))
    tk = (jnp.arange(nb)[:, None, None] - 1) * blk + m[None]
    valid = (jnp.abs(rel_t) <= radius)[None] & (tk >= 0) & (tk < L)

    logits = jnp.einsum('bdhjqc,bdhjkc->bdhjqk', qs, kw) * (dh ** -0.5)
    logits = logits + bias[None, None, :, None]
    logits = jnp.where(valid, logits, NEG_INF)
    lse = jax.nn.logsumexp(logits, axis=-1)
    p = jnp.exp(logits - lse[..., None])
    o = jnp.einsum('bdhjqk,bdhjkc->bdhjqc', p, vw)

    o = o.reshape(Bsz, dil, H, Lp, dh)[:, :, :, :L].transpose(0, 3, 1, 2, 4).reshape(Bsz, S, H, dh)
    lse = lse.reshape(Bsz, dil, H, Lp)[:, :, :, :L].transpose(0, 3, 1, 2).reshape(Bsz, S, H)
    return o, lse

def dilated_mixture(qb, kb, vb, rel_bias):
    Bsz, S, _ = qb.shape
    q = qb.reshape(Bsz, S, DIL_HEADS, DIL_HEAD_DIM)
    k = kb.reshape(Bsz, S, DIL_HEADS, DIL_HEAD_DIM)
    v = vb.reshape(Bsz, S, DIL_HEADS, DIL_HEAD_DIM)
    outs, lses = [], []
    for g, (window, dil) in enumerate(DIL_PAIRS):
        hs = slice(g * DIL_HEADS_PER_GROUP, (g + 1) * DIL_HEADS_PER_GROUP)
        o, lse = dilated_window_attention(q[:, :, hs], k[:, :, hs], v[:, :, hs],
                                          rel_bias[:, hs], window, dil)
        outs.append(o)
        lses.append(lse)
    o = jnp.stack(outs, axis=0)
    w = jax.nn.softmax(jnp.stack(lses, axis=0), axis=0)
    y = jnp.sum(w[..., None] * o, axis=0)
    return y.reshape(Bsz, S, DIL_OUT_WIDTH).astype(qb.dtype)

def diff_attention(qc, kc, vc, bias_cols, lam, subln_g, lam_init):
    Bsz, S, _ = qc.shape
    H, dh = DIFF_HEADS, DIFF_HEAD_DIM
    nq = S // Q_BLOCK
    qb = qc.reshape(Bsz, nq, Q_BLOCK, H, 2, dh).transpose(1, 0, 2, 3, 4, 5).astype(jnp.float32)
    kf = kc.reshape(Bsz, S, H, 2, dh).astype(jnp.float32)
    vf = vc.reshape(Bsz, S, H, DIFF_V_DIM).astype(jnp.float32)
    kpos = jnp.arange(S)
    scale = dh ** -0.5

    def one_block(args):
        j, qj = args
        qpos = j * Q_BLOCK + jnp.arange(Q_BLOCK)
        bias = bias_cols[rel_bucket(kpos[None, :] - qpos[:, None])].astype(jnp.float32)
        bias = jnp.transpose(bias, (2, 0, 1))
        logits = jnp.einsum('bqhmc,bkhmc->bhmqk', qj, kf) * scale + bias[None, :, None]
        p = jax.nn.softmax(logits, axis=-1)
        a = p[:, :, 0] - lam * p[:, :, 1]
        return jnp.einsum('bhqk,bkhe->bqhe', a, vf)

    o = lax.map(one_block, (jnp.arange(nq), qb))
    o = o.transpose(1, 0, 2, 3, 4).reshape(Bsz, S, H, DIFF_V_DIM)
    o = rmsnorm(o, subln_g, SUBLN_EPS) * (1.0 - lam_init)
    return o.reshape(Bsz, S, DIFF_V_WIDTH).astype(qc.dtype)

def first_inputs(seed: int = 0) -> dict:
    key = jax.random.key(seed)
    ks = jax.random.split(key, 26)

    def nrm(k, shape, fan_in):
        return jax.random.normal(k, shape, jnp.float32) * (fan_in ** -0.5)

    def gain(k, shape):
        return 1.0 + 0.05 * jax.random.normal(k, shape, jnp.float32)

    L = DEPTH
    return {
        "x": jax.random.normal(ks[0], (BATCH, SEQ, D_MODEL), jnp.float32),
        "g_ffn1": gain(ks[1], (L, D_MODEL)),
        "w_ffn1_gate": nrm(ks[2], (L, D_MODEL, D_FF), D_MODEL),
        "w_ffn1_up": nrm(ks[3], (L, D_MODEL, D_FF), D_MODEL),
        "w_ffn1_down": nrm(ks[4], (L, D_FF, D_MODEL), D_FF),
        "g_mix": gain(ks[5], (L, D_MODEL)),
        "w_in": nrm(ks[6], (L, D_MODEL, IN_WIDTH), D_MODEL),
        "w_gate": nrm(ks[7], (L, D_MODEL, N_BRANCHES * D_MODEL), D_MODEL),
        "b_gate": 0.02 * jax.random.normal(ks[8], (L, N_BRANCHES * D_MODEL), jnp.float32),
        "w_br_a": nrm(ks[9], (L, FOURIER_WIDTH, D_MODEL), FOURIER_WIDTH),
        "w_br_b": nrm(ks[10], (L, DIL_OUT_WIDTH, D_MODEL), DIL_OUT_WIDTH),
        "w_br_c": nrm(ks[11], (L, DIFF_V_WIDTH, D_MODEL), DIFF_V_WIDTH),
        "w_out": nrm(ks[12], (L, D_MODEL, D_MODEL), D_MODEL),
        "lam_q1": 0.1 * jax.random.normal(ks[13], (L, DIFF_HEAD_DIM), jnp.float32),
        "lam_k1": 0.1 * jax.random.normal(ks[14], (L, DIFF_HEAD_DIM), jnp.float32),
        "lam_q2": 0.1 * jax.random.normal(ks[15], (L, DIFF_HEAD_DIM), jnp.float32),
        "lam_k2": 0.1 * jax.random.normal(ks[16], (L, DIFF_HEAD_DIM), jnp.float32),
        "subln_g": gain(ks[17], (L, DIFF_V_DIM)),
        "rel_bias": 0.5 * jax.random.normal(ks[18], (NUM_BUCKETS, N_BIAS_HEADS), jnp.float32),
        "g_ffn2": gain(ks[19], (L, D_MODEL)),
        "w_ffn2_gate": nrm(ks[20], (L, D_MODEL, D_FF), D_MODEL),
        "w_ffn2_up": nrm(ks[21], (L, D_MODEL, D_FF), D_MODEL),
        "w_ffn2_down": nrm(ks[22], (L, D_FF, D_MODEL), D_FF),
        "g_final": gain(ks[23], (D_MODEL,)),
    }

def first_block(x, g_ffn1, w_ffn1_gate, w_ffn1_up, w_ffn1_down, g_mix, w_in, w_gate, b_gate,
              w_br_a, w_br_b, w_br_c, w_out, lam_q1, lam_k1, lam_q2, lam_k2, subln_g,
              rel_bias, g_ffn2, w_ffn2_gate, w_ffn2_up, w_ffn2_down, g_final):
    Bsz, S, D = x.shape
    c0 = FOURIER_WIDTH
    c1 = c0 + DIL_WIDTH
    c2 = c1 + DIL_WIDTH
    c3 = c2 + DIL_WIDTH
    c4 = c3 + DIFF_QK_WIDTH
    c5 = c4 + DIFF_QK_WIDTH
    for l in range(DEPTH):
        x = x + 0.5 * swiglu(rmsnorm(x, g_ffn1[l]), w_ffn1_gate[l], w_ffn1_up[l], w_ffn1_down[l])

        u = rmsnorm(x, g_mix[l])
        p = u @ w_in[l]
        a_in = p[..., :c0]
        qb, kb, vb = p[..., c0:c1], p[..., c1:c2], p[..., c2:c3]
        qc, kc, vc = p[..., c3:c4], p[..., c4:c5], p[..., c5:]

        y_a = fourier_mix(a_in) @ w_br_a[l]
        y_b = dilated_mixture(qb, kb, vb, rel_bias[:, :DIL_HEADS]) @ w_br_b[l]
        lam_init = 0.8 - 0.6 * math.exp(-0.3 * l)
        lam = (jnp.exp(jnp.sum(lam_q1[l].astype(jnp.float32) * lam_k1[l].astype(jnp.float32)))
               - jnp.exp(jnp.sum(lam_q2[l].astype(jnp.float32) * lam_k2[l].astype(jnp.float32)))
               + lam_init)
        y_c = diff_attention(qc, kc, vc, rel_bias[:, DIL_HEADS:], lam, subln_g[l], lam_init) @ w_br_c[l]

        gates = jax.nn.sigmoid(u @ w_gate[l] + b_gate[l]).reshape(Bsz, S, N_BRANCHES, D)
        merged = gates[:, :, 0] * y_a + gates[:, :, 1] * y_b + gates[:, :, 2] * y_c
        x = x + merged @ w_out[l]

        x = x + 0.5 * swiglu(rmsnorm(x, g_ffn2[l]), w_ffn2_gate[l], w_ffn2_up[l], w_ffn2_down[l])
    return rmsnorm(x, g_final)


DEPTH_2 = 1

MOBA_HEADS = 8
MOBA_HEAD_DIM = 128
MOBA_WIDTH = MOBA_HEADS * MOBA_HEAD_DIM
MOBA_BLOCK = 256
MOBA_TOPK = 3
MOBA_QCHUNK = 32
ROPE_DIM = MOBA_HEAD_DIM // 4
ROPE_THETA = 500000.0

GLA_HEADS = 4
GLA_KEY_DIM = D_MODEL // 2
GLA_VAL_DIM = D_MODEL
GLA_DK = GLA_KEY_DIM // GLA_HEADS
GLA_DV = GLA_VAL_DIM // GLA_HEADS
GLA_GATE_RANK = 16
GLA_GATE_NORMALIZER = 16.0
GLA_CHUNK = 64

N_EXPERTS = 32
TOP_K = 4
D_EXPERT = D_MODEL
SWIGLU_ALPHA = 1.702
SWIGLU_LIMIT = 7.0
EXPERT_ROW_BLOCK = 128

RMS_EPS = 1e-5
N_BRANCHES_2 = 2
IN_SPLITS = (MOBA_WIDTH, MOBA_WIDTH, MOBA_WIDTH, GLA_KEY_DIM, GLA_KEY_DIM, GLA_VAL_DIM, GLA_VAL_DIM, GLA_GATE_RANK, D_MODEL, D_MODEL)
N_IN = 3 * MOBA_WIDTH + 2 * GLA_KEY_DIM + 2 * GLA_VAL_DIM + GLA_GATE_RANK + N_BRANCHES_2 * D_MODEL


def _rmsnorm(x, w):
    xf = x.astype(jnp.float32)
    y = xf * lax.rsqrt(jnp.mean(xf * xf, axis=-1, keepdims=True) + RMS_EPS)
    return (y * w.astype(jnp.float32)).astype(x.dtype)

def _partial_rope(x):
    S = x.shape[1]
    half = ROPE_DIM // 2
    inv_freq = jnp.float32(ROPE_THETA) ** (-jnp.arange(half, dtype=jnp.float32) * 2.0 / ROPE_DIM)
    ang = jnp.arange(S, dtype=jnp.float32)[:, None] * inv_freq[None, :]
    cos = jnp.cos(ang)[None, :, None, :]
    sin = jnp.sin(ang)[None, :, None, :]
    xr = x[..., :ROPE_DIM].astype(jnp.float32)
    x1, x2 = xr[..., :half], xr[..., half:]
    rot = jnp.concatenate([x1 * cos - x2 * sin, x2 * cos + x1 * sin], axis=-1).astype(x.dtype)
    return jnp.concatenate([rot, x[..., ROPE_DIM:]], axis=-1)

def _moba_attention(q, k, v):
    B, S, H, Dh = q.shape
    n_blocks = -(-S // MOBA_BLOCK)
    s_pad = n_blocks * MOBA_BLOCK
    topk = min(MOBA_TOPK, n_blocks)
    scale = Dh ** -0.5

    def prep(t):
        t = jnp.pad(t, ((0, 0), (0, s_pad - S), (0, 0), (0, 0)))
        return t.transpose(0, 2, 1, 3)

    qh, kh, vh = prep(q), prep(k), prep(v)
    kb = kh.reshape(B, H, n_blocks, MOBA_BLOCK, Dh)
    vb = vh.reshape(B, H, n_blocks, MOBA_BLOCK, Dh)
    k_mean = jnp.mean(kb.astype(jnp.float32), axis=3)
    b_idx = jnp.arange(B)[:, None, None, None]
    h_idx = jnp.arange(H)[None, :, None, None]
    block_ids = jnp.arange(n_blocks)

    def query_chunk(ci):
        start = ci * MOBA_QCHUNK
        blk = start // MOBA_BLOCK
        qc = lax.dynamic_slice_in_dim(qh, start, MOBA_QCHUNK, axis=2)
        gate = jnp.einsum('bhqd,bhnd->bhqn', qc.astype(jnp.float32), k_mean)
        gate = jnp.where(block_ids < blk, gate, -jnp.inf)
        _, sel = lax.top_k(gate, topk)
        valid = sel < blk
        k_sel = kb[b_idx, h_idx, sel]
        v_sel = vb[b_idx, h_idx, sel]
        s_sel = jnp.einsum('bhqd,bhqnkd->bhqnk', qc, k_sel).astype(jnp.float32) * scale
        s_sel = jnp.where(valid[..., None], s_sel, -jnp.inf).reshape(B, H, MOBA_QCHUNK, topk * MOBA_BLOCK)
        k_own = lax.dynamic_index_in_dim(kb, blk, axis=2, keepdims=False)
        v_own = lax.dynamic_index_in_dim(vb, blk, axis=2, keepdims=False)
        s_own = jnp.einsum('bhqd,bhkd->bhqk', qc, k_own).astype(jnp.float32) * scale
        q_pos = start + jnp.arange(MOBA_QCHUNK)
        k_pos = blk * MOBA_BLOCK + jnp.arange(MOBA_BLOCK)
        s_own = jnp.where(k_pos[None, :] <= q_pos[:, None], s_own, -jnp.inf)
        p = jax.nn.softmax(jnp.concatenate([s_sel, s_own], axis=-1), axis=-1).astype(vh.dtype)
        p_sel = p[..., :topk * MOBA_BLOCK].reshape(B, H, MOBA_QCHUNK, topk, MOBA_BLOCK)
        p_own = p[..., topk * MOBA_BLOCK:]
        return (jnp.einsum('bhqnk,bhqnkd->bhqd', p_sel, v_sel)
                + jnp.einsum('bhqk,bhkd->bhqd', p_own, v_own))

    out = lax.map(query_chunk, jnp.arange(s_pad // MOBA_QCHUNK))
    out = out.transpose(1, 0, 3, 2, 4).reshape(B, s_pad, H, Dh)
    return out[:, :S]

def _gla_chunked(q, k, v, log_g):
    B, S, H, dk = q.shape
    dv = v.shape[-1]
    n_chunks = S // GLA_CHUNK

    def to_chunks(t):
        t = t.astype(jnp.float32).reshape(B, n_chunks, GLA_CHUNK, H, t.shape[-1])
        return t.transpose(1, 0, 3, 2, 4)

    qc = to_chunks(q) * (dk ** -0.5)
    kc, vc, gc = to_chunks(k), to_chunks(v), to_chunks(log_g)
    causal = jnp.tril(jnp.ones((GLA_CHUNK, GLA_CHUNK), dtype=bool))[:, :, None]

    def step(state, inp):
        qi, ki, vi, gi = inp
        b = jnp.cumsum(gi, axis=2)
        b_last = b[:, :, -1:, :]
        o_inter = jnp.einsum('bhcd,bhdv->bhcv', qi * jnp.exp(b), state)
        diff = b[:, :, :, None, :] - b[:, :, None, :, :]
        decay = jnp.exp(jnp.where(causal, diff, -jnp.inf))
        scores = jnp.einsum('bhid,bhjd,bhijd->bhij', qi, ki, decay)
        o = o_inter + jnp.einsum('bhij,bhjv->bhiv', scores, vi)
        state = (state * jnp.exp(b_last[:, :, 0, :, None])
                 + jnp.einsum('bhcd,bhcv->bhdv', ki * jnp.exp(b_last - b), vi))
        return state, o

    state0 = jnp.zeros((B, H, dk, dv), jnp.float32)
    _, o = lax.scan(step, state0, (qc, kc, vc, gc))
    return o.transpose(1, 0, 3, 2, 4).reshape(B, S, H, dv)

def _mixer(h, w_in, gla_gate_w, gla_gate_b, gla_norm_w, w_o_moba, w_o_gla, b_merge, w_out):
    B, S, _ = h.shape
    proj = h @ w_in
    idx = []
    acc = 0
    for size in IN_SPLITS[:-1]:
        acc += size
        idx.append(acc)
    mq, mk, mv, gq, gk, gv, gr, g_low, gate_a, gate_b = jnp.split(proj, idx, axis=-1)

    def heads(t, n):
        return t.reshape(B, S, n, -1)

    mq = _partial_rope(heads(mq, MOBA_HEADS))
    mk = _partial_rope(heads(mk, MOBA_HEADS))
    o_a = _moba_attention(mq, mk, heads(mv, MOBA_HEADS)).reshape(B, S, MOBA_WIDTH)
    y_a = o_a @ w_o_moba

    log_g = jax.nn.log_sigmoid((g_low @ gla_gate_w + gla_gate_b).astype(jnp.float32)) / GLA_GATE_NORMALIZER
    o_b = _gla_chunked(heads(gq, GLA_HEADS), heads(gk, GLA_HEADS), heads(gv, GLA_HEADS), heads(log_g, GLA_HEADS))
    o_b = _rmsnorm(o_b, gla_norm_w) * jax.nn.silu(heads(gr, GLA_HEADS).astype(jnp.float32))
    y_b = o_b.reshape(B, S, GLA_VAL_DIM).astype(h.dtype) @ w_o_gla

    g_a = jax.nn.sigmoid(gate_a + b_merge[:D_MODEL])
    g_b = jax.nn.sigmoid(gate_b + b_merge[D_MODEL:])
    return (g_a * y_a + g_b * y_b) @ w_out

def _clamped_swiglu(h):
    x_glu = jnp.minimum(h[..., ::2], SWIGLU_LIMIT)
    x_lin = jnp.clip(h[..., 1::2], -SWIGLU_LIMIT, SWIGLU_LIMIT)
    return x_glu * jax.nn.sigmoid(SWIGLU_ALPHA * x_glu) * (x_lin + 1.0)

def _moe(h, w_router, b_router, w_exp_in, b_exp_in, w_exp_out, b_exp_out):
    B, S, D = h.shape
    T = B * S
    R = EXPERT_ROW_BLOCK
    tokens = h.reshape(T, D)
    logits = (tokens @ w_router + b_router).astype(jnp.float32)
    top_logits, top_idx = lax.top_k(logits, TOP_K)
    top_w = jax.nn.softmax(top_logits, axis=-1)
    flat_expert = top_idx.reshape(-1)
    flat_token = jnp.arange(T * TOP_K, dtype=jnp.int32) // TOP_K
    flat_w = top_w.reshape(-1)
    order = jnp.argsort(flat_expert)
    sorted_expert = flat_expert[order]
    counts = jax.ops.segment_sum(jnp.ones_like(flat_expert), flat_expert, num_segments=N_EXPERTS)
    group_start = jnp.cumsum(counts) - counts
    padded_counts = (counts + R - 1) // R * R
    padded_end = jnp.cumsum(padded_counts)
    padded_start = padded_end - padded_counts
    rank = jnp.arange(T * TOP_K, dtype=jnp.int32) - group_start[sorted_expert]
    dest = padded_start[sorted_expert] + rank
    n_row_blocks = -(-(T * TOP_K + N_EXPERTS * (R - 1)) // R)
    P = n_row_blocks * R
    row_token = jnp.zeros((P,), jnp.int32).at[dest].set(flat_token[order])
    row_weight = jnp.zeros((P,), jnp.float32).at[dest].set(flat_w[order])
    block_expert = jnp.minimum(
        jnp.searchsorted(padded_end, jnp.arange(n_row_blocks) * R, side='right'), N_EXPERTS - 1)

    def expert_block(j):
        rows = lax.dynamic_slice_in_dim(row_token, j * R, R)
        wts = lax.dynamic_slice_in_dim(row_weight, j * R, R)
        e = block_expert[j]
        hid = tokens[rows] @ w_exp_in[e] + b_exp_in[e]
        out = _clamped_swiglu(hid) @ w_exp_out[e] + b_exp_out[e]
        return out * wts[:, None].astype(out.dtype)

    out = lax.map(expert_block, jnp.arange(n_row_blocks)).reshape(P, D)
    y = jnp.zeros((T, D), out.dtype).at[row_token].add(out)
    return y.reshape(B, S, D)

def second_inputs(seed: int = 0) -> dict:
    key = jax.random.key(seed)
    ks = jax.random.split(key, 21)
    L = DEPTH_2

    def nrm(k, shape, scale):
        return jax.random.normal(k, shape, jnp.float32) * scale

    return {
        'x': nrm(ks[0], (BATCH, SEQ, D_MODEL), 1.0),
        'c': nrm(ks[1], (BATCH, D_MODEL), 1.0),
        'w_ada': nrm(ks[2], (L, D_MODEL, 6 * D_MODEL), 0.5 * D_MODEL ** -0.5),
        'b_ada': nrm(ks[3], (L, 6 * D_MODEL), 0.01),
        'norm1_w': 1.0 + nrm(ks[4], (L, D_MODEL), 0.01),
        'w_in': nrm(ks[5], (L, D_MODEL, N_IN), D_MODEL ** -0.5),
        'gla_gate_w': nrm(ks[6], (L, GLA_GATE_RANK, GLA_KEY_DIM), GLA_GATE_RANK ** -0.5),
        'gla_gate_b': nrm(ks[7], (L, GLA_KEY_DIM), 0.01),
        'gla_norm_w': 1.0 + nrm(ks[8], (L, GLA_DV), 0.01),
        'w_o_moba': nrm(ks[9], (L, MOBA_WIDTH, D_MODEL), MOBA_WIDTH ** -0.5),
        'w_o_gla': nrm(ks[10], (L, GLA_VAL_DIM, D_MODEL), GLA_VAL_DIM ** -0.5),
        'b_merge': nrm(ks[11], (L, N_BRANCHES_2 * D_MODEL), 0.01),
        'w_out': nrm(ks[12], (L, D_MODEL, D_MODEL), D_MODEL ** -0.5),
        'norm2_w': 1.0 + nrm(ks[13], (L, D_MODEL), 0.01),
        'w_router': nrm(ks[14], (L, D_MODEL, N_EXPERTS), D_MODEL ** -0.5),
        'b_router': nrm(ks[15], (L, N_EXPERTS), 0.01),
        'w_exp_in': nrm(ks[16], (L, N_EXPERTS, D_MODEL, 2 * D_EXPERT), D_MODEL ** -0.5),
        'b_exp_in': nrm(ks[17], (L, N_EXPERTS, 2 * D_EXPERT), 0.01),
        'w_exp_out': nrm(ks[18], (L, N_EXPERTS, D_EXPERT, D_MODEL), D_EXPERT ** -0.5),
        'b_exp_out': nrm(ks[19], (L, N_EXPERTS, D_MODEL), 0.01),
        'final_norm_w': 1.0 + nrm(ks[20], (D_MODEL,), 0.01),
    }

def second_block(x, c, w_ada, b_ada, norm1_w, w_in, gla_gate_w, gla_gate_b, gla_norm_w, w_o_moba, w_o_gla, b_merge, w_out, norm2_w, w_router, b_router, w_exp_in, b_exp_in, w_exp_out, b_exp_out, final_norm_w):
    c_act = jax.nn.silu(c)
    for l in range(DEPTH_2):
        mod = (c_act @ w_ada[l] + b_ada[l])[:, None, :]
        shift1, scale1, gate1, shift2, scale2, gate2 = jnp.split(mod, 6, axis=-1)
        h = _rmsnorm(x, norm1_w[l]) * (1.0 + scale1) + shift1
        x = x + gate1 * _mixer(h, w_in[l], gla_gate_w[l], gla_gate_b[l], gla_norm_w[l],
                               w_o_moba[l], w_o_gla[l], b_merge[l], w_out[l])
        h = _rmsnorm(x, norm2_w[l]) * (1.0 + scale2) + shift2
        x = x + gate2 * _moe(h, w_router[l], b_router[l], w_exp_in[l], b_exp_in[l],
                             w_exp_out[l], b_exp_out[l])
    return _rmsnorm(x, final_norm_w)


_first_inputs = second_inputs


def second_inputs(seed=0):
    import zlib

    import numpy as np

    out = dict(_first_inputs(seed))
    spreads = {}
    factors = {'b_ada': 3.529,
     'norm1_w': 8.0,
     'gla_gate_w': 2.892,
     'gla_gate_b': 58.811,
     'gla_norm_w': 34.207,
     'b_merge': 30.277,
     'norm2_w': 24.568,
     'b_router': 42.216,
     'b_exp_in': 57.636,
     'b_exp_out': 64.0,
     'final_norm_w': 32.504}
    for name, (base, spread) in spreads.items():
        noise = np.random.default_rng([zlib.crc32(name.encode()), seed]).standard_normal(out[name].shape)
        drawn = base * np.exp(spread * noise) if base else spread * noise
        out[name] = jnp.asarray(drawn.astype(out[name].dtype))
    for name, factor in factors.items():
        out[name] = (out[name] * factor).astype(out[name].dtype)
    return out


_narrow_inputs = second_inputs


def second_inputs(seed=0):

    out = dict(_narrow_inputs(seed))
    wider = {'gla_norm_w': 4.64,
     'norm2_w': 6.21,
     'b_router': 6.76,
     'b_exp_in': 5.2,
     'b_exp_out': 12.0,
     'final_norm_w': 6.15}
    for name, times in wider.items():
        mean = out[name].mean()
        out[name] = (mean + times * (out[name] - mean)).astype(out[name].dtype)
    return out


def setup_inputs(seed=0):
    out = dict(first_inputs(seed))
    for name, value in second_inputs(seed + 1).items():
        if name != "x":
            out[name + "_2"] = value
    return out


def reference(
    x, g_ffn1, w_ffn1_gate, w_ffn1_up, w_ffn1_down, g_mix, w_in, w_gate, b_gate, w_br_a, w_br_b,
    w_br_c, w_out, lam_q1, lam_k1, lam_q2, lam_k2, subln_g, rel_bias, g_ffn2, w_ffn2_gate,
    w_ffn2_up, w_ffn2_down, g_final, c_2, w_ada_2, b_ada_2, norm1_w_2, w_in_2, gla_gate_w_2,
    gla_gate_b_2, gla_norm_w_2, w_o_moba_2, w_o_gla_2, b_merge_2, w_out_2, norm2_w_2,
    w_router_2, b_router_2, w_exp_in_2, b_exp_in_2, w_exp_out_2, b_exp_out_2, final_norm_w_2,
):
    x = first_block(
        x, g_ffn1, w_ffn1_gate, w_ffn1_up, w_ffn1_down, g_mix, w_in, w_gate, b_gate, w_br_a,
        w_br_b, w_br_c, w_out, lam_q1, lam_k1, lam_q2, lam_k2, subln_g, rel_bias, g_ffn2,
        w_ffn2_gate, w_ffn2_up, w_ffn2_down, g_final,
    )
    return second_block(
        x, c_2, w_ada_2, b_ada_2, norm1_w_2, w_in_2, gla_gate_w_2, gla_gate_b_2, gla_norm_w_2,
        w_o_moba_2, w_o_gla_2, b_merge_2, w_out_2, norm2_w_2, w_router_2, b_router_2,
        w_exp_in_2, b_exp_in_2, w_exp_out_2, b_exp_out_2, final_norm_w_2,
    )


_drawn_inputs = setup_inputs


def setup_inputs(seed=0):
    import zlib

    import numpy as np

    out = dict(_drawn_inputs(seed))
    spreads = {}
    factors = {}
    for name, (base, spread) in spreads.items():
        noise = np.random.default_rng([zlib.crc32(name.encode()), seed]).standard_normal(out[name].shape)
        drawn = base * np.exp(spread * noise) if base else spread * noise
        out[name] = jnp.asarray(drawn.astype(out[name].dtype))
    for name, factor in factors.items():
        out[name] = (out[name] * factor).astype(out[name].dtype)
    return out
```

```python
import math
from contextlib import ExitStack

import concourse.bass as bass
from concourse import mybir
import numpy as np

F32 = mybir.dt.float32
U32 = mybir.dt.uint32
ALU = mybir.AluOpType
ACT = mybir.ActivationFunctionType
AX = mybir.AxisListType

P = 128
TOK = 256
TT = TOK // P
D = 1024
DC = D // P
LAYERS = 2
D_FF = 2816
FF_TILES = D_FF // P
TILE_BLOCKS = 3 * DC
TILE = TILE_BLOCKS * P
RING = 5

EPS1, EPS2, SUBLN_EPS = 1e-6, 1e-5, 1e-5
NEG = -1e30

DIL_PAIRS = ((128, 1), (512, 4), (2048, 16))
DIL_GROUPS, DIL_SLOTS, DH = 3, 2, 64
DIFF_HEADS = 4
BIAS_HEADS = DIL_GROUPS * DIL_SLOTS + DIFF_HEADS
BUCKETS, MAX_DISTANCE = 32, 1024
QK_CHUNKS = 2 * DIL_GROUPS + 2 * DIFF_HEADS
UNITS = DIL_SLOTS * TT + DIFF_HEADS * TT
DIL_UNITS = DIL_SLOTS * TT
FOURIER_GROUPS = 8
MERGE_BLOCKS = 3 * DC + DC + 1 + DIFF_HEADS
VEC = 2 * TOK
PROJ = QK_CHUNKS // 2 + 2 * TT + 2 * TT
MIX_BLOCKS = QK_CHUNKS * DC + 3 * DC + 4 * DC + 8 * DC + DC * MERGE_BLOCKS + DC * DC
MIX_TILES = -(-MIX_BLOCKS // TILE_BLOCKS)
LAYER_TILES = -(-(2 * FF_TILES + MIX_TILES) // RING) * RING
PAD_TILES = LAYER_TILES - 2 * FF_TILES - MIX_TILES
GROUPS = LAYER_TILES // RING
MIX0, FFN2 = FF_TILES, FF_TILES + MIX_TILES + PAD_TILES
NORMS = 3
OUTS = DC // 2

HEADS = 8
GLA_HEADS, GLA_DV = 4, 256
RANK = 16
ROT = 32
ADA = 6 * DC
ADA_TILES = ADA * DC // TILE_BLOCKS
SEC_BLOCKS = 16 * DC + 8 * DC + (4 + 4 + 8 + 1) * DC + 8 * DC + DC * 4 * DC + DC * DC
SEC_TILES = ADA_TILES + -(-SEC_BLOCKS // TILE_BLOCKS)
DENSE_TILES = LAYERS * LAYER_TILES + SEC_TILES
LEVELS = (64, 32, 16, 8, 4, 2, 1)
EXPERTS, TOPK = 32, 4
MOE_RING = DC
LAYER_STEPS, MOE_STEPS = 44, 4 * DC
ALPHA, LIMIT = 1.702, 7.0

LP_FFN1, LP_MIX, LP_FFN2, LP_BGATE, LP_SUBLN, LP_LAMI, LP_LAM = 0, 8, 16, 24, 48, 49, 51
LP = LP_LAM + 4 * DH
(C_X, C_GFIN, C_BADA, C_N1, C_GLAB, C_GLAN, C_BMERGE, C_N2, C_NF, C_BEXP) = (
    0, 8, 16, 64, 72, 76, 78, 94, 102, 110)
COLS = C_BEXP + EXPERTS * 16
K_ID, K_ONES, K_CAUSAL, K_LEVEL, K_IOTA, K_EPS = 0, 128, 384, 768, 768 + 8 * 128, 768 + 8 * 128 + 32
K_DSEQ = K_EPS + 4
K_DCH = K_DSEQ + 2 * VEC
K_COS, K_SIN, K_ROT = K_DCH + 2 * P, K_DCH + 2 * P + TOK, K_DCH + 2 * P + 2 * TOK
KONST = K_ROT + ROT


def build(nc, stream, experts, x_in, konst_in, layer_in, cols_in, relb_in, onehot_in, glaw_in,
          router_in, brouter_in, bout_in, bias_rows, out):
    with ExitStack() as ctx:
        def sb(name, shape, dt=F32):
            return ctx.enter_context(nc.sbuf_tensor(name, shape, dt))

        def sem(name):
            return ctx.enter_context(nc.semaphore(name))

        ring = sb("ring", [P, RING, TILE])
        x = sb("x", [P, DC, TOK])
        h = sb("h", [P, DC, TOK])
        sq = sb("sq", [P, DC, TOK])
        std = sb("std", [P, 4 * TOK])
        rstd = sb("rstd", [P, 4 * TOK])
        konst = sb("konst", [P, KONST])
        lp_all = sb("lp_all", [P, LAYERS, LP])
        lp = sb("lp", [P, LP])
        cols = sb("cols", [P, COLS])
        glaw = sb("glaw", [RANK, 512])
        router = sb("router", [P, DC, EXPERTS])
        brouter = sb("brouter", [P, EXPERTS])
        bout = sb("bout", [EXPERTS, D])
        small = sb("small", [P, 64])
        mod = sb("mod", [P, ADA])
        modgain = sb("modgain", [P, 2 * DC])
        work = sb("work", [P, 20480])
        ps = ctx.enter_context(nc.psum_tensor("ps", [P, 8, 512], F32))

        def carve(at, *shape):
            n = math.prod(shape)
            v = work[:, at:at + n]
            if len(shape) == 2:
                v = v.rearrange("p (a b) -> p a b", b=shape[1])
            if len(shape) == 3:
                v = v.rearrange("p (a b c) -> p a b c", b=shape[1], c=shape[2])
            return v

        bias = carve(0, BIAS_HEADS, TT, TOK)
        vecs = carve(5120, BIAS_HEADS, VEC)
        relb = carve(10240, BIAS_HEADS, P)
        onehot = carve(11520, 4, VEC)
        x_tok = carve(13568, TT, D)
        silu = carve(17920, 5, TOK)
        act = carve(19200, 5, TOK)
        qk = carve(5120, QK_CHUNKS, TOK)
        vc = carve(8704, TT, 512)
        vb = carve(9728, TT, 384)
        a_tok = carve(10496, TT, D)
        four = carve(12544, FOURIER_GROUPS, TOK)
        S = carve(14592, 2, 768)
        PT = carve(16128, 2, 768)
        ob = carve(17664, TOK)
        oc = carve(17920, DIFF_HEADS, TOK)
        dft1 = carve(5120, 2, VEC)
        merged = carve(10496, DC, TOK)
        sg = carve(14592, 2, 3, TOK)
        mqk = carve(0, 16, TOK)
        mv = carve(4096, TT, D)
        oa = carve(6144, HEADS, TOK)
        mS = carve(8192, 2, 384)
        mPT = carve(8960, 2, 384)
        gqk = carve(0, 2 * GLA_HEADS, TOK)
        lg = carve(2048, GLA_HEADS, TOK)
        bcum = carve(3072, GLA_HEADS * TOK)
        glow = carve(9728, TOK)
        off = carve(9984, GLA_HEADS, P)
        tmp = carve(10496, GLA_HEADS, P)
        gv = carve(11008, TT, D)
        gr = carve(13056, DC, TOK)
        expd = carve(15104, GLA_HEADS * TOK)
        qd = carve(16128, GLA_HEADS, TOK)
        kd = carve(17152, GLA_HEADS, TOK)
        acc = carve(18176, TT, GLA_HEADS, P)
        gtmp = carve(19200, GLA_HEADS * TOK)
        go = carve(4096, DC, TOK)
        merged2 = carve(0, DC, TOK)
        sg2 = carve(16128, 2, 2, TOK)
        moe_hi = carve(0, 3, TILE)
        wt = carve(9216, TT, EXPERTS)
        wtT = carve(9280, TOK)
        wsel = carve(9536, 2, TOK)
        wb = carve(10048, 2, TOK)
        glu = carve(10560, 2, TOK)
        sig = carve(11072, 2, TOK)
        lin = carve(11584, 2, TOK)
        eact = carve(12096, 2, TOK)
        lgt = carve(12608, TT, EXPERTS)
        eqs = carve(12672, TOPK, EXPERTS)
        y_tok = carve(13056, TT, D)
        top8 = small[:, 32:40]
        topi = small[:, 40:48].bitcast(U32)
        topf = small[:, 48:52]
        topw = small[:, 52:56]

        ident = konst[:, K_ID:K_ID + P]
        ones = konst[:, K_ONES:K_ONES + P]
        ones_tok = konst[:, K_ONES:K_ONES + TOK]
        causal = konst[:, K_CAUSAL:K_CAUSAL + 384]
        iota = konst[:, K_IOTA:K_IOTA + EXPERTS]
        eps_col = {EPS1: konst[:, K_EPS:K_EPS + 1], EPS2: konst[:, K_EPS + 1:K_EPS + 2]}
        one_col = konst[:, K_EPS + 2:K_EPS + 3]
        dseq = konst[:, K_DSEQ:K_DSEQ + 2 * VEC].rearrange("p (a b) -> p a b", b=VEC)
        dch = konst[:, K_DCH:K_DCH + 2 * P].rearrange("p (a b) -> p a b", b=P)
        cosT = konst[0:ROT, K_COS:K_COS + TOK]
        sinT = konst[0:ROT, K_SIN:K_SIN + TOK]
        rotT = konst[0:ROT, K_ROT:K_ROT + ROT]

        def level_mask(i):
            return konst[:, K_LEVEL + i * P:K_LEVEL + (i + 1) * P]

        ff_banks = (0, 1, 3, 0, 1)
        SSUM, DOWN = 2, 4

        tile_landed = [sem(f"tile_landed{i}") for i in range(RING)]
        tile_used = sem("tile_used")
        moe_landed = [sem(f"moe_landed{i}") for i in range(MOE_RING)]
        moe_used = sem("moe_used")
        konst_landed, x_landed, par_landed = sem("konst_landed"), sem("x_landed"), sem("par_landed")
        rel_landed = sem("rel_landed")
        xt_ready, xt_taken = sem("xt_ready"), sem("xt_taken")
        vec_ready, vec_taken = sem("vec_ready"), sem("vec_taken")
        rows_written, bias_landed = sem("rows_written"), sem("bias_landed")
        x_ready = sem("x_ready")
        sq_ready, ssum_ready, std_ready, h_ready = (
            sem("sq_ready"), sem("ssum_ready"), sem("std_ready"), sem("h_ready"))
        gu_ready, silu_ready, act_ready = sem("gu_ready"), sem("silu_ready"), sem("act_ready")
        proj_ready, proj_taken = sem("proj_ready"), sem("proj_taken")
        logits_ready, scores_made, max_ready = sem("logits_ready"), sem("scores_made"), sem("max_ready")
        exp_ready, probs_ready = sem("exp_ready"), sem("probs_ready")
        pt_ready, pt_taken = sem("pt_ready"), sem("pt_taken")
        o_ready, o_taken = sem("o_ready"), sem("o_taken")
        osq_ready, ossum_ready, ostd_ready, yc_ready = (
            sem("osq_ready"), sem("ossum_ready"), sem("ostd_ready"), sem("yc_ready"))
        lamdot_ready, lamexp_ready = sem("lamdot_ready"), sem("lamexp_ready")
        dft1_ready, dft1_taken = sem("dft1_ready"), sem("dft1_taken")
        dft2_ready, dft2_taken = sem("dft2_ready"), sem("dft2_taken")
        gates_ready, sig_ready, ys_ready, merged_ready = (
            sem("gates_ready"), sem("sig_ready"), sem("ys_ready"), sem("merged_ready"))
        out_ready = sem("out_ready")
        cact_ready, ada_ready, mod_ready = sem("cact_ready"), sem("ada_ready"), sem("mod_ready")
        rot_ready, rot_taken, roped = sem("rot_ready"), sem("rot_taken"), sem("roped")
        z_ready, zb_ready, sp_ready = sem("z_ready"), sem("zb_ready"), sem("sp_ready")
        diff_ready, decay_ready, k_decayed = sem("diff_ready"), sem("decay_ready"), sem("k_decayed")
        qk_decayed = sem("qk_decayed")
        lev_ready, lev_taken, added, scores_done = (
            sem("lev_ready"), sem("lev_taken"), sem("added"), sem("scores_done"))
        go_ready, go_taken, gla_ready = sem("go_ready"), sem("go_taken"), sem("gla_ready")
        route_ready, top_ready, topexp_ready, wt_ready = (
            sem("route_ready"), sem("top_ready"), sem("topexp_ready"), sem("wt_ready"))
        wtT_ready, wtT_taken = sem("wtT_ready"), sem("wtT_taken")
        wsel_ready, wb_ready, wb_taken = sem("wsel_ready"), sem("wb_ready"), sem("wb_taken")
        hid_ready, glu_ready, esig_ready, eact_ready = (
            sem("hid_ready"), sem("glu_ready"), sem("esig_ready"), sem("eact_ready"))
        ytok_ready, ytok_taken, stored = (
            sem("ytok_ready"), sem("ytok_taken"), sem("stored"))
        act_step, dve_step = sem("act_step"), sem("dve_step")

        class Steps:

            def __init__(self, eng, sem):
                self.eng, self.sem, self.base, self.k = eng, sem, 0, 0

            def __call__(self, ins):
                ins.then_inc(self.sem, 1)
                self.k += 1
                self.eng.wait_ge(self.sem, self.base + self.k)

        class Blocks:

            def __init__(self, pe, l, tile):
                self.pe, self.l, self.first, self.n = pe, l, tile * TILE_BLOCKS, tile * TILE_BLOCKS
                self.taken = 0

            def take(self, k=1):
                t, b = divmod(self.n, TILE_BLOCKS)
                if b == 0:
                    self.pe.wait_ge(tile_landed[t % RING], (self.l * GROUPS + t // RING + 1) * 16)
                assert b + k <= TILE_BLOCKS
                self.n += k
                self.taken = k
                return ring[:, t % RING, b * P:(b + k) * P]

            def used(self, mm):
                start = self.n - self.taken
                if start % TILE_BLOCKS == 0 and start > self.first:
                    mm.then_inc(tile_used, 1)
                return mm

        block = ctx.enter_context(nc.Block())

        @block.sync
        def _(sp):
            sp.dma_start(x_tok[:, :, :], x_in.rearrange("(t p) d -> p t d", p=P)).then_inc(x_landed, 16)
            for s in range(RING):
                sp.dma_start(ring[:, s, :], stream[s]).then_inc(tile_landed[s], 16)
            whole = DENSE_TILES // RING
            with sp.Fori(1, whole) as g:
                for s in range(RING):
                    sp.wait_ge(tile_used, g * RING + (s + 1 - RING))
                    sp.dma_start(ring[:, s, :], stream[g * RING + s]).then_inc(tile_landed[s], 16)
            for s in range(DENSE_TILES - whole * RING):
                sp.wait_ge(tile_used, (whole - 1) * RING + s + 1)
                sp.dma_start(ring[:, s, :], stream[whole * RING + s]).then_inc(tile_landed[s], 16)

            def slot(j):
                return ring[:, j, :] if j < RING else moe_hi[:, j - RING, :]

            sp.wait_ge(tile_used, DENSE_TILES)
            for j in range(MOE_RING):
                if j == RING:
                    sp.wait_ge(x_ready, 1 + LAYERS * NORMS + 2)
                sp.dma_start(slot(j), experts[j]).then_inc(moe_landed[j], 16)
            with sp.Fori(1, EXPERTS) as e:
                for j in range(MOE_RING):
                    sp.wait_ge(moe_used, e * MOE_RING + (j + 1 - MOE_RING))
                    sp.dma_start(slot(j), experts[e * MOE_RING + j]).then_inc(moe_landed[j], 16)
            sp.wait_ge(ytok_taken, 2 * OUTS)
            sp.dma_start(out.rearrange("(t p) d -> p t d", p=P), y_tok[:, :, :]).then_inc(stored, 16)
            sp.wait_ge(stored, 16)

        @block.gpsimd
        def _(pool):
            pool.dma_start(konst[:, :], konst_in).then_inc(konst_landed, 16)
            pool.dma_start(lp_all[:, :, :], layer_in).then_inc(par_landed, 16)
            pool.dma_start(cols[:, :], cols_in).then_inc(par_landed, 16)
            pool.dma_start(relb[0:BUCKETS + 1], relb_in).then_inc(rel_landed, 16)
            pool.dma_start(onehot[0:BUCKETS + 1], onehot_in).then_inc(rel_landed, 16)
            pool.dma_start(glaw[:, :], glaw_in).then_inc(par_landed, 16)
            pool.dma_start(router[:, :, :], router_in).then_inc(par_landed, 16)
            pool.dma_start(brouter[:, :], brouter_in).then_inc(par_landed, 16)
            pool.dma_start(bout[:, :], bout_in).then_inc(par_landed, 16)
            pool.wait_ge(vec_taken, BIAS_HEADS)
            pool.dma_start(bias_rows.rearrange("h p v -> p h v"), vecs[:, :, :]).then_inc(rows_written, 16)
            pool.wait_ge(rows_written, 16)
            for qt in range(TT):
                skew = bass.AP(bias_rows.tensor, (TOK - 1) - qt * P,
                               [[VEC - 1, P], [P * VEC, BIAS_HEADS], [1, TOK]])
                pool.dma_start(bias[:, :, qt, :], skew).then_inc(bias_landed, 16)

            for v in range(len(LEVELS) + 1):
                pool.wait_ge(decay_ready, v + 1)
                if v > 0:
                    pool.wait_ge(lev_ready, (v - 1) * TT + 1)
                pool.tensor_tensor(kd[:, :, :], gqk[:, GLA_HEADS:, :],
                                   expd.rearrange("p (h t) -> p h t", t=TOK), ALU.mult).then_inc(k_decayed, 1)

        @block.scalar
        def _(a):
            step = Steps(a, act_step)

            def norm(l, n, eps, scale=1.0 / D):
                a.wait_ge(x_ready, l * NORMS + n + 1)
                nc.scalar.activation(sq[:, :, :], x[:, :, :], ACT.Square).then_inc(sq_ready, 1)
                a.wait_ge(ssum_ready, l * NORMS + n + 1)
                nc.scalar.activation(std[:, 0:TOK], ps[:, SSUM, 0:TOK], ACT.Sqrt, bias=eps_col[eps],
                                     scale=scale).then_inc(std_ready, 1)

            def ffn_tile(l, f, i, g=0):
                s = (i - 1) % 5
                a.wait_ge(gu_ready, l * (2 * FF_TILES) + g * 5 + (f * FF_TILES + i + 1))
                nc.scalar.activation(silu[:, s, :], ps[:, ff_banks[s], 0:TOK], ACT.Silu).then_inc(silu_ready, 1)

            def ffn(l, f):
                ffn_tile(l, f, 0)
                with a.Fori(0, (FF_TILES - 2) // 5) as g:
                    for s in range(5):
                        ffn_tile(l, f, 1 + s, g)
                ffn_tile(l, f, FF_TILES - 1)

            a.wait_ge(par_landed, 6 * 16)
            for i in range(BIAS_HEADS):
                a.wait_ge(vec_ready, i + 1)
                nc.scalar.activation(vecs[:, i, :], ps[:, i % 4, :], ACT.Copy).then_inc(vec_taken, 1)
            nc.scalar.activation(small[:, 16:24], cols[:, C_X:C_X + DC], ACT.Silu).then_inc(cact_ready, 1)

            with a.Fori(0, LAYERS) as l:
                norm(l, 0, EPS1)
                ffn(l, 0)
                norm(l, 1, EPS1)
                a.wait_ge(lamdot_ready, l + 1)
                nc.scalar.activation(small[:, 2:4], small[:, 0:2], ACT.Exp).then_inc(lamexp_ready, 1)

                def take_proj(r):
                    a.wait_ge(proj_ready, l * PROJ + r + 1)
                    bank = ps[:, r % 4, :]
                    if r < 7:
                        dst = qk[:, 2 * r:2 * r + 2, :]
                        bank = bank.rearrange("p (a b) -> p a b", b=TOK)
                    elif r < 9:
                        dst = vc[:, r - 7, :]
                    elif r < 11:
                        dst, bank = vb[:, r - 9, :], ps[:, r % 4, 0:384]
                    else:
                        dst = a_tok[:, (r - 11) % 2, (r - 11) // 2 * 512:(r - 11) // 2 * 512 + 512]
                    nc.scalar.activation(dst, bank, ACT.Copy).then_inc(proj_taken, 1)

                a.wait_ge(rows_written, 16)
                for r in range(11):
                    take_proj(r)

                def exps(u):
                    a.wait_ge(max_ready, l * UNITS + u + 1)
                    if u < DIL_UNITS:
                        nc.scalar.activation(S[:, u % 2, :], S[:, u % 2, :], ACT.Exp, bias=small[:, 8 + u % 2 * 2:9 + u % 2 * 2],
                                             accum_out=small[:, 12 + u % 2 * 2:13 + u % 2 * 2]).then_inc(exp_ready, 1)
                    else:
                        for m in range(2):
                            c = u % 2 * 2 + m
                            e = nc.scalar.activation(S[:, u % 2, m * TOK:(m + 1) * TOK], S[:, u % 2, m * TOK:(m + 1) * TOK],
                                                     ACT.Exp, bias=small[:, 8 + c:9 + c], accum_out=small[:, 12 + c:13 + c])
                        e.then_inc(exp_ready, 1)

                def take_pt(u):
                    a.wait_ge(pt_ready, l * UNITS + u + 1)
                    n = 768 if u < DIL_UNITS else 256
                    nc.scalar.activation(PT[:, u % 2, 0:n], ps[:, 4:6, :].rearrange("p a b -> p (a b)")[:, 0:n],
                                         ACT.Copy).then_inc(pt_taken, 1)

                def take_o(i):
                    a.wait_ge(o_ready, l * 5 + i + 1)
                    if i == 0:
                        nc.scalar.activation(ob[:, :], ps[:, 6, 0:TOK], ACT.Copy).then_inc(o_taken, 1)
                    else:
                        hh = i - 1
                        nc.scalar.activation(oc[:, hh, :], ps[:, 7 - hh % 2, 0:TOK], ACT.Copy).then_inc(o_taken, 1)

                for u in range(UNITS + 2):
                    if u < UNITS:
                        exps(u)
                    if u >= 1 and u - 1 < UNITS:
                        take_pt(u - 1)
                    if u >= 2:
                        w = u - 2
                        if w == DIL_UNITS - 1:
                            take_o(0)
                        if w >= DIL_UNITS and w % 2 == 1:
                            take_o(1 + (w - DIL_UNITS) // 2)
                a.wait_ge(o_taken, l * 5 + 5)
                nc.scalar.activation(sq[:, 0:4, :], oc[:, :, :], ACT.Square).then_inc(osq_ready, 1)
                for r in range(11, PROJ):
                    take_proj(r)
                a.wait_ge(ossum_ready, l + 1)
                nc.scalar.activation(std[:, :], ps[:, 6:8, :].rearrange("p a b -> p (a b)"), ACT.Sqrt, bias=eps_col[SUBLN_EPS],
                                     scale=1.0 / P).then_inc(ostd_ready, 1)
                for g in range(FOURIER_GROUPS):
                    a.wait_ge(dft1_ready, l * FOURIER_GROUPS + g + 1)
                    nc.scalar.activation(dft1[:, g % 2, :], ps[:, g % 2, :], ACT.Copy).then_inc(dft1_taken, 1)
                for m in range(DC):
                    a.wait_ge(gates_ready, l * DC + m + 1)
                    if m >= 2:
                        a.wait_ge(merged_ready, l * DC + m - 1)
                    b0 = 4 * (1 - m % 2)
                    for j in range(3):
                        c = LP_BGATE + j * DC + m
                        e = nc.scalar.activation(sg[:, m % 2, j, :], ps[:, b0 + j // 2, j % 2 * TOK:(j % 2 + 1) * TOK], ACT.Sigmoid, bias=lp[:, c:c + 1])
                    e.then_inc(sig_ready, 1)
                norm(l, 2, EPS1)
                ffn(l, 1)

            norm(LAYERS, 0, EPS1)
            norm(LAYERS, 1, EPS2)

            def take_proj2(r):
                a.wait_ge(proj_ready, LAYERS * PROJ + r + 1)
                bank = ps[:, r % 4, :]
                pair = bank.rearrange("p (a b) -> p a b", b=TOK)
                if r < 4:
                    op = nc.scalar.activation(mv[:, r % 2, r // 2 * 512:r // 2 * 512 + 512], bank, ACT.Copy)
                elif r < 12:
                    op = nc.scalar.activation(mqk[:, 2 * (r - 4):2 * (r - 4) + 2, :], pair, ACT.Copy)
                elif r < 14:
                    op = nc.scalar.activation(gqk[:, 2 * (r - 12):2 * (r - 12) + 2, :], pair, ACT.Copy, scale=float(P) ** -0.5)
                elif r < 16:
                    op = nc.scalar.activation(gqk[:, 2 * (r - 12):2 * (r - 12) + 2, :], pair, ACT.Copy)
                elif r == 16:
                    op = nc.scalar.activation(glow[0:RANK, :], ps[0:RANK, r % 4, 0:TOK], ACT.Copy)
                elif r < 21:
                    op = nc.scalar.activation(gr[:, 2 * (r - 17):2 * (r - 17) + 2, :], pair, ACT.Silu)
                else:
                    op = nc.scalar.activation(gv[:, (r - 21) % 2, (r - 21) // 2 * 512:(r - 21) // 2 * 512 + 512], bank, ACT.Copy)
                op.then_inc(proj_taken, 1)

            for r in range(12):
                take_proj2(r)

            U0 = LAYERS * UNITS

            def exps2(u):
                a.wait_ge(max_ready, U0 + u + 1)
                for m, (lo, hi) in enumerate(((0, 128), (128, 384))):
                    c = u % 2 * 2 + m
                    e = nc.scalar.activation(mS[:, u % 2, lo:hi], mS[:, u % 2, lo:hi], ACT.Exp, bias=small[:, 8 + c:9 + c],
                                             accum_out=small[:, 12 + c:13 + c])
                e.then_inc(exp_ready, 1)

            for u in range(HEADS + 2):
                if u < HEADS:
                    exps2(u)
                if 1 <= u <= HEADS:
                    a.wait_ge(pt_ready, U0 + u)
                    nc.scalar.activation(mPT[:, (u - 1) % 2, :], ps[:, 4, 0:384], ACT.Copy).then_inc(pt_taken, 1)
                if u >= 2:
                    a.wait_ge(o_ready, LAYERS * 5 + u - 1)
                    nc.scalar.activation(oa[:, u - 2, :], ps[:, 6 + u % 2, 0:TOK], ACT.Copy).then_inc(o_taken, 1)
            for r in range(12, 25):
                take_proj2(r)
            a.wait_ge(zb_ready, 1)
            step(nc.scalar.activation(gtmp[:, :], lg.rearrange("p h t -> p (h t)"), ACT.Abs))
            step(nc.scalar.activation(gtmp[:, :], gtmp[:, :], ACT.Exp, scale=-1.0))
            nc.scalar.activation(gtmp[:, :], gtmp[:, :], ACT.Ln, bias=one_col).then_inc(sp_ready, 1)
            for v in range(len(LEVELS) + 1):
                a.wait_ge(diff_ready, v + 1)
                if v > 0:
                    a.wait_ge(k_decayed, v)
                    a.wait_ge(qk_decayed, v)
                nc.scalar.activation(expd[:, :], gtmp[:, :], ACT.Exp, scale=1.0 / 16).then_inc(decay_ready, 1)
            for i in range(OUTS):
                a.wait_ge(go_ready, i + 1)
                nc.scalar.activation(go[:, 2 * i:2 * i + 2, :], ps[:, 4 + i, :].rearrange("p (a b) -> p a b", b=TOK),
                                     ACT.Copy).then_inc(go_taken, 1)
            a.wait_ge(go_taken, OUTS)
            nc.scalar.activation(sq[:, :, :], go[:, :, :], ACT.Square).then_inc(osq_ready, 1)
            a.wait_ge(ossum_ready, LAYERS + 1)
            nc.scalar.activation(std[:, :], ps[:, 0:2, :].rearrange("p a b -> p (a b)"), ACT.Sqrt, bias=eps_col[EPS2],
                                 scale=1.0 / GLA_DV).then_inc(ostd_ready, 1)
            for m in range(DC):
                a.wait_ge(gates_ready, LAYERS * DC + m + 1)
                if m >= 2:
                    a.wait_ge(merged_ready, LAYERS * DC + m - 1)
                for j in range(2):
                    c = C_BMERGE + j * DC + m
                    e = nc.scalar.activation(sg2[:, m % 2, j, :], ps[:, 2 + 2 * (m % 2), j * TOK:(j + 1) * TOK], ACT.Sigmoid,
                                             bias=cols[:, c:c + 1])
                e.then_inc(sig_ready, 1)
            norm(LAYERS, 2, EPS2)
            for t in range(TT):
                a.wait_ge(top_ready, t + 1)
                nc.scalar.activation(topw, top8[:, 0:TOPK], ACT.Exp, bias=small[:, 56:57],
                                     accum_out=small[:, 57:58]).then_inc(topexp_ready, 1)
            with a.Fori(0, EXPERTS) as e:
                for j in range(DC):
                    a.wait_ge(glu_ready, e * DC + j + 1)
                    nc.scalar.activation(sig[:, j % 2, :], glu[:, j % 2, :], ACT.Sigmoid, scale=ALPHA).then_inc(esig_ready, 1)
            norm(LAYERS, 3, EPS2)
            for i in range(2 * OUTS):
                t, half = divmod(i, OUTS)
                a.wait_ge(ytok_ready, i + 1)
                nc.scalar.activation(y_tok[:, t, half * 256:half * 256 + 256], ps[:, i % 4, 0:256],
                                     ACT.Copy).then_inc(ytok_taken, 1)

        @block.vector
        def _(v):
            step = Steps(v, dve_step)

            def add_level(i):
                for t in range(TT):
                    n = 1 + (i - 1) * TT + t
                    v.wait_ge(lev_ready, n + 1)
                    sc = ps[:, 2 * (i % 2) + t, :].rearrange("p (h t) -> p h t", t=P)
                    mask = level_mask(i - 1).unsqueeze(1).to_broadcast([P, GLA_HEADS, P])
                    dst = acc[:, t, :, :] if i == 1 else tmp[:, :, :]
                    nc.vector.tensor_tensor(dst, sc, mask, ALU.mult).then_inc(lev_taken, 1)
                    v.wait_ge(lev_taken, n + 1)
                    if i > 1:
                        op = nc.vector.tensor_tensor(acc[:, t, :, :], acc[:, t, :, :], tmp[:, :, :], ALU.add)
                        if i == len(LEVELS) + 1 and t == TT - 1:
                            op.then_inc(scores_done, 1)
                        else:
                            step(op)

            def recip_std(l, n):
                v.wait_ge(std_ready, l * NORMS + n + 1)
                step(nc.vector.reciprocal(rstd[:, 0:TOK], std[:, 0:TOK]))

            def norm(l, n, gain, out=None):
                recip_std(l, n)
                for c in range(DC):
                    op = nc.vector.scalar_tensor_tensor(out=(h if out is None else out)[:, c, :], in0=x[:, c, :], scalar=gain[:, c:c + 1],
                                                        in1=rstd[:, 0:TOK], op0=ALU.mult, op1=ALU.mult)
                return op

            def ffn_tile(l, f, i, g=0):
                s = (i - 1) % 5
                v.wait_ge(silu_ready, l * (2 * FF_TILES) + g * 5 + (f * FF_TILES + i + 1))
                nc.vector.tensor_tensor(act[:, s, :], silu[:, s, :], ps[:, ff_banks[s], TOK:2 * TOK],
                                        ALU.mult).then_inc(act_ready, 1)

            def ffn(l, f):
                ffn_tile(l, f, 0)
                with v.Fori(0, (FF_TILES - 2) // 5) as g:
                    for s in range(5):
                        ffn_tile(l, f, 1 + s, g)
                ffn_tile(l, f, FF_TILES - 1)
                v.wait_ge(tile_used, l * LAYER_TILES + (FFN2 if f else 0) + FF_TILES)
                for b in range(OUTS):
                    xs = x[:, 2 * b:2 * b + 2, :]
                    op = nc.vector.scalar_tensor_tensor(out=xs, in0=ps[:, DOWN + b, :].rearrange("p (a b) -> p a b", b=TOK), scalar=0.5,
                                                        in1=xs, op0=ALU.mult, op1=ALU.add)
                op.then_inc(x_ready, 1)

            for i in range(OUTS):
                v.wait_ge(xt_ready, i + 1)
                op = nc.vector.tensor_copy(x[:, 2 * i:2 * i + 2, :], ps[:, 4 + i, :].rearrange("p (a b) -> p a b", b=TOK))
            op.then_inc(x_ready, 1)
            v.wait_ge(par_landed, 6 * 16)
            v.wait_ge(konst_landed, 16)

            first_k = step.k
            with v.Fori(0, LAYERS) as l:
                step.base = l * LAYER_STEPS
                step(nc.vector.tensor_copy(lp[:, :], lp_all[:, l, :]))
                for i in range(2):
                    q = lp[:, LP_LAM + i * 2 * DH:LP_LAM + i * 2 * DH + DH]
                    k = lp[:, LP_LAM + i * 2 * DH + DH:LP_LAM + (i + 1) * 2 * DH]
                    op = nc.vector.tensor_tensor_reduce(rstd[:, 512 + i * DH:512 + (i + 1) * DH], q, k, 1.0, 0.0, ALU.mult, ALU.add, small[:, i:i + 1])
                op.then_inc(lamdot_ready, 1)
                step(nc.vector.tensor_scalar(small[:, 6:7], lp[:, LP_SUBLN:LP_SUBLN + 1], lp[:, LP_LAMI + 1:LP_LAMI + 2], None, ALU.mult))
                norm(l, 0, lp[:, LP_FFN1:LP_FFN1 + DC]).then_inc(h_ready, 1)
                ffn(l, 0)
                norm(l, 1, lp[:, LP_MIX:LP_MIX + DC]).then_inc(h_ready, 1)
                v.wait_ge(lamexp_ready, l + 1)
                step(nc.vector.tensor_scalar(small[:, 5:6], small[:, 2:3], lp[:, LP_LAMI:LP_LAMI + 1], None, ALU.add))
                step(nc.vector.tensor_tensor(small[:, 4:5], small[:, 3:4], small[:, 5:6], ALU.subtract))
                v.wait_ge(bias_landed, TT * 16)

                def scores(u):
                    v.wait_ge(logits_ready, l * UNITS + u + 1)
                    if u >= 2:
                        v.wait_ge(pt_ready, l * UNITS + u - 1)
                    b = 2 * (u % 2)
                    if u < DIL_UNITS:
                        slot, qt = divmod(u, TT)
                        lo = ps[:, b:b + 2, :].rearrange("p a b -> p (a b)")[:, 0:768].rearrange("p (a b) -> p a b", b=TOK)
                        bi = bias[:, slot:slot + 5:2, qt, :]
                        dst = S[:, u % 2, :].rearrange("p (a b) -> p a b", b=TOK)
                    else:
                        hh, qt = divmod(u - DIL_UNITS, TT)
                        lo = ps[:, b:b + 2, 0:TOK]
                        bi = bias[:, 6 + hh, qt, :].unsqueeze(1).to_broadcast([P, 2, TOK])
                        dst = S[:, u % 2, 0:512].rearrange("p (a b) -> p a b", b=TOK)
                    nc.vector.scalar_tensor_tensor(out=dst, in0=lo, scalar=DH ** -0.5, in1=bi, op0=ALU.mult,
                                                   op1=ALU.add).then_inc(scores_made, 1)
                    v.wait_ge(scores_made, l * UNITS + u + 1)
                    c = 8 + u % 2 * 2
                    if u < DIL_UNITS:
                        op = nc.vector.tensor_reduce(small[:, c:c + 1], S[:, u % 2, :], AX.X, ALU.max, negate=True)
                    else:
                        op = nc.vector.tensor_reduce(small[:, c:c + 2], dst, AX.X, ALU.max, negate=True)
                    op.then_inc(max_ready, 1)

                def probs(u):
                    v.wait_ge(exp_ready, l * UNITS + u + 1)
                    c = u % 2 * 2
                    if u < DIL_UNITS:
                        step(nc.vector.reciprocal(small[:, 24 + c:25 + c], small[:, 12 + c:13 + c]))
                        op = nc.vector.tensor_scalar(S[:, u % 2, :], S[:, u % 2, :], small[:, 24 + c:25 + c], None, ALU.mult)
                    else:
                        step(nc.vector.reciprocal(small[:, 24 + c:26 + c], small[:, 12 + c:14 + c]))
                        step(nc.vector.tensor_scalar(S[:, u % 2, TOK:512], S[:, u % 2, TOK:512], small[:, 25 + c:26 + c], small[:, 4:5], ALU.mult, ALU.mult))
                        op = nc.vector.scalar_tensor_tensor(out=S[:, u % 2, 0:TOK], in0=S[:, u % 2, 0:TOK], scalar=small[:, 24 + c:25 + c],
                                                            in1=S[:, u % 2, TOK:512], op0=ALU.mult, op1=ALU.add)
                    op.then_inc(probs_ready, 1)

                for u in range(UNITS + 1):
                    if u < UNITS:
                        scores(u)
                    if u >= 1:
                        probs(u - 1)
                v.wait_ge(ostd_ready, l + 1)
                step(nc.vector.reciprocal(rstd[:, :], std[:, :]))
                for hh in range(DIFF_HEADS):
                    op = nc.vector.scalar_tensor_tensor(out=oc[:, hh, :], in0=oc[:, hh, :], scalar=small[:, 6:7],
                                                        in1=rstd[:, hh * TOK:(hh + 1) * TOK], op0=ALU.mult, op1=ALU.mult)
                op.then_inc(yc_ready, 1)
                for g in range(FOURIER_GROUPS):
                    v.wait_ge(dft2_ready, l * FOURIER_GROUPS + g + 1)
                    nc.vector.tensor_copy(four[:, g, :], ps[:, 2 + g % 2, 0:TOK]).then_inc(dft2_taken, 1)
                for m in range(DC):
                    v.wait_ge(sig_ready, l * DC + m + 1)
                    v.wait_ge(ys_ready, l * DC + m + 1)
                    b0 = 4 * (1 - m % 2) + 2
                    branches = ps[:, b0:b0 + 2, :].rearrange("p a b -> p (a b)")[:, 0:3 * TOK].rearrange("p (a b) -> p a b", b=TOK)
                    step(nc.vector.tensor_tensor(sg[:, m % 2, :, :], sg[:, m % 2, :, :], branches, ALU.mult))
                    step(nc.vector.tensor_tensor(sg[:, m % 2, 0, :], sg[:, m % 2, 0, :], sg[:, m % 2, 1, :], ALU.add))
                    nc.vector.tensor_tensor(merged[:, m, :], sg[:, m % 2, 0, :], sg[:, m % 2, 2, :], ALU.add).then_inc(merged_ready, 1)
                for b in range(OUTS):
                    v.wait_ge(out_ready, l * OUTS + b + 1)
                    xs = x[:, 2 * b:2 * b + 2, :]
                    op = nc.vector.tensor_tensor(xs, xs, ps[:, DOWN + b, :].rearrange("p (a b) -> p a b", b=TOK), ALU.add)
                op.then_inc(x_ready, 1)
                norm(l, 2, lp[:, LP_FFN2:LP_FFN2 + DC]).then_inc(h_ready, 1)
                ffn(l, 1)
            assert step.k - first_k == LAYER_STEPS, step.k - first_k
            step.base = LAYERS * LAYER_STEPS
            step.k = first_k

            norm(LAYERS, 0, cols[:, C_GFIN:C_GFIN + DC], out=x).then_inc(x_ready, 1)
            v.wait_ge(ada_ready, 1)
            step(nc.vector.tensor_tensor(mod[:, :], ps[:, 3, 0:ADA], cols[:, C_BADA:C_BADA + ADA], ALU.add))
            for n, (sc, w) in enumerate(((DC, C_N1), (4 * DC, C_N2))):
                step(nc.vector.scalar_tensor_tensor(out=modgain[:, n * DC:(n + 1) * DC], in0=mod[:, sc:sc + DC], scalar=1.0,
                                                    in1=cols[:, w:w + DC], op0=ALU.add, op1=ALU.mult))

            def mod_norm(n, i):
                step(norm(LAYERS, n, modgain[:, i * DC:(i + 1) * DC]))
                shift = mod[:, 3 * i * DC:(3 * i + 1) * DC]
                op = nc.vector.tensor_tensor(h[:, :, :], h[:, :, :], shift.unsqueeze(2).to_broadcast([P, DC, TOK]), ALU.add)
                op.then_inc(h_ready, 1)

            mod_norm(1, 0)
            for i in range(HEADS):
                v.wait_ge(rot_ready, i + 1)
                qs = mqk[0:ROT, 2 * i:2 * i + 2, :]
                rp = ps[0:ROT, 4 + i % 2, :].rearrange("p (a b) -> p a b", b=TOK)
                rt = rstd[0:ROT, 512:1024].rearrange("p (a b) -> p a b", b=TOK)
                step(nc.vector.tensor_tensor(rt, rp, sinT.unsqueeze(1).to_broadcast([ROT, 2, TOK]), ALU.mult))
                step(nc.vector.tensor_tensor(qs, qs, cosT.unsqueeze(1).to_broadcast([ROT, 2, TOK]), ALU.mult))
                nc.vector.tensor_tensor(qs, qs, rt, ALU.add).then_inc(roped, 1)
                v.wait_ge(roped, i + 1)
            U0 = LAYERS * UNITS
            for u in range(HEADS + 1):
                if u < HEADS:
                    v.wait_ge(logits_ready, U0 + u + 1)
                    if u >= 2:
                        v.wait_ge(pt_ready, U0 + u - 1)
                    nc.vector.scalar_tensor_tensor(out=mS[:, u % 2, :], in0=ps[:, u % 2, 0:384], scalar=P ** -0.5, in1=causal,
                                                   op0=ALU.mult, op1=ALU.add).then_inc(scores_made, 1)
                    v.wait_ge(scores_made, U0 + u + 1)
                    c = 8 + u % 2 * 2
                    nc.vector.tensor_reduce(small[:, c:c + 1], mS[:, u % 2, 0:128], AX.X, ALU.max, negate=True)
                    nc.vector.tensor_reduce(small[:, c + 1:c + 2], mS[:, u % 2, 128:384], AX.X, ALU.max, negate=True).then_inc(max_ready, 1)
                if u >= 1:
                    w = u - 1
                    c = w % 2 * 2
                    v.wait_ge(exp_ready, U0 + w + 1)
                    step(nc.vector.reciprocal(small[:, 24 + c:26 + c], small[:, 12 + c:14 + c]))
                    nc.vector.tensor_scalar(mS[:, w % 2, 0:128], mS[:, w % 2, 0:128], small[:, 24 + c:25 + c], None, ALU.mult)
                    nc.vector.tensor_scalar(mS[:, w % 2, 128:384], mS[:, w % 2, 128:384], small[:, 25 + c:26 + c], None, ALU.mult).then_inc(probs_ready, 1)
            v.wait_ge(z_ready, 1)
            for hh in range(GLA_HEADS):
                op = nc.vector.tensor_scalar(lg[:, hh, :], ps[:, 4 + hh // 2, hh % 2 * TOK:(hh % 2 + 1) * TOK], cols[:, C_GLAB + hh:C_GLAB + hh + 1], None, ALU.add)
            op.then_inc(zb_ready, 1)
            v.wait_ge(sp_ready, 1)
            lgf = lg.rearrange("p h t -> p (h t)")
            step(nc.vector.scalar_tensor_tensor(out=lgf, in0=lgf, scalar=0.0, in1=gtmp[:, :], op0=ALU.min, op1=ALU.subtract))
            for hh in range(GLA_HEADS):
                op = nc.vector.tensor_tensor_scan(out=bcum[:, hh * TOK:(hh + 1) * TOK], data0=ones_tok, data1=lg[:, hh, :],
                                                  initial=0.0, op0=ALU.mult, op1=ALU.add)
            step(op)
            for i, s in enumerate((P,) + LEVELS):
                if i > 0:
                    v.wait_ge(decay_ready, i)
                bv = bcum.rearrange("p (n two s) -> p n two s", two=2, s=s)
                gv_ = gtmp.rearrange("p (n two s) -> p n two s", two=2, s=s)
                n = GLA_HEADS * TOK // (2 * s)
                ref = bv[:, :, 0, s - 1:s].to_broadcast([P, n, s])
                nc.vector.tensor_tensor(gv_[:, :, 0, :], ref, bv[:, :, 0, :], ALU.subtract)
                nc.vector.tensor_tensor(gv_[:, :, 1, :], bv[:, :, 1, :], ref, ALU.subtract).then_inc(diff_ready, 1)
                v.wait_ge(decay_ready, i + 1)
                if i > 0:
                    v.wait_ge(lev_ready, (i - 1) * TT + 1)
                nc.vector.tensor_tensor(qd[:, :, :], gqk[:, 0:GLA_HEADS, :], expd.rearrange("p (h t) -> p h t", t=TOK), ALU.mult).then_inc(qk_decayed, 1)
                if i == 1:
                    v.wait_ge(lev_ready, 1)
                    nc.vector.tensor_copy(off[:, :, :], ps[:, 0, :].rearrange("p (h t) -> p h t", t=P)).then_inc(lev_taken, 1)
                if i >= 2:
                    add_level(i - 1)
            add_level(len(LEVELS))
            add_level(len(LEVELS) + 1)
            v.wait_ge(ostd_ready, LAYERS + 1)
            step(nc.vector.reciprocal(rstd[:, :], std[:, :]))
            for c in range(DC):
                op = nc.vector.scalar_tensor_tensor(out=go[:, c, :], in0=go[:, c, :], scalar=cols[:, C_GLAN + c % 2:C_GLAN + c % 2 + 1],
                                                    in1=rstd[:, c // 2 * TOK:(c // 2 + 1) * TOK], op0=ALU.mult, op1=ALU.mult)
            step(op)
            nc.vector.tensor_tensor(go[:, :, :], go[:, :, :], gr[:, :, :], ALU.mult).then_inc(gla_ready, 1)
            for m in range(DC):
                v.wait_ge(sig_ready, LAYERS * DC + m + 1)
                v.wait_ge(ys_ready, LAYERS * DC + m + 1)
                b0 = 2 + 2 * (m % 2)
                step(nc.vector.tensor_tensor(sg2[:, m % 2, :, :], sg2[:, m % 2, :, :], ps[:, b0 + 1, :].rearrange("p (a b) -> p a b", b=TOK), ALU.mult))
                nc.vector.tensor_tensor(merged2[:, m, :], sg2[:, m % 2, 0, :], sg2[:, m % 2, 1, :], ALU.add).then_inc(merged_ready, 1)

            def add_gated(c, bank, half, gate):
                g = mod[:, gate * DC + c:gate * DC + c + 1]
                return nc.vector.scalar_tensor_tensor(out=x[:, c, :], in0=ps[:, bank, half * TOK:(half + 1) * TOK], scalar=g,
                                                      in1=x[:, c, :], op0=ALU.mult, op1=ALU.add)

            for b in range(OUTS):
                v.wait_ge(out_ready, LAYERS * OUTS + b + 1)
                add_gated(2 * b, DOWN + b, 0, 2)
                op = add_gated(2 * b + 1, DOWN + b, 1, 2)
            op.then_inc(x_ready, 1)
            mod_norm(2, 1)
            v.wait_ge(route_ready, 1)
            for t in range(TT):
                step(nc.vector.tensor_tensor(lgt[:, t, :], ps[:, 3, t * EXPERTS:(t + 1) * EXPERTS], brouter[:, :], ALU.add))
                step(nc.vector.max(top8, lgt[:, t, :]))
                step(nc.vector.max_index(topi, top8, lgt[:, t, :]))
                step(nc.vector.tensor_copy(topf, topi[:, 0:TOPK]))
                nc.vector.tensor_scalar(small[:, 56:57], top8[:, 0:1], -1.0, None, ALU.mult).then_inc(top_ready, 1)
                v.wait_ge(topexp_ready, t + 1)
                step(nc.vector.reciprocal(small[:, 58:59], small[:, 57:58]))
                step(nc.vector.tensor_scalar(topw, topw, small[:, 58:59], None, ALU.mult))
                for k in range(TOPK):
                    op = nc.vector.tensor_scalar(eqs[:, k, :], iota, topf[:, k:k + 1], topw[:, k:k + 1], ALU.is_equal, ALU.mult)
                step(op)
                step(nc.vector.tensor_tensor(eqs[:, 0:2, :], eqs[:, 0:2, :], eqs[:, 2:4, :], ALU.add))
                op = nc.vector.tensor_tensor(wt[:, t, :], eqs[:, 0, :], eqs[:, 1, :], ALU.add)
                if t < TT - 1:
                    step(op)
            op.then_inc(wt_ready, 1)
            v.wait_ge(wtT_ready, 1)
            nc.vector.tensor_copy(wtT[0:EXPERTS, :], ps[0:EXPERTS, 3, 0:TOK]).then_inc(wtT_taken, 1)
            v.wait_ge(wtT_taken, 1)

            moe_base = step.base + step.k
            first_k = step.k
            with v.Fori(0, EXPERTS) as e:
                step.base, step.k = moe_base + e * MOE_STEPS, 0
                nc.vector.tensor_scalar(wsel[0:EXPERTS, 0, :], wtT[0:EXPERTS, :], ident[0:EXPERTS, bass.ds(e, 1)], None, ALU.mult).then_inc(wsel_ready, 1)
                v.wait_ge(wb_ready, e + 1)
                nc.vector.tensor_copy(wb[:, 0, :], ps[:, 3, 0:TOK]).then_inc(wb_taken, 1)
                for j in range(DC):
                    hid = ps[:, j % 2, :]
                    v.wait_ge(hid_ready, e * DC + j + 1)
                    nc.vector.tensor_scalar(glu[:, j % 2, :], hid[:, 0:TOK], cols[:, bass.ds(e * 16 + (C_BEXP + j), 1)], LIMIT, ALU.add, ALU.min).then_inc(glu_ready, 1)
                    step(nc.vector.tensor_scalar(lin[:, j % 2, :], hid[:, TOK:2 * TOK], cols[:, bass.ds(e * 16 + (C_BEXP + DC + j), 1)], LIMIT, ALU.add, ALU.min))
                    step(nc.vector.tensor_scalar(lin[:, j % 2, :], lin[:, j % 2, :], -LIMIT, 1.0, ALU.max, ALU.add))
                    step(nc.vector.tensor_tensor(lin[:, j % 2, :], lin[:, j % 2, :], wb[:, 0, :], ALU.mult))
                    v.wait_ge(glu_ready, e * DC + j + 1)
                    step(nc.vector.tensor_tensor(lin[:, j % 2, :], lin[:, j % 2, :], glu[:, j % 2, :], ALU.mult))
                    v.wait_ge(esig_ready, e * DC + j + 1)
                    nc.vector.tensor_tensor(eact[:, j % 2, :], lin[:, j % 2, :], sig[:, j % 2, :], ALU.mult).then_inc(eact_ready, 1)
                assert step.k == MOE_STEPS, step.k
            step.base, step.k = moe_base + EXPERTS * MOE_STEPS, 0
            v.wait_ge(moe_used, EXPERTS * DC)
            for c in range(DC):
                op = add_gated(c, DOWN + c // 2, c % 2, 5)
            op.then_inc(x_ready, 1)
            norm(LAYERS, 3, cols[:, C_NF:C_NF + DC]).then_inc(h_ready, 1)

        @block.tensor
        def _(pe):
            mm_ = nc.tensor.matmul

            def sums(l, n, tiles=0):
                pe.wait_ge(sq_ready, l * NORMS + n + 1)
                for c in range(DC):
                    mm = mm_(ps[:, SSUM, 0:TOK], ones, sq[:, c, :], start=c == 0, stop=c == DC - 1)
                    if c == 0 and tiles:
                        mm.then_inc(tile_used, tiles)
                mm.then_inc(ssum_ready, 1)

            def ffn_in(l, f, t0, i, g=0):
                s = (i - 1) % 5
                t = t0 + i
                slot = ring[:, t % RING, :]
                pe.wait_ge(tile_landed[t % RING], (l * GROUPS + g + t // RING + 1) * 16)
                for half in range(2):
                    for c in range(DC):
                        b = (half * DC + c) * P
                        mm = mm_(ps[:, ff_banks[s], half * TOK:(half + 1) * TOK], slot[:, b:b + P], h[:, c, :],
                                 start=c == 0, stop=c == DC - 1)
                mm.then_inc(gu_ready, 1)

            def ffn_down(l, f, t0, i, g=0):
                s = (i - 1) % 5
                slot = ring[:, (t0 + i) % RING, :]
                pe.wait_ge(act_ready, l * (2 * FF_TILES) + g * 5 + (f * FF_TILES + i + 1))
                for m in range(DC):
                    b = (2 * DC + m) * P
                    mm = mm_(ps[:, DOWN + m // 2, m % 2 * TOK:(m % 2 + 1) * TOK], slot[:, b:b + P], act[:, s, :],
                             start=i == 0 and m % 2 == 0, stop=i == FF_TILES - 1, skip_group_check=True)
                mm.then_inc(tile_used, 1)

            def ffn(l, f, t0):
                ffn_in(l, f, t0, 0)
                ffn_in(l, f, t0, 1)
                ffn_down(l, f, t0, 0)
                with pe.Fori(0, (FF_TILES - 2) // 5) as g:
                    for s in range(5):
                        ffn_in(l, f, t0, 2 + s, g)
                        ffn_down(l, f, t0, 1 + s, g)
                ffn_down(l, f, t0, FF_TILES - 1)

            def project_t(w, bank, half, m=P):
                for c in range(DC):
                    mm = w.used(mm_(ps[0:m, bank, half * TOK:(half + 1) * TOK], w.take()[:, 0:m], h[:, c, :],
                                    start=c == 0, stop=c == DC - 1))
                return mm

            def project_tok(w, banks, n):
                for c in range(DC):
                    blk = w.take(n)
                    for t in range(TT):
                        mm = mm_(ps[:, banks[t], 0:n * P], h[:, c, t * P:(t + 1) * P], blk, start=c == 0, stop=c == DC - 1)
                        if t == TT - 1:
                            w.used(mm)
                        if c == DC - 1:
                            mm.then_inc(proj_ready, 1)

            def out_proj(w, src):
                for m in range(DC):
                    for c in range(DC):
                        mm = w.used(mm_(ps[:, DOWN + m // 2, m % 2 * TOK:(m % 2 + 1) * TOK], w.take(), src[:, c, :],
                                        start=c == 0, stop=c == DC - 1))
                    if m % 2:
                        mm.then_inc(out_ready, 1)

            pe.wait_ge(konst_landed, 16)
            pe.wait_ge(x_landed, 16)
            for i in range(OUTS):
                for c in range(2 * i, 2 * i + 2):
                    for t in range(TT):
                        mm = nc.tensor.transpose(ps[:, 4 + i, c % 2 * TOK + t * P:c % 2 * TOK + (t + 1) * P], x_tok[:, t, c * P:(c + 1) * P], ident)
                mm.then_inc(xt_ready, 1)
            pe.wait_ge(rel_landed, 2 * 16)
            for i in range(BIAS_HEADS):
                if i >= 4:
                    pe.wait_ge(vec_taken, i - 3)
                mm_(ps[:, i % 4, :], relb[0:BUCKETS + 1, i, :], onehot[0:BUCKETS + 1, min(i // DIL_SLOTS, DIL_GROUPS), :],
                    start=True, stop=True).then_inc(vec_ready, 1)
            pe.wait_ge(vec_taken, BIAS_HEADS)

            with pe.Fori(0, LAYERS) as l:
                sums(l, 0)
                pe.wait_ge(h_ready, l * NORMS + 1)
                ffn(l, 0, 0)
                sums(l, 1)
                pe.wait_ge(h_ready, l * NORMS + 2)
                w = Blocks(pe, l, MIX0)

                def free_bank(r):
                    if r >= 4:
                        pe.wait_ge(proj_taken, l * PROJ + r - 3)

                for r in range(QK_CHUNKS // 2):
                    free_bank(r)
                    project_t(w, r % 4, 0)
                    project_t(w, r % 4, 1).then_inc(proj_ready, 1)
                free_bank(8)
                project_tok(w, (7 % 4, 8 % 4), 4)
                free_bank(10)
                project_tok(w, (9 % 4, 10 % 4), 3)
                pe.wait_ge(proj_taken, l * PROJ + 11)

                def logits(u):
                    if u >= 2:
                        pe.wait_ge(scores_made, l * UNITS + u - 1)
                    b = 2 * (u % 2)
                    if u < DIL_UNITS:
                        s, qt = divmod(u, TT)
                        jobs = [(s, g, DIL_GROUPS + g) for g in range(DIL_GROUPS)]
                    else:
                        hh, qt = divmod(u - DIL_UNITS, TT)
                        jobs = [(m, 2 * DIL_GROUPS + hh, 2 * DIL_GROUPS + DIFF_HEADS + hh) for m in range(2)]
                    for i, (s, cq, ck) in enumerate(jobs):
                        rows = slice(s * DH, (s + 1) * DH)
                        col = 2 * i if u >= DIL_UNITS else i
                        mm = mm_(ps[:, b + col // 2, col % 2 * TOK:(col % 2 + 1) * TOK], qk[rows, cq, qt * P:(qt + 1) * P],
                                 qk[rows, ck, :], start=True, stop=True)
                    mm.then_inc(logits_ready, 1)

                def transposes(u):
                    pe.wait_ge(probs_ready, l * UNITS + u + 1)
                    if u >= 1:
                        pe.wait_ge(pt_taken, l * UNITS + u)
                    for i in range(6 if u < DIL_UNITS else 2):
                        mm = nc.tensor.transpose(ps[:, 4 + i // 4, i % 4 * P:(i % 4 + 1) * P], S[:, u % 2, i * P:(i + 1) * P], ident)
                    mm.then_inc(pt_ready, 1)

                def weighted_values(u):
                    pe.wait_ge(pt_taken, l * UNITS + u + 1)
                    if u < DIL_UNITS:
                        s, qt = divmod(u, TT)
                        for i in range(6):
                            hd = 2 * (i // 2) + s
                            mm = mm_(ps[s * DH:(s + 1) * DH, 6, qt * P:(qt + 1) * P], vb[:, i % 2, hd * DH:(hd + 1) * DH],
                                     PT[:, u % 2, i * P:(i + 1) * P], start=i == 0, stop=i == 5)
                        if u == DIL_UNITS - 1:
                            mm.then_inc(o_ready, 1)
                    else:
                        hh, qt = divmod(u - DIL_UNITS, TT)
                        if hh >= 1 and qt == 0:
                            pe.wait_ge(o_taken, l * 5 + hh)
                        for i in range(2):
                            mm = mm_(ps[:, 7 - hh % 2, qt * P:(qt + 1) * P], vc[:, i, hh * P:(hh + 1) * P],
                                     PT[:, u % 2, i * P:(i + 1) * P], start=i == 0, stop=i == 1)
                        if qt == 1:
                            mm.then_inc(o_ready, 1)

                for u in range(UNITS + 2):
                    if u < UNITS:
                        logits(u)
                    if 1 <= u <= UNITS:
                        transposes(u - 1)
                    if u >= 2:
                        weighted_values(u - 2)
                pe.wait_ge(scores_made, l * UNITS + UNITS)
                project_tok(w, (11 % 4, 12 % 4), 4)
                project_tok(w, (13 % 4, 14 % 4), 4)
                pe.wait_ge(osq_ready, l + 1)
                for i in range(2):
                    mm = mm_(ps[:, 6 + i, :], ones, sq[:, 2 * i:2 * i + 2, :], start=True, stop=True)
                mm.then_inc(ossum_ready, 1)
                pe.wait_ge(proj_taken, l * PROJ + PROJ)

                def dft_channels(g):
                    pe.wait_ge(dft1_taken, l * FOURIER_GROUPS + g + 1)
                    if g >= 2:
                        pe.wait_ge(dft2_taken, l * FOURIER_GROUPS + g - 1)
                    for i in range(2):
                        mm = mm_(ps[:, 2 + g % 2, 0:TOK], dch[:, i, :], dft1[:, g % 2, i * TOK:(i + 1) * TOK],
                                 start=i == 0, stop=i == 1)
                    mm.then_inc(dft2_ready, 1)

                for g in range(FOURIER_GROUPS):
                    if g >= 2:
                        pe.wait_ge(dft1_taken, l * FOURIER_GROUPS + g - 1)
                    for t in range(TT):
                        mm = mm_(ps[:, g % 2, :], a_tok[:, t, g * P:(g + 1) * P], dseq[:, t, :], start=t == 0, stop=t == TT - 1)
                    mm.then_inc(dft1_ready, 1)
                    if g >= 1:
                        dft_channels(g - 1)
                dft_channels(FOURIER_GROUPS - 1)
                pe.wait_ge(pt_taken, l * UNITS + UNITS)
                for m in range(DC):
                    b0 = 4 * (1 - m % 2)
                    if m == 1:
                        pe.wait_ge(dft2_taken, l * FOURIER_GROUPS + FOURIER_GROUPS)
                    if m >= 2:
                        pe.wait_ge(merged_ready, l * DC + m - 1)
                    for j in range(3):
                        mm = project_t(w, b0 + j // 2, j % 2)
                    mm.then_inc(gates_ready, 1)
                    if m == 0:
                        pe.wait_ge(dft2_taken, l * FOURIER_GROUPS + FOURIER_GROUPS)
                        pe.wait_ge(o_taken, l * 5 + 5)
                        pe.wait_ge(yc_ready, l + 1)
                    for c in range(FOURIER_GROUPS):
                        w.used(mm_(ps[:, b0 + 2, 0:TOK], w.take(), four[:, c, :], start=c == 0, stop=c == FOURIER_GROUPS - 1))
                    w.used(mm_(ps[:, b0 + 2, TOK:2 * TOK], w.take(), ob[:, :], start=True, stop=True))
                    for c in range(DIFF_HEADS):
                        mm = w.used(mm_(ps[:, b0 + 3, 0:TOK], w.take(), oc[:, c, :], start=c == 0, stop=c == DIFF_HEADS - 1))
                    mm.then_inc(ys_ready, 1)
                last = MIX0 + MIX_TILES
                for t in range(last, last + PAD_TILES):
                    pe.wait_ge(tile_landed[t % RING], (l * GROUPS + t // RING + 1) * 16)
                pe.wait_ge(merged_ready, l * DC + DC)
                out_proj(w, merged)
                sums(l, 2, PAD_TILES + 1)
                pe.wait_ge(h_ready, l * NORMS + 3)
                ffn(l, 1, FFN2)

            sums(LAYERS, 0)
            w = Blocks(pe, LAYERS, 0)
            pe.wait_ge(cact_ready, 1)
            for m in range(ADA):
                for c in range(DC):
                    mm = w.used(mm_(ps[:, 3, m:m + 1], w.take(), small[:, 16 + c:17 + c], start=c == 0, stop=c == DC - 1))
            mm.then_inc(ada_ready, 1)
            sums(LAYERS, 1)
            pe.wait_ge(h_ready, LAYERS * NORMS + 1)
            R0 = LAYERS * PROJ

            def free2(r):
                if r >= 4:
                    pe.wait_ge(proj_taken, R0 + r - 3)

            def project_pairs(r0, n):
                for r in range(r0, r0 + n):
                    free2(r)
                    project_t(w, r % 4, 0)
                    project_t(w, r % 4, 1).then_inc(proj_ready, 1)

            for i in range(2):
                free2(2 * i + 1)
                project_tok(w, (2 * i % 4, (2 * i + 1) % 4), 4)
            project_pairs(4, 8)
            for i in range(HEADS):
                if i >= 2:
                    pe.wait_ge(roped, i - 1)
                pe.wait_ge(proj_taken, R0 + 5 + i)
                mm_(ps[0:ROT, 4 + i % 2, :], rotT, mqk[0:ROT, 2 * i:2 * i + 2, :], start=True, stop=True).then_inc(rot_ready, 1)
            pe.wait_ge(roped, HEADS)
            U0 = LAYERS * UNITS
            for u in range(HEADS + 2):
                if u < HEADS:
                    if u >= 2:
                        pe.wait_ge(scores_made, U0 + u - 1)
                    q, k = mqk[:, u, :], mqk[:, HEADS + u, :]
                    mm_(ps[:, u % 2, 0:P], q[:, 0:P], k[:, 0:P], start=True, stop=True)
                    mm_(ps[:, u % 2, P:3 * P], q[:, P:TOK], k, start=True, stop=True).then_inc(logits_ready, 1)
                if 1 <= u <= HEADS:
                    pe.wait_ge(probs_ready, U0 + u)
                    if u >= 2:
                        pe.wait_ge(pt_taken, U0 + u - 1)
                    for i in range(3):
                        mm = nc.tensor.transpose(ps[:, 4, i * P:(i + 1) * P], mS[:, (u - 1) % 2, i * P:(i + 1) * P], ident)
                    mm.then_inc(pt_ready, 1)
                if u >= 2:
                    hd = u - 2
                    pe.wait_ge(pt_taken, U0 + hd + 1)
                    if hd >= 2:
                        pe.wait_ge(o_taken, LAYERS * 5 + hd - 1)
                    vs = [mv[:, t, hd * P:(hd + 1) * P] for t in range(TT)]
                    pt = mPT[:, hd % 2, :]
                    mm_(ps[:, 6 + hd % 2, 0:P], vs[0], pt[:, 0:P], start=True, stop=True)
                    mm_(ps[:, 6 + hd % 2, P:TOK], vs[0], pt[:, P:2 * P], start=True, stop=False)
                    mm_(ps[:, 6 + hd % 2, P:TOK], vs[1], pt[:, 2 * P:3 * P], start=False, stop=True).then_inc(o_ready, 1)
            pe.wait_ge(scores_made, U0 + HEADS)
            project_pairs(12, 4)
            free2(16)
            project_t(w, 0, 0, RANK).then_inc(proj_ready, 1)
            project_pairs(17, 4)
            free2(22)
            project_tok(w, (21 % 4, 22 % 4), 4)
            free2(24)
            project_tok(w, (23 % 4, 24 % 4), 4)
            pe.wait_ge(pt_taken, U0 + HEADS)
            pe.wait_ge(proj_taken, R0 + 17)
            for hh in range(GLA_HEADS):
                mm = mm_(ps[:, 4 + hh // 2, hh % 2 * TOK:(hh % 2 + 1) * TOK], glaw[:, hh * P:(hh + 1) * P], glow[0:RANK, :], start=True, stop=True)
            mm.then_inc(z_ready, 1)
            pe.wait_ge(proj_taken, R0 + 25)
            pe.wait_ge(k_decayed, 1)
            pe.wait_ge(qk_decayed, 1)
            for hh in range(GLA_HEADS):
                mm = mm_(ps[:, 0, hh * P:(hh + 1) * P], kd[:, hh, 0:P], qd[:, hh, P:TOK], start=True, stop=True)
            mm.then_inc(lev_ready, 1)
            for i in range(1, len(LEVELS) + 2):
                if i <= len(LEVELS):
                    pe.wait_ge(k_decayed, i + 1)
                    pe.wait_ge(qk_decayed, i + 1)
                q, k = (qd, kd) if i <= len(LEVELS) else (gqk[:, 0:GLA_HEADS], gqk[:, GLA_HEADS:])
                if i == 2:
                    pe.wait_ge(lev_taken, 1)
                if i >= 3:
                    pe.wait_ge(lev_taken, 1 + (i - 2) * TT)
                for t in range(TT):
                    for hh in range(GLA_HEADS):
                        mm = mm_(ps[:, 2 * (i % 2) + t, hh * P:(hh + 1) * P], k[:, hh, t * P:(t + 1) * P], q[:, hh, t * P:(t + 1) * P],
                                 start=True, stop=True)
                    mm.then_inc(lev_ready, 1)
            pe.wait_ge(scores_done, 1)
            for c in range(DC):
                hh = c // 2
                o = ps[:, 4 + c // 2, c % 2 * TOK:(c % 2 + 1) * TOK]
                vs = [gv[:, t, c * P:(c + 1) * P] for t in range(TT)]
                mm_(o[:, 0:P], vs[0], acc[:, 0, hh, :], start=True, stop=True)
                mm_(o[:, P:TOK], vs[0], off[:, hh, :], start=True, stop=False)
                mm = mm_(o[:, P:TOK], vs[1], acc[:, 1, hh, :], start=False, stop=True)
                if c % 2:
                    mm.then_inc(go_ready, 1)
            pe.wait_ge(osq_ready, LAYERS + 1)
            for hh in range(GLA_HEADS):
                for i in range(2):
                    mm = mm_(ps[:, hh // 2, hh % 2 * TOK:(hh % 2 + 1) * TOK], ones, sq[:, 2 * hh + i, :], start=i == 0, stop=i == 1)
            mm.then_inc(ossum_ready, 1)
            for m in range(DC):
                b0 = 2 + 2 * (m % 2)
                if m >= 2:
                    pe.wait_ge(merged_ready, LAYERS * DC + m - 1)
                project_t(w, b0, 0)
                project_t(w, b0, 1).then_inc(gates_ready, 1)
                for c in range(HEADS):
                    w.used(mm_(ps[:, b0 + 1, 0:TOK], w.take(), oa[:, c, :], start=c == 0, stop=c == DC - 1))
                if m == 0:
                    pe.wait_ge(gla_ready, 1)
                for c in range(DC):
                    mm = w.used(mm_(ps[:, b0 + 1, TOK:2 * TOK], w.take(), go[:, c, :], start=c == 0, stop=c == DC - 1))
                mm.then_inc(ys_ready, 1)
            pe.wait_ge(merged_ready, LAYERS * DC + DC)
            out_proj(w, merged2)
            sums(LAYERS, 2, 1)
            pe.wait_ge(h_ready, LAYERS * NORMS + 2)
            for t in range(TT):
                for c in range(DC):
                    mm = mm_(ps[:, 3, t * EXPERTS:(t + 1) * EXPERTS], h[:, c, t * P:(t + 1) * P], router[:, c, :], start=c == 0, stop=c == DC - 1)
            mm.then_inc(route_ready, 1)
            pe.wait_ge(wt_ready, 1)
            for t in range(TT):
                mm = nc.tensor.transpose(ps[0:EXPERTS, 3, t * P:(t + 1) * P], wt[:, t, :], ident)
            mm.then_inc(wtT_ready, 1)
            pe.wait_ge(wtT_taken, 1)
            for m in range(DC):
                mm_(ps[:, DOWN + m // 2, m % 2 * TOK:(m % 2 + 1) * TOK], bout[:, m * P:(m + 1) * P], wtT[0:EXPERTS, :],
                    start=m % 2 == 0, stop=False, skip_group_check=True)

            def slot(j):
                return ring[:, j, :] if j < RING else moe_hi[:, j - RING, :]

            def expert_in(e, j):
                pe.wait_ge(moe_landed[j], (e + 1) * 16)
                for half in range(2):
                    for c in range(DC):
                        b = (half * DC + c) * P
                        mm = mm_(ps[:, j % 2, half * TOK:(half + 1) * TOK], slot(j)[:, b:b + P], h[:, c, :], start=c == 0, stop=c == DC - 1)
                mm.then_inc(hid_ready, 1)

            def spread_weights(e):
                pe.wait_ge(wsel_ready, e + 1)
                mm_(ps[:, 3, 0:TOK], ones[0:EXPERTS, :], wsel[0:EXPERTS, 0, :], start=True, stop=True).then_inc(wb_ready, 1)

            def expert_out(e, j, last=False):
                pe.wait_ge(eact_ready, e * DC + j + 1)
                for m in range(DC):
                    b = (2 * DC + m) * P
                    mm = mm_(ps[:, DOWN + m // 2, m % 2 * TOK:(m % 2 + 1) * TOK], slot(j)[:, b:b + P], eact[:, j % 2, :],
                             start=False, stop=last, skip_group_check=True)
                mm.then_inc(moe_used, 1)

            expert_in(0, 0)
            with pe.Fori(0, EXPERTS - 1) as e:
                spread_weights(e)
                for j in range(DC - 1):
                    expert_in(e, j + 1)
                    expert_out(e, j)
                expert_in(e + 1, 0)
                expert_out(e, DC - 1)
            spread_weights(EXPERTS - 1)
            for j in range(DC):
                if j < DC - 1:
                    expert_in(EXPERTS - 1, j + 1)
                expert_out(EXPERTS - 1, j, j == DC - 1)
            sums(LAYERS, 3)
            pe.wait_ge(h_ready, LAYERS * NORMS + 3)
            for i in range(2 * OUTS):
                t, half = divmod(i, OUTS)
                if i >= 4:
                    pe.wait_ge(ytok_taken, i - 3)
                for c in range(2):
                    mm = nc.tensor.transpose(ps[:, i % 4, c * P:(c + 1) * P], h[:, 2 * half + c, t * P:(t + 1) * P], ident)
                mm.then_inc(ytok_ready, 1)


def constants():
    k = np.zeros((P, KONST), np.float32)
    k[:, K_ID:K_ID + P] = np.eye(P)
    k[:, K_ONES:K_ONES + TOK] = 1.0
    r = np.arange(P)
    tri = np.where(r[None, :] <= r[:, None], 0.0, NEG)
    k[:, K_CAUSAL:K_CAUSAL + 384] = np.concatenate([tri, np.zeros((P, P)), tri], 1)
    for i, s in enumerate(LEVELS):
        j, q = r[:, None], r[None, :]
        k[:, K_LEVEL + i * P:K_LEVEL + (i + 1) * P] = (j // (2 * s) == q // (2 * s)) & (j % (2 * s) < s) & (q % (2 * s) >= s)
    k[:, K_LEVEL + 7 * P:K_LEVEL + 8 * P] = np.eye(P)
    k[:, K_IOTA:K_IOTA + EXPERTS] = np.arange(EXPERTS)
    k[:, K_EPS:K_EPS + 3] = (EPS1, EPS2, 1.0)
    ang = 2 * np.pi * np.outer(np.arange(TOK), np.arange(TOK)) / TOK
    seq = np.concatenate([np.cos(ang), np.sin(ang)], 1) / math.sqrt(TOK)
    k[:, K_DSEQ:K_DSEQ + 2 * VEC] = seq.reshape(TT, P, VEC).transpose(1, 0, 2).reshape(P, -1)
    ang = 2 * np.pi * np.outer(r, r) / P
    k[:, K_DCH:K_DCH + 2 * P] = np.concatenate([np.cos(ang), -np.sin(ang)], 1) / math.sqrt(P)
    half = ROT // 2
    freq = np.float32(500000.0) ** (-np.arange(half, dtype=np.float32) * np.float32(2.0) / np.float32(ROT))
    a = (np.arange(TOK, dtype=np.float32)[:, None] * freq[None, :]).T
    k[0:ROT, K_COS:K_COS + TOK] = np.cos(np.concatenate([a, a]))
    k[0:ROT, K_SIN:K_SIN + TOK] = np.sin(np.concatenate([a, a]))
    for i in range(half):
        k[half + i, K_ROT + i] = -1.0
        k[i, K_ROT + half + i] = 1.0
    return k


def bucket_tables():
    rel = np.arange(VEC) - (TOK - 1)
    half = BUCKETS // 2
    exact = half // 2
    n = np.abs(rel)
    nf = np.maximum(n, 1).astype(np.float32)
    large = exact + (np.log(nf / np.float32(exact)) / np.float32(math.log(MAX_DISTANCE / exact)) * np.float32(half - exact)).astype(np.int32)
    bucket = np.where(rel > 0, half, 0) + np.where(n < exact, n, np.minimum(large, half - 1))
    tables = np.zeros((BUCKETS + 1, 4, VEC), np.float32)
    for g in range(4):
        seen = np.ones(VEC, bool)
        if g < DIL_GROUPS:
            window, dil = DIL_PAIRS[g]
            seen = (n % dil == 0) & (n // dil <= window // (2 * dil))
        tables[bucket[seen], g, np.nonzero(seen)[0]] = 1.0
        tables[BUCKETS, g, ~seen] = NEG
    return tables


def by_output(w):
    k, n = w.shape
    return w.reshape(k // P, P, n // P, P).transpose(2, 0, 1, 3).reshape(-1, P, P)


def by_input(w, n):
    k, cols = w.shape
    return w.reshape(k // P, P, cols // (n * P), n, P).transpose(2, 0, 3, 1, 4).reshape(-1, P, P)


def tiles(blocks, n):
    b = np.concatenate(blocks)
    b = np.concatenate([b, np.zeros((n * TILE_BLOCKS - len(b), P, P), np.float32)])
    return b.reshape(n, TILE_BLOCKS, P, P).transpose(0, 2, 1, 3).reshape(n, P, TILE)


def ffn_tiles(gate, up, down):
    f = gate.shape[-1] // P
    t = np.empty((f, P, 3, DC, P), np.float32)
    t[:, :, 0] = gate.reshape(DC, P, f, P).transpose(2, 1, 0, 3)
    t[:, :, 1] = up.reshape(DC, P, f, P).transpose(2, 1, 0, 3)
    t[:, :, 2] = down.reshape(f, P, DC, P)
    return t.reshape(f, P, TILE)


def columns(v):
    v = np.asarray(v, np.float32).reshape(-1, P)
    return v.T


def lay_out(i):
    parts = []
    for l in range(LAYERS):
        parts.append(ffn_tiles(i["w_ffn1_gate"][l], i["w_ffn1_up"][l], i["w_ffn1_down"][l]))
        w_in = i["w_in"][l]
        qa, ka, va = (w_in[:, D + 384 * n:D + 384 * (n + 1)] for n in range(3))
        qc, kc, vcw = (w_in[:, 2176 + 512 * n:2176 + 512 * (n + 1)] for n in range(3))
        blocks = [by_output(w) for w in (qa, ka, qc, kc)] + [by_input(vcw, 4), by_input(va, 3), by_input(w_in[:, :D], 4)]
        gate = by_output(i["w_gate"][l]).reshape(3, DC, DC, P, P).transpose(1, 0, 2, 3, 4).reshape(DC, 3 * DC, P, P)
        branch = [by_output(i[n][l]).reshape(DC, -1, P, P) for n in ("w_br_a", "w_br_b", "w_br_c")]
        blocks += [np.concatenate([gate] + branch, 1).reshape(-1, P, P), by_output(i["w_out"][l])]
        parts.append(tiles(blocks, MIX_TILES + PAD_TILES))
        parts.append(ffn_tiles(i["w_ffn2_gate"][l], i["w_ffn2_up"][l], i["w_ffn2_down"][l]))
    w_in = i["w_in_2"][0]
    cut = np.cumsum([0, D, D, D, 512, 512, D, D, RANK, D, D])
    mq, mk, mvw, gq, gk, gvw, grw, low, ga, gb = (w_in[:, a:b] for a, b in zip(cut[:-1], cut[1:]))
    low = np.pad(low, ((0, 0), (0, P - RANK)))
    blocks = [by_output(i["w_ada_2"][0]), by_input(mvw, 4)] + [by_output(w) for w in (mq, mk, gq, gk, low, grw)] + [by_input(gvw, 4)]
    blocks.append(np.concatenate([by_output(w).reshape(DC, DC, P, P) for w in (ga, gb, i["w_o_moba_2"][0], i["w_o_gla_2"][0])], 1).reshape(-1, P, P))
    blocks.append(by_output(i["w_out_2"][0]))
    parts.append(tiles(blocks, SEC_TILES))
    w_exp = i["w_exp_in_2"][0]
    experts = np.empty((EXPERTS, DC, P, 3, DC, P), np.float32)
    for half in range(2):
        experts[:, :, :, half] = w_exp[:, :, half::2].reshape(EXPERTS, DC, P, DC, P).transpose(0, 3, 2, 1, 4)
    experts[:, :, :, 2] = i["w_exp_out_2"][0].reshape(EXPERTS, DC, P, DC, P)

    layers = np.zeros((P, LAYERS, LP), np.float32)
    for l in range(LAYERS):
        lam_init = 0.8 - 0.6 * math.exp(-0.3 * l)
        layers[:, l, :LP_LAM] = np.concatenate([columns(i[n][l]) for n in ("g_ffn1", "g_mix", "g_ffn2", "b_gate", "subln_g")]
                                               + [np.full((P, 1), lam_init), np.full((P, 1), 1 - lam_init)], 1)
        layers[:, l, LP_LAM:] = np.concatenate([i[n][l] for n in ("lam_q1", "lam_k1", "lam_q2", "lam_k2")])[None]
    b_exp = i["b_exp_in_2"][0]
    b_exp = np.concatenate([b_exp[:, 0::2].reshape(EXPERTS, DC, P), b_exp[:, 1::2].reshape(EXPERTS, DC, P)], 1)
    cols = np.concatenate([columns(i[n]) for n in ("c_2", "g_final", "b_ada_2", "norm1_w_2", "gla_gate_b_2", "gla_norm_w_2", "b_merge_2",
                                                   "norm2_w_2", "final_norm_w_2")] + [columns(b_exp)], 1)
    relb = np.ones((BUCKETS + 1, BIAS_HEADS, P), np.float32)
    relb[:BUCKETS] = i["rel_bias"][:, :, None]
    return {
        "stream": np.concatenate(parts),
        "experts": experts.reshape(EXPERTS * DC, P, TILE),
        "x": i["x"].reshape(TOK, D),
        "konst": constants(),
        "layers": layers,
        "cols": cols,
        "relb": relb,
        "onehot": bucket_tables(),
        "glaw": i["gla_gate_w_2"][0],
        "router": i["w_router_2"][0].reshape(DC, P, EXPERTS).transpose(1, 0, 2),
        "brouter": np.broadcast_to(i["b_router_2"], (P, EXPERTS)),
        "bout": i["b_exp_out_2"][0],
    }


def kernel(**inputs):
    import concourse.bacc as bacc
    from concourse.bass_utils import run_bass_kernel_spmd

    arrays = {n: np.ascontiguousarray(a) for n, a in lay_out({k: np.asarray(v) for k, v in inputs.items()}).items()}
    nc = bacc.Bacc("TRN2", target_bir_lowering=False, num_devices=1)
    args = [nc.dram_tensor("in_" + n, a.shape, F32, kind="ExternalInput").ap() for n, a in arrays.items()]
    rows = nc.dram_tensor("bias_rows", (BIAS_HEADS, P, VEC), F32, kind="Internal").ap()
    out = nc.dram_tensor("out", (TOK, D), F32, kind="ExternalOutput").ap()
    build(nc, *args, rows, out)
    r = run_bass_kernel_spmd(nc, [{"in_" + n: a for n, a in arrays.items()}], core_ids=[0])
    return r.results[0]["out"].reshape(1, TOK, D)
```

```python
import math
from contextlib import ExitStack

import concourse.bass as bass
from concourse import mybir
import numpy as np

F32 = mybir.dt.float32
U32 = mybir.dt.uint32
I32 = mybir.dt.int32
F32R = mybir.dt.float32r
ALU = mybir.AluOpType
ACT = mybir.ActivationFunctionType
AX = mybir.AxisListType

P = 128
TOK = 256
TT = TOK // P
D = 1024
DC = D // P
LAYERS = 2
D_FF = 2816
FF_TILES = D_FF // P
TILE_BLOCKS = 3 * DC
TILE = TILE_BLOCKS * P
RING = 5
WORK, WORK2 = 16128, 4352

EPS1, EPS2, SUBLN_EPS = 1e-6, 1e-5, 1e-5
NEG = -1e30

DIL_PAIRS = ((128, 1), (512, 4), (2048, 16))
DIL_GROUPS, DIL_SLOTS, DH = 3, 2, 64
DIFF_HEADS = 4
BIAS_HEADS = DIL_GROUPS * DIL_SLOTS + DIFF_HEADS
BUCKETS, MAX_DISTANCE = 32, 1024
QK_CHUNKS = 2 * DIL_GROUPS + 2 * DIFF_HEADS
UNITS = DIL_SLOTS * TT + DIFF_HEADS * TT
DIL_UNITS = DIL_SLOTS * TT
FOURIER_GROUPS = 8
MERGE_BLOCKS = 3 * DC + DC + 1 + DIFF_HEADS
VEC = 2 * TOK
PROJ = QK_CHUNKS // 2 + 2 * TT + 2 * TT
MIX_BLOCKS = QK_CHUNKS * DC + 3 * DC + 4 * DC + 8 * DC + DC * MERGE_BLOCKS + DC * DC
MIX_TILES = -(-MIX_BLOCKS // TILE_BLOCKS)
LAYER_TILES = -(-(2 * FF_TILES + MIX_TILES) // RING) * RING
PAD_TILES = LAYER_TILES - 2 * FF_TILES - MIX_TILES
GROUPS = LAYER_TILES // RING
MIX0, FFN2 = FF_TILES, FF_TILES + MIX_TILES + PAD_TILES
NORMS = 3
OUTS = DC // 2

HEADS = 8
GLA_HEADS, GLA_DV = 4, 256
RANK = 16
ROT = 32
ADA = 6 * DC
ADA_TILES = ADA * DC // TILE_BLOCKS
SEC_BLOCKS = 16 * DC + 8 * DC + (4 + 4 + 8 + 1) * DC + 8 * DC + DC * 4 * DC + DC * DC
SEC_TILES = ADA_TILES + -(-SEC_BLOCKS // TILE_BLOCKS)
DENSE_TILES = LAYERS * LAYER_TILES + SEC_TILES
LEVELS = (64, 32, 16, 8, 4, 2, 1)
EXPERTS, TOPK = 32, 4
HALF = DC // 2
MOE_RING = DC
UNIT, UNITS_E, W_UNITS = DC * P, 2 * DC, 4
CAP = 64
PASSES = TOK // CAP
LAYER_STEPS, MOE_STEPS = 44, 2 * DC
ALPHA, LIMIT = 1.702, 7.0

LP_FFN1, LP_MIX, LP_FFN2, LP_BGATE, LP_SUBLN, LP_LAMI, LP_LAM = 0, 8, 16, 24, 48, 49, 51
LP = LP_LAM + 4 * DH
(C_X, C_GFIN, C_BADA, C_N1, C_GLAB, C_GLAN, C_BMERGE, C_N2, C_NF, C_BEXP) = (
    0, 8, 16, 64, 72, 76, 78, 94, 102, 110)
COLS = C_BEXP + EXPERTS * 16
K_ID, K_ONES, K_CAUSAL, K_LEVEL, K_IOTA = 0, 128, 384, 768, 768 + 8 * 128
K_BEFORE, K_FOLD, K_EPS = K_IOTA + CAP, K_IOTA + CAP + P, K_IOTA + 2 * CAP + P
K_DSEQ = K_EPS + 4
K_DCH = K_DSEQ + 2 * VEC
K_COS, K_SIN, K_ROT = K_DCH + 2 * P, K_DCH + 2 * P + TOK, K_DCH + 2 * P + 2 * TOK
KONST = K_ROT + ROT


def build(nc, stream, experts, x_in, konst_in, layer_in, cols_in, relb_in, onehot_in, glaw_in,
          router_in, brouter_in, bout_in, bias_rows, out):
    with ExitStack() as ctx:
        def sb(name, shape, dt=F32):
            return ctx.enter_context(nc.sbuf_tensor(name, shape, dt))

        def sem(name):
            return ctx.enter_context(nc.semaphore(name))

        ring = sb("ring", [P, RING, TILE])
        x = sb("x", [P, DC, TOK])
        konst = sb("konst", [P, KONST])
        lp_all = sb("lp_all", [P, LAYERS, LP])
        lp = sb("lp", [P, LP])
        cols = sb("cols", [P, COLS])
        glaw = sb("glaw", [RANK, 512])
        router = sb("router", [P, DC, EXPERTS])
        brouter = sb("brouter", [P, EXPERTS])
        bout = sb("bout", [EXPERTS, D])
        small = sb("small", [P, 64])
        mod = sb("mod", [P, ADA])
        modgain = sb("modgain", [P, 2 * DC])
        work = sb("work", [P, WORK])
        with ExitStack() as dense:
            def sb_dense(name, shape):
                return dense.enter_context(nc.sbuf_tensor(name, shape, F32))

            h = sb_dense("h", [P, DC, TOK])
            sq = sb_dense("sq", [P, DC, TOK])
            std = sb_dense("std", [P, 4 * TOK])
            rstd = sb_dense("rstd", [P, 4 * TOK])
            work2 = sb_dense("work2", [P, WORK2])
        w_hi = [sb(f"w_hi{i}", [P, UNIT], F32R)[:, :] for i in range(W_UNITS)]
        w_lo = [sb(f"w_lo{i}", [P, UNIT], F32R)[:, :] for i in range(W_UNITS)]
        xg = sb("xg", [P, DC, 2, CAP], F32R)[:, :, :, :]
        moe_work = sb("moe_work", [P, 12 * CAP + TOK + 4 * P])
        ps = ctx.enter_context(nc.psum_tensor("ps", [P, 8, 512], F32))

        def carve(at, *shape):
            n = math.prod(shape)
            v = work[:, at:at + n] if at < WORK else work2[:, at - WORK:at - WORK + n]
            if len(shape) == 2:
                v = v.rearrange("p (a b) -> p a b", b=shape[1])
            if len(shape) == 3:
                v = v.rearrange("p (a b c) -> p a b c", b=shape[1], c=shape[2])
            return v

        bias = carve(0, BIAS_HEADS, TT, TOK)
        vecs = carve(5120, BIAS_HEADS, VEC)
        relb = carve(10240, BIAS_HEADS, P)
        onehot = carve(11520, 4, VEC)
        x_tok = carve(13568, TT, D)
        silu = carve(17920, 5, TOK)
        act = carve(19200, 5, TOK)
        qk = carve(5120, QK_CHUNKS, TOK)
        vc = carve(8704, TT, 512)
        vb = carve(9728, TT, 384)
        a_tok = carve(10496, TT, D)
        four = carve(12544, FOURIER_GROUPS, TOK)
        S = carve(14592, 2, 768)
        PT = carve(16128, 2, 768)
        ob = carve(17664, TOK)
        oc = carve(17920, DIFF_HEADS, TOK)
        dft1 = carve(5120, 2, VEC)
        merged = carve(10496, DC, TOK)
        sg = carve(14592, 2, 3, TOK)
        mqk = carve(0, 16, TOK)
        mv = carve(4096, TT, D)
        oa = carve(6144, HEADS, TOK)
        mS = carve(8192, 2, 384)
        mPT = carve(8960, 2, 384)
        gqk = carve(0, 2 * GLA_HEADS, TOK)
        lg = carve(2048, GLA_HEADS, TOK)
        bcum = carve(3072, GLA_HEADS * TOK)
        glow = carve(9728, TOK)
        off = carve(9984, GLA_HEADS, P)
        tmp = carve(10496, GLA_HEADS, P)
        gv = carve(11008, TT, D)
        gr = carve(13056, DC, TOK)
        expd = carve(15104, GLA_HEADS * TOK)
        qd = carve(16128, GLA_HEADS, TOK)
        kd = carve(17152, GLA_HEADS, TOK)
        acc = carve(18176, TT, GLA_HEADS, P)
        gtmp = carve(19200, GLA_HEADS * TOK)
        go = carve(4096, DC, TOK)
        merged2 = carve(0, DC, TOK)
        sg2 = carve(16128, 2, 2, TOK)
        moe_hi = carve(0, 3, TILE)
        wt = carve(9216, TT, EXPERTS)
        wtT = carve(9280, TOK)
        sel = carve(9536, TT, EXPERTS)
        rank = carve(9600, TT, EXPERTS)
        lgt = carve(9664, TT, EXPERTS)
        eqs = carve(9728, TOPK, EXPERTS)
        sels = carve(9856, TOPK, EXPERTS)
        fullest = carve(9984, 1)
        flagf = carve(9988, PASSES + 1)
        flags = carve(10000, PASSES + 1).bitcast(I32)
        outd = carve(10016, D)
        h_tok = carve(11040, TT, D)
        y_tok = carve(13088, TT, D)

        def carve_moe(at, *shape):
            v = moe_work[:, at:at + math.prod(shape)]
            return v.rearrange("p (a b) -> p a b", b=shape[-1]) if len(shape) == 2 else v

        glu = carve_moe(0, 2, CAP)
        sig = carve_moe(2 * CAP, 2, CAP)
        lin = carve_moe(4 * CAP, 2, CAP)
        eact = carve_moe(6 * CAP, 4, CAP)
        place = carve_moe(10 * CAP, TT, CAP)
        placeT = carve_moe(12 * CAP, TOK)
        hid_tok = carve_moe(12 * CAP + TOK, 2, 2 * P)
        top8 = small[:, 32:40]
        topi = small[:, 40:48].bitcast(U32)
        topf = small[:, 48:52]
        topw = small[:, 52:56]

        ident = konst[:, K_ID:K_ID + P]
        ones = konst[:, K_ONES:K_ONES + P]
        ones_tok = konst[:, K_ONES:K_ONES + TOK]
        causal = konst[:, K_CAUSAL:K_CAUSAL + 384]
        iota = konst[:, K_IOTA:K_IOTA + CAP]
        before = konst[:, K_BEFORE:K_BEFORE + P]
        fold = konst[0:2 * CAP, K_FOLD:K_FOLD + CAP]
        eps_col = {EPS1: konst[:, K_EPS:K_EPS + 1], EPS2: konst[:, K_EPS + 1:K_EPS + 2]}
        one_col = konst[:, K_EPS + 2:K_EPS + 3]
        dseq = konst[:, K_DSEQ:K_DSEQ + 2 * VEC].rearrange("p (a b) -> p a b", b=VEC)
        dch = konst[:, K_DCH:K_DCH + 2 * P].rearrange("p (a b) -> p a b", b=P)
        cosT = konst[0:ROT, K_COS:K_COS + TOK]
        sinT = konst[0:ROT, K_SIN:K_SIN + TOK]
        rotT = konst[0:ROT, K_ROT:K_ROT + ROT]

        def level_mask(i):
            return konst[:, K_LEVEL + i * P:K_LEVEL + (i + 1) * P]

        ff_banks = (0, 1, 3, 0, 1)
        SSUM, DOWN = 2, 4

        tile_landed = [sem(f"tile_landed{i}") for i in range(RING)]
        tile_used = sem("tile_used")
        moe_landed = [sem(f"moe_landed{i}") for i in range(MOE_RING)]
        moe_used = sem("moe_used")
        konst_landed, x_landed, par_landed = sem("konst_landed"), sem("x_landed"), sem("par_landed")
        rel_landed = sem("rel_landed")
        xt_ready, xt_taken = sem("xt_ready"), sem("xt_taken")
        vec_ready, vec_taken = sem("vec_ready"), sem("vec_taken")
        rows_written, bias_landed = sem("rows_written"), sem("bias_landed")
        x_ready = sem("x_ready")
        sq_ready, ssum_ready, std_ready, h_ready = (
            sem("sq_ready"), sem("ssum_ready"), sem("std_ready"), sem("h_ready"))
        gu_ready, silu_ready, act_ready = sem("gu_ready"), sem("silu_ready"), sem("act_ready")
        proj_ready, proj_taken = sem("proj_ready"), sem("proj_taken")
        logits_ready, scores_made, max_ready = sem("logits_ready"), sem("scores_made"), sem("max_ready")
        exp_ready, probs_ready = sem("exp_ready"), sem("probs_ready")
        pt_ready, pt_taken = sem("pt_ready"), sem("pt_taken")
        o_ready, o_taken = sem("o_ready"), sem("o_taken")
        osq_ready, ossum_ready, ostd_ready, yc_ready = (
            sem("osq_ready"), sem("ossum_ready"), sem("ostd_ready"), sem("yc_ready"))
        lamdot_ready, lamexp_ready = sem("lamdot_ready"), sem("lamexp_ready")
        dft1_ready, dft1_taken = sem("dft1_ready"), sem("dft1_taken")
        dft2_ready, dft2_taken = sem("dft2_ready"), sem("dft2_taken")
        gates_ready, sig_ready, ys_ready, merged_ready = (
            sem("gates_ready"), sem("sig_ready"), sem("ys_ready"), sem("merged_ready"))
        out_ready = sem("out_ready")
        cact_ready, ada_ready, mod_ready = sem("cact_ready"), sem("ada_ready"), sem("mod_ready")
        rot_ready, rot_taken, roped = sem("rot_ready"), sem("rot_taken"), sem("roped")
        z_ready, zb_ready, sp_ready = sem("z_ready"), sem("zb_ready"), sem("sp_ready")
        diff_ready, decay_ready, k_decayed = sem("diff_ready"), sem("decay_ready"), sem("k_decayed")
        qk_decayed = sem("qk_decayed")
        lev_ready, lev_taken, added, scores_done = (
            sem("lev_ready"), sem("lev_taken"), sem("added"), sem("scores_done"))
        go_ready, go_taken, gla_ready = sem("go_ready"), sem("go_taken"), sem("gla_ready")
        route_ready, top_ready, topexp_ready, wt_ready = (
            sem("route_ready"), sem("top_ready"), sem("topexp_ready"), sem("wt_ready"))
        wtT_ready, wtT_taken = sem("wtT_ready"), sem("wtT_taken")
        htok_ready, htok_taken = sem("htok_ready"), sem("htok_taken")
        ranks_ready, flags_ready, bias_sums_ready = sem("ranks_ready"), sem("flags_ready"), sem("bias_sums_ready")
        place_ready, xg_ready, xg_taken = sem("place_ready"), sem("xg_ready"), sem("xg_taken")
        placeT_ready, placeT_taken = sem("placeT_ready"), sem("placeT_taken")
        whi_ready, wlo_ready, xhi_ready = sem("whi_ready"), sem("wlo_ready"), sem("xhi_ready")
        w_used, htok_copied = sem("w_used"), sem("htok_copied")
        hid_ready, glu_ready, esig_ready, eact_ready = (
            sem("hid_ready"), sem("glu_ready"), sem("esig_ready"), sem("eact_ready"))
        eout_ready, eout_taken = sem("eout_ready"), sem("eout_taken")
        scat_ready, scat_added, y_ready = sem("scat_ready"), sem("scat_added"), sem("y_ready")
        yT_ready = sem("yT_ready")
        ytok_ready, ytok_taken, stored = (
            sem("ytok_ready"), sem("ytok_taken"), sem("stored"))
        act_step, dve_step, moe_step = sem("act_step"), sem("dve_step"), sem("moe_step")

        class Steps:

            def __init__(self, eng, sem):
                self.eng, self.sem, self.base, self.k = eng, sem, 0, 0

            def __call__(self, ins):
                ins.then_inc(self.sem, 1)
                self.k += 1
                self.eng.wait_ge(self.sem, self.base + self.k)

        class Blocks:

            def __init__(self, pe, l, tile):
                self.pe, self.l, self.first, self.n = pe, l, tile * TILE_BLOCKS, tile * TILE_BLOCKS
                self.taken = 0

            def take(self, k=1):
                t, b = divmod(self.n, TILE_BLOCKS)
                if b == 0:
                    self.pe.wait_ge(tile_landed[t % RING], (self.l * GROUPS + t // RING + 1) * 16)
                assert b + k <= TILE_BLOCKS
                self.n += k
                self.taken = k
                return ring[:, t % RING, b * P:(b + k) * P]

            def used(self, mm):
                start = self.n - self.taken
                if start % TILE_BLOCKS == 0 and start > self.first:
                    mm.then_inc(tile_used, 1)
                return mm

        def slot(j):
            return ring[:, j, :] if j < RING else moe_hi[:, j - RING, :]

        block = ctx.enter_context(nc.Block())

        @block.sync
        def _(sp):
            sp.dma_start(x_tok[:, :, :], x_in.rearrange("(t p) d -> p t d", p=P)).then_inc(x_landed, 16)
            for s in range(RING):
                sp.dma_start(ring[:, s, :], stream[s]).then_inc(tile_landed[s], 16)
            whole = DENSE_TILES // RING
            with sp.Fori(1, whole) as g:
                for s in range(RING):
                    sp.wait_ge(tile_used, g * RING + (s + 1 - RING))
                    sp.dma_start(ring[:, s, :], stream[g * RING + s]).then_inc(tile_landed[s], 16)
            for s in range(DENSE_TILES - whole * RING):
                sp.wait_ge(tile_used, (whole - 1) * RING + s + 1)
                sp.dma_start(ring[:, s, :], stream[whole * RING + s]).then_inc(tile_landed[s], 16)

            sp.wait_ge(tile_used, DENSE_TILES)
            for j in range(MOE_RING):
                if j == RING:
                    sp.wait_ge(x_ready, 1 + LAYERS * NORMS + 2)
                sp.dma_start(slot(j), experts[j]).then_inc(moe_landed[j], 16)
            sp.wait_ge(flags_ready, 1)
            with sp.Fori(0, PASSES) as p:
                needed = sp.value_load(flags[0:1, bass.ds(p, 1)], min_val=0, max_val=1)
                with sp.If(needed > 0):
                    with sp.Fori(1, EXPERTS) as e:
                        for j in range(MOE_RING):
                            sp.wait_ge(moe_used, p * (EXPERTS * DC) + e * DC + (j + 1 - DC))
                            sp.dma_start(slot(j), experts[e * DC + j]).then_inc(moe_landed[j], 16)
                again = sp.value_load(flags[0:1, bass.ds(p + 1, 1)], min_val=0, max_val=1)
                with sp.If(again > 0):
                    for j in range(MOE_RING):
                        sp.wait_ge(moe_used, p * (EXPERTS * DC) + (EXPERTS * DC - DC + j + 1))
                        sp.dma_start(slot(j), experts[j]).then_inc(moe_landed[j], 16)
            sp.wait_ge(ytok_taken, 2 * OUTS)
            sp.dma_start(out.rearrange("(t p) d -> p t d", p=P), y_tok[:, :, :]).then_inc(stored, 16)
            sp.wait_ge(stored, 16)

        @block.gpsimd
        def _(pool):
            pool.dma_start(konst[:, :], konst_in).then_inc(konst_landed, 16)
            pool.dma_start(lp_all[:, :, :], layer_in).then_inc(par_landed, 16)
            pool.dma_start(cols[:, :], cols_in).then_inc(par_landed, 16)
            pool.dma_start(relb[0:BUCKETS + 1], relb_in).then_inc(rel_landed, 16)
            pool.dma_start(onehot[0:BUCKETS + 1], onehot_in).then_inc(rel_landed, 16)
            pool.dma_start(glaw[:, :], glaw_in).then_inc(par_landed, 16)
            pool.dma_start(router[:, :, :], router_in).then_inc(par_landed, 16)
            pool.dma_start(brouter[:, :], brouter_in).then_inc(par_landed, 16)
            pool.dma_start(bout[:, :], bout_in).then_inc(par_landed, 16)
            pool.wait_ge(vec_taken, BIAS_HEADS)
            pool.dma_start(bias_rows.rearrange("h p v -> p h v"), vecs[:, :, :]).then_inc(rows_written, 16)
            pool.wait_ge(rows_written, 16)
            for qt in range(TT):
                skew = bass.AP(bias_rows.tensor, (TOK - 1) - qt * P,
                               [[VEC - 1, P], [P * VEC, BIAS_HEADS], [1, TOK]])
                pool.dma_start(bias[:, :, qt, :], skew).then_inc(bias_landed, 16)

            for v in range(len(LEVELS) + 1):
                pool.wait_ge(decay_ready, v + 1)
                if v > 0:
                    pool.wait_ge(lev_ready, (v - 1) * TT + 1)
                pool.tensor_tensor(kd[:, :, :], gqk[:, GLA_HEADS:, :],
                                   expd.rearrange("p (h t) -> p h t", t=TOK), ALU.mult).then_inc(k_decayed, 1)

        @block.scalar
        def _(a):
            step = Steps(a, act_step)

            def norm(l, n, eps, scale=1.0 / D):
                a.wait_ge(x_ready, l * NORMS + n + 1)
                nc.scalar.activation(sq[:, :, :], x[:, :, :], ACT.Square).then_inc(sq_ready, 1)
                a.wait_ge(ssum_ready, l * NORMS + n + 1)
                nc.scalar.activation(std[:, 0:TOK], ps[:, SSUM, 0:TOK], ACT.Sqrt, bias=eps_col[eps],
                                     scale=scale).then_inc(std_ready, 1)

            def ffn_tile(l, f, i, g=0):
                s = (i - 1) % 5
                a.wait_ge(gu_ready, l * (2 * FF_TILES) + g * 5 + (f * FF_TILES + i + 1))
                nc.scalar.activation(silu[:, s, :], ps[:, ff_banks[s], 0:TOK], ACT.Silu).then_inc(silu_ready, 1)

            def ffn(l, f):
                ffn_tile(l, f, 0)
                with a.Fori(0, (FF_TILES - 2) // 5) as g:
                    for s in range(5):
                        ffn_tile(l, f, 1 + s, g)
                ffn_tile(l, f, FF_TILES - 1)

            a.wait_ge(par_landed, 6 * 16)
            for i in range(BIAS_HEADS):
                a.wait_ge(vec_ready, i + 1)
                nc.scalar.activation(vecs[:, i, :], ps[:, i % 4, :], ACT.Copy).then_inc(vec_taken, 1)
            nc.scalar.activation(small[:, 16:24], cols[:, C_X:C_X + DC], ACT.Silu).then_inc(cact_ready, 1)

            with a.Fori(0, LAYERS) as l:
                norm(l, 0, EPS1)
                ffn(l, 0)
                norm(l, 1, EPS1)
                a.wait_ge(lamdot_ready, l + 1)
                nc.scalar.activation(small[:, 2:4], small[:, 0:2], ACT.Exp).then_inc(lamexp_ready, 1)

                def take_proj(r):
                    a.wait_ge(proj_ready, l * PROJ + r + 1)
                    bank = ps[:, r % 4, :]
                    if r < 7:
                        dst = qk[:, 2 * r:2 * r + 2, :]
                        bank = bank.rearrange("p (a b) -> p a b", b=TOK)
                    elif r < 9:
                        dst = vc[:, r - 7, :]
                    elif r < 11:
                        dst, bank = vb[:, r - 9, :], ps[:, r % 4, 0:384]
                    else:
                        dst = a_tok[:, (r - 11) % 2, (r - 11) // 2 * 512:(r - 11) // 2 * 512 + 512]
                    nc.scalar.activation(dst, bank, ACT.Copy).then_inc(proj_taken, 1)

                a.wait_ge(rows_written, 16)
                for r in range(11):
                    take_proj(r)

                def exps(u):
                    a.wait_ge(max_ready, l * UNITS + u + 1)
                    if u < DIL_UNITS:
                        nc.scalar.activation(S[:, u % 2, :], S[:, u % 2, :], ACT.Exp, bias=small[:, 8 + u % 2 * 2:9 + u % 2 * 2],
                                             accum_out=small[:, 12 + u % 2 * 2:13 + u % 2 * 2]).then_inc(exp_ready, 1)
                    else:
                        for m in range(2):
                            c = u % 2 * 2 + m
                            e = nc.scalar.activation(S[:, u % 2, m * TOK:(m + 1) * TOK], S[:, u % 2, m * TOK:(m + 1) * TOK],
                                                     ACT.Exp, bias=small[:, 8 + c:9 + c], accum_out=small[:, 12 + c:13 + c])
                        e.then_inc(exp_ready, 1)

                def take_pt(u):
                    a.wait_ge(pt_ready, l * UNITS + u + 1)
                    n = 768 if u < DIL_UNITS else 256
                    nc.scalar.activation(PT[:, u % 2, 0:n], ps[:, 4:6, :].rearrange("p a b -> p (a b)")[:, 0:n],
                                         ACT.Copy).then_inc(pt_taken, 1)

                def take_o(i):
                    a.wait_ge(o_ready, l * 5 + i + 1)
                    if i == 0:
                        nc.scalar.activation(ob[:, :], ps[:, 6, 0:TOK], ACT.Copy).then_inc(o_taken, 1)
                    else:
                        hh = i - 1
                        nc.scalar.activation(oc[:, hh, :], ps[:, 7 - hh % 2, 0:TOK], ACT.Copy).then_inc(o_taken, 1)

                for u in range(UNITS + 2):
                    if u < UNITS:
                        exps(u)
                    if u >= 1 and u - 1 < UNITS:
                        take_pt(u - 1)
                    if u >= 2:
                        w = u - 2
                        if w == DIL_UNITS - 1:
                            take_o(0)
                        if w >= DIL_UNITS and w % 2 == 1:
                            take_o(1 + (w - DIL_UNITS) // 2)
                a.wait_ge(o_taken, l * 5 + 5)
                nc.scalar.activation(sq[:, 0:4, :], oc[:, :, :], ACT.Square).then_inc(osq_ready, 1)
                for r in range(11, PROJ):
                    take_proj(r)
                a.wait_ge(ossum_ready, l + 1)
                nc.scalar.activation(std[:, :], ps[:, 6:8, :].rearrange("p a b -> p (a b)"), ACT.Sqrt, bias=eps_col[SUBLN_EPS],
                                     scale=1.0 / P).then_inc(ostd_ready, 1)
                for g in range(FOURIER_GROUPS):
                    a.wait_ge(dft1_ready, l * FOURIER_GROUPS + g + 1)
                    nc.scalar.activation(dft1[:, g % 2, :], ps[:, g % 2, :], ACT.Copy).then_inc(dft1_taken, 1)
                for m in range(DC):
                    a.wait_ge(gates_ready, l * DC + m + 1)
                    if m >= 2:
                        a.wait_ge(merged_ready, l * DC + m - 1)
                    b0 = 4 * (1 - m % 2)
                    for j in range(3):
                        c = LP_BGATE + j * DC + m
                        e = nc.scalar.activation(sg[:, m % 2, j, :], ps[:, b0 + j // 2, j % 2 * TOK:(j % 2 + 1) * TOK], ACT.Sigmoid, bias=lp[:, c:c + 1])
                    e.then_inc(sig_ready, 1)
                norm(l, 2, EPS1)
                ffn(l, 1)

            norm(LAYERS, 0, EPS1)
            norm(LAYERS, 1, EPS2)

            def take_proj2(r):
                a.wait_ge(proj_ready, LAYERS * PROJ + r + 1)
                bank = ps[:, r % 4, :]
                pair = bank.rearrange("p (a b) -> p a b", b=TOK)
                if r < 4:
                    op = nc.scalar.activation(mv[:, r % 2, r // 2 * 512:r // 2 * 512 + 512], bank, ACT.Copy)
                elif r < 12:
                    op = nc.scalar.activation(mqk[:, 2 * (r - 4):2 * (r - 4) + 2, :], pair, ACT.Copy)
                elif r < 14:
                    op = nc.scalar.activation(gqk[:, 2 * (r - 12):2 * (r - 12) + 2, :], pair, ACT.Copy, scale=float(P) ** -0.5)
                elif r < 16:
                    op = nc.scalar.activation(gqk[:, 2 * (r - 12):2 * (r - 12) + 2, :], pair, ACT.Copy)
                elif r == 16:
                    op = nc.scalar.activation(glow[0:RANK, :], ps[0:RANK, r % 4, 0:TOK], ACT.Copy)
                elif r < 21:
                    op = nc.scalar.activation(gr[:, 2 * (r - 17):2 * (r - 17) + 2, :], pair, ACT.Silu)
                else:
                    op = nc.scalar.activation(gv[:, (r - 21) % 2, (r - 21) // 2 * 512:(r - 21) // 2 * 512 + 512], bank, ACT.Copy)
                op.then_inc(proj_taken, 1)

            for r in range(12):
                take_proj2(r)

            U0 = LAYERS * UNITS

            def exps2(u):
                a.wait_ge(max_ready, U0 + u + 1)
                for m, (lo, hi) in enumerate(((0, 128), (128, 384))):
                    c = u % 2 * 2 + m
                    e = nc.scalar.activation(mS[:, u % 2, lo:hi], mS[:, u % 2, lo:hi], ACT.Exp, bias=small[:, 8 + c:9 + c],
                                             accum_out=small[:, 12 + c:13 + c])
                e.then_inc(exp_ready, 1)

            for u in range(HEADS + 2):
                if u < HEADS:
                    exps2(u)
                if 1 <= u <= HEADS:
                    a.wait_ge(pt_ready, U0 + u)
                    nc.scalar.activation(mPT[:, (u - 1) % 2, :], ps[:, 4, 0:384], ACT.Copy).then_inc(pt_taken, 1)
                if u >= 2:
                    a.wait_ge(o_ready, LAYERS * 5 + u - 1)
                    nc.scalar.activation(oa[:, u - 2, :], ps[:, 6 + u % 2, 0:TOK], ACT.Copy).then_inc(o_taken, 1)
            for r in range(12, 25):
                take_proj2(r)
            a.wait_ge(zb_ready, 1)
            step(nc.scalar.activation(gtmp[:, :], lg.rearrange("p h t -> p (h t)"), ACT.Abs))
            step(nc.scalar.activation(gtmp[:, :], gtmp[:, :], ACT.Exp, scale=-1.0))
            nc.scalar.activation(gtmp[:, :], gtmp[:, :], ACT.Ln, bias=one_col).then_inc(sp_ready, 1)
            for v in range(len(LEVELS) + 1):
                a.wait_ge(diff_ready, v + 1)
                if v > 0:
                    a.wait_ge(k_decayed, v)
                    a.wait_ge(qk_decayed, v)
                nc.scalar.activation(expd[:, :], gtmp[:, :], ACT.Exp, scale=1.0 / 16).then_inc(decay_ready, 1)
            for i in range(OUTS):
                a.wait_ge(go_ready, i + 1)
                nc.scalar.activation(go[:, 2 * i:2 * i + 2, :], ps[:, 4 + i, :].rearrange("p (a b) -> p a b", b=TOK),
                                     ACT.Copy).then_inc(go_taken, 1)
            a.wait_ge(go_taken, OUTS)
            nc.scalar.activation(sq[:, :, :], go[:, :, :], ACT.Square).then_inc(osq_ready, 1)
            a.wait_ge(ossum_ready, LAYERS + 1)
            nc.scalar.activation(std[:, :], ps[:, 0:2, :].rearrange("p a b -> p (a b)"), ACT.Sqrt, bias=eps_col[EPS2],
                                 scale=1.0 / GLA_DV).then_inc(ostd_ready, 1)
            for m in range(DC):
                a.wait_ge(gates_ready, LAYERS * DC + m + 1)
                if m >= 2:
                    a.wait_ge(merged_ready, LAYERS * DC + m - 1)
                for j in range(2):
                    c = C_BMERGE + j * DC + m
                    e = nc.scalar.activation(sg2[:, m % 2, j, :], ps[:, 2 + 2 * (m % 2), j * TOK:(j + 1) * TOK], ACT.Sigmoid,
                                             bias=cols[:, c:c + 1])
                e.then_inc(sig_ready, 1)
            norm(LAYERS, 2, EPS2)
            for t in range(TT):
                a.wait_ge(top_ready, t + 1)
                nc.scalar.activation(topw, top8[:, 0:TOPK], ACT.Exp, bias=small[:, 56:57],
                                     accum_out=small[:, 57:58]).then_inc(topexp_ready, 1)
            for i in range(2 * TT):
                a.wait_ge(htok_ready, i + 1)
                nc.scalar.activation(h_tok[:, i // 2, i % 2 * 512:i % 2 * 512 + 512], ps[:, 4 + i, :], ACT.Copy).then_inc(htok_taken, 1)

            def take_tokens(n):
                a.wait_ge(xg_ready, n)
                nc.scalar.activation(xg[:, :, 0, :], ps[:, 2, 0:DC * CAP].rearrange("p (a b) -> p a b", b=CAP), ACT.Copy).then_inc(xhi_ready, 1)

            def round_weights(n, j, first=False):
                a.wait_ge(moe_landed[j], n * 16 + 16)
                for half in range(2):
                    u = 2 * j + half
                    if not first:
                        a.wait_ge(w_used, n * UNITS_E + (u + 1 - W_UNITS))
                    nc.scalar.activation(w_hi[u % W_UNITS], slot(j)[:, half * UNIT:(half + 1) * UNIT], ACT.Copy).then_inc(whi_ready, 1)

            def take_hidden(n, j):
                a.wait_ge(w_used, n * UNITS_E + 2 * (j + 1))
                nc.scalar.activation(hid_tok[0:2 * CAP, j % 2, :], ps[0:2 * CAP, j % 2, 0:2 * P], ACT.Copy).then_inc(htok_copied, 1)

            def take_out(n):
                for half in range(2):
                    if half == 0:
                        a.wait_ge(eout_ready, n + 1)
                    else:
                        a.wait_ge(moe_used, n * DC + DC)
                    nc.scalar.activation(outd[0:CAP, half * 512:half * 512 + 512], ps[0:CAP, 4 + half, :], ACT.Copy).then_inc(eout_taken, 1)

            def expert_step(n, j, after=False, last=False):
                if j + 2 < DC:
                    round_weights(n, j + 2)
                elif not last:
                    round_weights(n + 1, j + 2 - DC)
                if j == DC - 2 and not last:
                    take_tokens(n + 2)
                if j + 1 < DC:
                    take_hidden(n, j + 1)
                elif not last:
                    take_hidden(n + 1, 0)
                if j == 0 and after:
                    take_out(n - 1)
                a.wait_ge(glu_ready, n * DC + (j + 1))
                nc.scalar.activation(sig[:, j % 2, :], glu[:, j % 2, :], ACT.Sigmoid, scale=ALPHA).then_inc(esig_ready, 1)
                if j == HALF:
                    a.wait_ge(placeT_ready, n + 1)
                    nc.scalar.activation(placeT[0:CAP, :], ps[0:CAP, 2, 0:TOK], ACT.Copy).then_inc(placeT_taken, 1)

            a.wait_ge(flags_ready, 1)
            with a.Fori(0, PASSES) as p:
                needed = a.value_load(flags[0:1, bass.ds(p, 1)], min_val=0, max_val=1)
                with a.If(needed > 0):
                    n = p * EXPERTS
                    round_weights(n, 0, True)
                    take_tokens(n + 1)
                    round_weights(n, 1, True)
                    take_hidden(n, 0)
                    for j in range(HALF):
                        expert_step(n, j)
                    with a.Fori(0, EXPERTS - 1) as e:
                        for j in range(HALF, DC):
                            expert_step(p * EXPERTS + e, j)
                        for j in range(HALF):
                            expert_step(p * EXPERTS + e + 1, j, after=True)
                    for j in range(HALF, DC):
                        expert_step(n + (EXPERTS - 1), j, last=True)
                    take_out(n + (EXPERTS - 1))
            norm(LAYERS, 3, EPS2)
            for i in range(2 * OUTS):
                t, half = divmod(i, OUTS)
                a.wait_ge(ytok_ready, i + 1)
                nc.scalar.activation(y_tok[:, t, half * 256:half * 256 + 256], ps[:, i % 4, 0:256],
                                     ACT.Copy).then_inc(ytok_taken, 1)

        @block.vector
        def _(v):
            step = Steps(v, dve_step)

            def add_level(i):
                for t in range(TT):
                    n = 1 + (i - 1) * TT + t
                    v.wait_ge(lev_ready, n + 1)
                    sc = ps[:, 2 * (i % 2) + t, :].rearrange("p (h t) -> p h t", t=P)
                    mask = level_mask(i - 1).unsqueeze(1).to_broadcast([P, GLA_HEADS, P])
                    dst = acc[:, t, :, :] if i == 1 else tmp[:, :, :]
                    nc.vector.tensor_tensor(dst, sc, mask, ALU.mult).then_inc(lev_taken, 1)
                    v.wait_ge(lev_taken, n + 1)
                    if i > 1:
                        op = nc.vector.tensor_tensor(acc[:, t, :, :], acc[:, t, :, :], tmp[:, :, :], ALU.add)
                        if i == len(LEVELS) + 1 and t == TT - 1:
                            op.then_inc(scores_done, 1)
                        else:
                            step(op)

            def recip_std(l, n):
                v.wait_ge(std_ready, l * NORMS + n + 1)
                step(nc.vector.reciprocal(rstd[:, 0:TOK], std[:, 0:TOK]))

            def norm(l, n, gain, out=None):
                recip_std(l, n)
                for c in range(DC):
                    op = nc.vector.scalar_tensor_tensor(out=(h if out is None else out)[:, c, :], in0=x[:, c, :], scalar=gain[:, c:c + 1],
                                                        in1=rstd[:, 0:TOK], op0=ALU.mult, op1=ALU.mult)
                return op

            def ffn_tile(l, f, i, g=0):
                s = (i - 1) % 5
                v.wait_ge(silu_ready, l * (2 * FF_TILES) + g * 5 + (f * FF_TILES + i + 1))
                nc.vector.tensor_tensor(act[:, s, :], silu[:, s, :], ps[:, ff_banks[s], TOK:2 * TOK],
                                        ALU.mult).then_inc(act_ready, 1)

            def ffn(l, f):
                ffn_tile(l, f, 0)
                with v.Fori(0, (FF_TILES - 2) // 5) as g:
                    for s in range(5):
                        ffn_tile(l, f, 1 + s, g)
                ffn_tile(l, f, FF_TILES - 1)
                v.wait_ge(tile_used, l * LAYER_TILES + (FFN2 if f else 0) + FF_TILES)
                for b in range(OUTS):
                    xs = x[:, 2 * b:2 * b + 2, :]
                    op = nc.vector.scalar_tensor_tensor(out=xs, in0=ps[:, DOWN + b, :].rearrange("p (a b) -> p a b", b=TOK), scalar=0.5,
                                                        in1=xs, op0=ALU.mult, op1=ALU.add)
                op.then_inc(x_ready, 1)

            for i in range(OUTS):
                v.wait_ge(xt_ready, i + 1)
                op = nc.vector.tensor_copy(x[:, 2 * i:2 * i + 2, :], ps[:, 4 + i, :].rearrange("p (a b) -> p a b", b=TOK))
            op.then_inc(x_ready, 1)
            v.wait_ge(par_landed, 6 * 16)
            v.wait_ge(konst_landed, 16)

            first_k = step.k
            with v.Fori(0, LAYERS) as l:
                step.base = l * LAYER_STEPS
                step(nc.vector.tensor_copy(lp[:, :], lp_all[:, l, :]))
                for i in range(2):
                    q = lp[:, LP_LAM + i * 2 * DH:LP_LAM + i * 2 * DH + DH]
                    k = lp[:, LP_LAM + i * 2 * DH + DH:LP_LAM + (i + 1) * 2 * DH]
                    op = nc.vector.tensor_tensor_reduce(rstd[:, 512 + i * DH:512 + (i + 1) * DH], q, k, 1.0, 0.0, ALU.mult, ALU.add, small[:, i:i + 1])
                op.then_inc(lamdot_ready, 1)
                step(nc.vector.tensor_scalar(small[:, 6:7], lp[:, LP_SUBLN:LP_SUBLN + 1], lp[:, LP_LAMI + 1:LP_LAMI + 2], None, ALU.mult))
                norm(l, 0, lp[:, LP_FFN1:LP_FFN1 + DC]).then_inc(h_ready, 1)
                ffn(l, 0)
                norm(l, 1, lp[:, LP_MIX:LP_MIX + DC]).then_inc(h_ready, 1)
                v.wait_ge(lamexp_ready, l + 1)
                step(nc.vector.tensor_scalar(small[:, 5:6], small[:, 2:3], lp[:, LP_LAMI:LP_LAMI + 1], None, ALU.add))
                step(nc.vector.tensor_tensor(small[:, 4:5], small[:, 3:4], small[:, 5:6], ALU.subtract))
                v.wait_ge(bias_landed, TT * 16)

                def scores(u):
                    v.wait_ge(logits_ready, l * UNITS + u + 1)
                    if u >= 2:
                        v.wait_ge(pt_ready, l * UNITS + u - 1)
                    b = 2 * (u % 2)
                    if u < DIL_UNITS:
                        slot, qt = divmod(u, TT)
                        lo = ps[:, b:b + 2, :].rearrange("p a b -> p (a b)")[:, 0:768].rearrange("p (a b) -> p a b", b=TOK)
                        bi = bias[:, slot:slot + 5:2, qt, :]
                        dst = S[:, u % 2, :].rearrange("p (a b) -> p a b", b=TOK)
                    else:
                        hh, qt = divmod(u - DIL_UNITS, TT)
                        lo = ps[:, b:b + 2, 0:TOK]
                        bi = bias[:, 6 + hh, qt, :].unsqueeze(1).to_broadcast([P, 2, TOK])
                        dst = S[:, u % 2, 0:512].rearrange("p (a b) -> p a b", b=TOK)
                    nc.vector.scalar_tensor_tensor(out=dst, in0=lo, scalar=DH ** -0.5, in1=bi, op0=ALU.mult,
                                                   op1=ALU.add).then_inc(scores_made, 1)
                    v.wait_ge(scores_made, l * UNITS + u + 1)
                    c = 8 + u % 2 * 2
                    if u < DIL_UNITS:
                        op = nc.vector.tensor_reduce(small[:, c:c + 1], S[:, u % 2, :], AX.X, ALU.max, negate=True)
                    else:
                        op = nc.vector.tensor_reduce(small[:, c:c + 2], dst, AX.X, ALU.max, negate=True)
                    op.then_inc(max_ready, 1)

                def probs(u):
                    v.wait_ge(exp_ready, l * UNITS + u + 1)
                    c = u % 2 * 2
                    if u < DIL_UNITS:
                        step(nc.vector.reciprocal(small[:, 24 + c:25 + c], small[:, 12 + c:13 + c]))
                        op = nc.vector.tensor_scalar(S[:, u % 2, :], S[:, u % 2, :], small[:, 24 + c:25 + c], None, ALU.mult)
                    else:
                        step(nc.vector.reciprocal(small[:, 24 + c:26 + c], small[:, 12 + c:14 + c]))
                        step(nc.vector.tensor_scalar(S[:, u % 2, TOK:512], S[:, u % 2, TOK:512], small[:, 25 + c:26 + c], small[:, 4:5], ALU.mult, ALU.mult))
                        op = nc.vector.scalar_tensor_tensor(out=S[:, u % 2, 0:TOK], in0=S[:, u % 2, 0:TOK], scalar=small[:, 24 + c:25 + c],
                                                            in1=S[:, u % 2, TOK:512], op0=ALU.mult, op1=ALU.add)
                    op.then_inc(probs_ready, 1)

                for u in range(UNITS + 1):
                    if u < UNITS:
                        scores(u)
                    if u >= 1:
                        probs(u - 1)
                v.wait_ge(ostd_ready, l + 1)
                step(nc.vector.reciprocal(rstd[:, :], std[:, :]))
                for hh in range(DIFF_HEADS):
                    op = nc.vector.scalar_tensor_tensor(out=oc[:, hh, :], in0=oc[:, hh, :], scalar=small[:, 6:7],
                                                        in1=rstd[:, hh * TOK:(hh + 1) * TOK], op0=ALU.mult, op1=ALU.mult)
                op.then_inc(yc_ready, 1)
                for g in range(FOURIER_GROUPS):
                    v.wait_ge(dft2_ready, l * FOURIER_GROUPS + g + 1)
                    nc.vector.tensor_copy(four[:, g, :], ps[:, 2 + g % 2, 0:TOK]).then_inc(dft2_taken, 1)
                for m in range(DC):
                    v.wait_ge(sig_ready, l * DC + m + 1)
                    v.wait_ge(ys_ready, l * DC + m + 1)
                    b0 = 4 * (1 - m % 2) + 2
                    branches = ps[:, b0:b0 + 2, :].rearrange("p a b -> p (a b)")[:, 0:3 * TOK].rearrange("p (a b) -> p a b", b=TOK)
                    step(nc.vector.tensor_tensor(sg[:, m % 2, :, :], sg[:, m % 2, :, :], branches, ALU.mult))
                    step(nc.vector.tensor_tensor(sg[:, m % 2, 0, :], sg[:, m % 2, 0, :], sg[:, m % 2, 1, :], ALU.add))
                    nc.vector.tensor_tensor(merged[:, m, :], sg[:, m % 2, 0, :], sg[:, m % 2, 2, :], ALU.add).then_inc(merged_ready, 1)
                for b in range(OUTS):
                    v.wait_ge(out_ready, l * OUTS + b + 1)
                    xs = x[:, 2 * b:2 * b + 2, :]
                    op = nc.vector.tensor_tensor(xs, xs, ps[:, DOWN + b, :].rearrange("p (a b) -> p a b", b=TOK), ALU.add)
                op.then_inc(x_ready, 1)
                norm(l, 2, lp[:, LP_FFN2:LP_FFN2 + DC]).then_inc(h_ready, 1)
                ffn(l, 1)
            assert step.k - first_k == LAYER_STEPS, step.k - first_k
            step.base = LAYERS * LAYER_STEPS
            step.k = first_k

            norm(LAYERS, 0, cols[:, C_GFIN:C_GFIN + DC], out=x).then_inc(x_ready, 1)
            v.wait_ge(ada_ready, 1)
            step(nc.vector.tensor_tensor(mod[:, :], ps[:, 3, 0:ADA], cols[:, C_BADA:C_BADA + ADA], ALU.add))
            for n, (sc, w) in enumerate(((DC, C_N1), (4 * DC, C_N2))):
                step(nc.vector.scalar_tensor_tensor(out=modgain[:, n * DC:(n + 1) * DC], in0=mod[:, sc:sc + DC], scalar=1.0,
                                                    in1=cols[:, w:w + DC], op0=ALU.add, op1=ALU.mult))

            def mod_norm(n, i):
                step(norm(LAYERS, n, modgain[:, i * DC:(i + 1) * DC]))
                shift = mod[:, 3 * i * DC:(3 * i + 1) * DC]
                op = nc.vector.tensor_tensor(h[:, :, :], h[:, :, :], shift.unsqueeze(2).to_broadcast([P, DC, TOK]), ALU.add)
                op.then_inc(h_ready, 1)

            mod_norm(1, 0)
            for i in range(HEADS):
                v.wait_ge(rot_ready, i + 1)
                qs = mqk[0:ROT, 2 * i:2 * i + 2, :]
                rp = ps[0:ROT, 4 + i % 2, :].rearrange("p (a b) -> p a b", b=TOK)
                rt = rstd[0:ROT, 512:1024].rearrange("p (a b) -> p a b", b=TOK)
                step(nc.vector.tensor_tensor(rt, rp, sinT.unsqueeze(1).to_broadcast([ROT, 2, TOK]), ALU.mult))
                step(nc.vector.tensor_tensor(qs, qs, cosT.unsqueeze(1).to_broadcast([ROT, 2, TOK]), ALU.mult))
                nc.vector.tensor_tensor(qs, qs, rt, ALU.add).then_inc(roped, 1)
                v.wait_ge(roped, i + 1)
            U0 = LAYERS * UNITS
            for u in range(HEADS + 1):
                if u < HEADS:
                    v.wait_ge(logits_ready, U0 + u + 1)
                    if u >= 2:
                        v.wait_ge(pt_ready, U0 + u - 1)
                    nc.vector.scalar_tensor_tensor(out=mS[:, u % 2, :], in0=ps[:, u % 2, 0:384], scalar=P ** -0.5, in1=causal,
                                                   op0=ALU.mult, op1=ALU.add).then_inc(scores_made, 1)
                    v.wait_ge(scores_made, U0 + u + 1)
                    c = 8 + u % 2 * 2
                    nc.vector.tensor_reduce(small[:, c:c + 1], mS[:, u % 2, 0:128], AX.X, ALU.max, negate=True)
                    nc.vector.tensor_reduce(small[:, c + 1:c + 2], mS[:, u % 2, 128:384], AX.X, ALU.max, negate=True).then_inc(max_ready, 1)
                if u >= 1:
                    w = u - 1
                    c = w % 2 * 2
                    v.wait_ge(exp_ready, U0 + w + 1)
                    step(nc.vector.reciprocal(small[:, 24 + c:26 + c], small[:, 12 + c:14 + c]))
                    nc.vector.tensor_scalar(mS[:, w % 2, 0:128], mS[:, w % 2, 0:128], small[:, 24 + c:25 + c], None, ALU.mult)
                    nc.vector.tensor_scalar(mS[:, w % 2, 128:384], mS[:, w % 2, 128:384], small[:, 25 + c:26 + c], None, ALU.mult).then_inc(probs_ready, 1)
            v.wait_ge(z_ready, 1)
            for hh in range(GLA_HEADS):
                op = nc.vector.tensor_scalar(lg[:, hh, :], ps[:, 4 + hh // 2, hh % 2 * TOK:(hh % 2 + 1) * TOK], cols[:, C_GLAB + hh:C_GLAB + hh + 1], None, ALU.add)
            op.then_inc(zb_ready, 1)
            v.wait_ge(sp_ready, 1)
            lgf = lg.rearrange("p h t -> p (h t)")
            step(nc.vector.scalar_tensor_tensor(out=lgf, in0=lgf, scalar=0.0, in1=gtmp[:, :], op0=ALU.min, op1=ALU.subtract))
            for hh in range(GLA_HEADS):
                op = nc.vector.tensor_tensor_scan(out=bcum[:, hh * TOK:(hh + 1) * TOK], data0=ones_tok, data1=lg[:, hh, :],
                                                  initial=0.0, op0=ALU.mult, op1=ALU.add)
            step(op)
            for i, s in enumerate((P,) + LEVELS):
                if i > 0:
                    v.wait_ge(decay_ready, i)
                bv = bcum.rearrange("p (n two s) -> p n two s", two=2, s=s)
                gv_ = gtmp.rearrange("p (n two s) -> p n two s", two=2, s=s)
                n = GLA_HEADS * TOK // (2 * s)
                ref = bv[:, :, 0, s - 1:s].to_broadcast([P, n, s])
                nc.vector.tensor_tensor(gv_[:, :, 0, :], ref, bv[:, :, 0, :], ALU.subtract)
                nc.vector.tensor_tensor(gv_[:, :, 1, :], bv[:, :, 1, :], ref, ALU.subtract).then_inc(diff_ready, 1)
                v.wait_ge(decay_ready, i + 1)
                if i > 0:
                    v.wait_ge(lev_ready, (i - 1) * TT + 1)
                nc.vector.tensor_tensor(qd[:, :, :], gqk[:, 0:GLA_HEADS, :], expd.rearrange("p (h t) -> p h t", t=TOK), ALU.mult).then_inc(qk_decayed, 1)
                if i == 1:
                    v.wait_ge(lev_ready, 1)
                    nc.vector.tensor_copy(off[:, :, :], ps[:, 0, :].rearrange("p (h t) -> p h t", t=P)).then_inc(lev_taken, 1)
                if i >= 2:
                    add_level(i - 1)
            add_level(len(LEVELS))
            add_level(len(LEVELS) + 1)
            v.wait_ge(ostd_ready, LAYERS + 1)
            step(nc.vector.reciprocal(rstd[:, :], std[:, :]))
            for c in range(DC):
                op = nc.vector.scalar_tensor_tensor(out=go[:, c, :], in0=go[:, c, :], scalar=cols[:, C_GLAN + c % 2:C_GLAN + c % 2 + 1],
                                                    in1=rstd[:, c // 2 * TOK:(c // 2 + 1) * TOK], op0=ALU.mult, op1=ALU.mult)
            step(op)
            nc.vector.tensor_tensor(go[:, :, :], go[:, :, :], gr[:, :, :], ALU.mult).then_inc(gla_ready, 1)
            for m in range(DC):
                v.wait_ge(sig_ready, LAYERS * DC + m + 1)
                v.wait_ge(ys_ready, LAYERS * DC + m + 1)
                b0 = 2 + 2 * (m % 2)
                step(nc.vector.tensor_tensor(sg2[:, m % 2, :, :], sg2[:, m % 2, :, :], ps[:, b0 + 1, :].rearrange("p (a b) -> p a b", b=TOK), ALU.mult))
                nc.vector.tensor_tensor(merged2[:, m, :], sg2[:, m % 2, 0, :], sg2[:, m % 2, 1, :], ALU.add).then_inc(merged_ready, 1)

            def add_gated(c, bank, half, gate):
                g = mod[:, gate * DC + c:gate * DC + c + 1]
                return nc.vector.scalar_tensor_tensor(out=x[:, c, :], in0=ps[:, bank, half * TOK:(half + 1) * TOK], scalar=g,
                                                      in1=x[:, c, :], op0=ALU.mult, op1=ALU.add)

            for b in range(OUTS):
                v.wait_ge(out_ready, LAYERS * OUTS + b + 1)
                add_gated(2 * b, DOWN + b, 0, 2)
                op = add_gated(2 * b + 1, DOWN + b, 1, 2)
            op.then_inc(x_ready, 1)
            mod_norm(2, 1)
            v.wait_ge(route_ready, 1)
            for t in range(TT):
                step(nc.vector.tensor_tensor(lgt[:, t, :], ps[:, 3, t * EXPERTS:(t + 1) * EXPERTS], brouter[:, :], ALU.add))
                step(nc.vector.max(top8, lgt[:, t, :]))
                step(nc.vector.max_index(topi, top8, lgt[:, t, :]))
                step(nc.vector.tensor_copy(topf, topi[:, 0:TOPK]))
                nc.vector.tensor_scalar(small[:, 56:57], top8[:, 0:1], -1.0, None, ALU.mult).then_inc(top_ready, 1)
                v.wait_ge(topexp_ready, t + 1)
                step(nc.vector.reciprocal(small[:, 58:59], small[:, 57:58]))
                step(nc.vector.tensor_scalar(topw, topw, small[:, 58:59], None, ALU.mult))
                for k in range(TOPK):
                    nc.vector.tensor_scalar(sels[:, k, :], iota[:, 0:EXPERTS], topf[:, k:k + 1], None, ALU.is_equal)
                    op = nc.vector.tensor_scalar(eqs[:, k, :], iota[:, 0:EXPERTS], topf[:, k:k + 1], topw[:, k:k + 1], ALU.is_equal, ALU.mult)
                step(op)
                nc.vector.tensor_tensor(sels[:, 0:2, :], sels[:, 0:2, :], sels[:, 2:4, :], ALU.add)
                step(nc.vector.tensor_tensor(eqs[:, 0:2, :], eqs[:, 0:2, :], eqs[:, 2:4, :], ALU.add))
                nc.vector.tensor_tensor(sel[:, t, :], sels[:, 0, :], sels[:, 1, :], ALU.add)
                op = nc.vector.tensor_tensor(wt[:, t, :], eqs[:, 0, :], eqs[:, 1, :], ALU.add)
                if t < TT - 1:
                    step(op)
            op.then_inc(wt_ready, 1)
            v.wait_ge(ranks_ready, 1)
            rank_ps = ps[:, 2, 0:TT * EXPERTS].rearrange("p (t e) -> p t e", e=EXPERTS)
            step(nc.vector.scalar_tensor_tensor(out=rank[:, :, :], in0=rank_ps, scalar=float(CAP + 1), in1=sel[:, :, :], op0=ALU.add, op1=ALU.mult))
            nc.vector.tensor_scalar(rank[:, :, :], rank[:, :, :], -1.0, None, ALU.add)
            step(nc.vector.tensor_reduce(fullest[:, :], ps[:, 2, TT * EXPERTS:(TT + 1) * EXPERTS], AX.X, ALU.max))
            step(nc.vector.tensor_scalar(flagf[:, :], iota[:, 0:PASSES + 1], float(CAP), fullest[:, 0:1], ALU.mult, ALU.is_lt))
            nc.vector.tensor_copy(flags[:, :], flagf[:, :]).then_inc(flags_ready, 1)
            v.wait_ge(wtT_ready, 1)
            nc.vector.tensor_copy(wtT[0:EXPERTS, :], ps[0:EXPERTS, 3, 0:TOK]).then_inc(wtT_taken, 1)

            for i in range(2 * TT):
                v.wait_ge(bias_sums_ready, i + 1)
                op = nc.vector.tensor_copy(y_tok[:, i // 2, i % 2 * 512:i % 2 * 512 + 512], ps[:, 4 + i, :])
            step(op)

            moe = Steps(v, moe_step)

            def find_places(e):
                for t in range(TT):
                    op = nc.vector.tensor_scalar(place[:, t, :], iota, rank[:, t, bass.ds(e, 1)], None, ALU.is_equal)
                op.then_inc(place_ready, 1)

            def split_weights(n, j):
                for half in range(2):
                    u = 2 * j + half
                    v.wait_ge(whi_ready, n * UNITS_E + (u + 1))
                    nc.vector.tensor_tensor(w_lo[u % W_UNITS], slot(j)[:, half * UNIT:(half + 1) * UNIT], w_hi[u % W_UNITS].bitcast(F32),
                                            ALU.subtract).then_inc(wlo_ready, 1)

            def split_tokens(n):
                v.wait_ge(xhi_ready, n)
                nc.vector.tensor_tensor(xg[:, :, 1, :], ps[:, 2, 0:DC * CAP].rearrange("p (a b) -> p a b", b=CAP), xg[:, :, 0, :].bitcast(F32),
                                        ALU.subtract).then_inc(xg_taken, 1)

            def add_output(n, e, r):
                t, half = divmod(r, 2)
                v.wait_ge(scat_ready, n * (2 * TT) + (r + 1))
                ys = y_tok[:, t, half * 512:half * 512 + 512]
                nc.vector.scalar_tensor_tensor(out=ys, in0=ps[:, 6 + r % 2, :], scalar=wt[:, t, bass.ds(e, 1)], in1=ys, op0=ALU.mult,
                                               op1=ALU.add).then_inc(scat_added, 1)

            def expert_step(p, e, j, after=False, last=False):
                n = p * EXPERTS + e
                moe.base, moe.k = p * (EXPERTS * MOE_STEPS + 1) + e * MOE_STEPS + 1, 2 * j
                if j + 2 < DC:
                    split_weights(n, j + 2)
                elif not last:
                    split_weights(n + 1, j + 2 - DC)
                if j == DC - 2 and not last:
                    split_tokens(n + 2)
                if after:
                    for r in ((), (0,), (1,), (2, 3))[j]:
                        add_output(n - 1, e - 1, r)
                v.wait_ge(hid_ready, n * DC + (j + 1))
                nc.vector.tensor_scalar(lin[:, j % 2, :], ps[:, 3, CAP:2 * CAP], cols[:, bass.ds(e * 16 + (C_BEXP + DC + j), 1)], LIMIT, ALU.add, ALU.min)
                nc.vector.tensor_scalar(glu[:, j % 2, :], ps[:, 3, 0:CAP], cols[:, bass.ds(e * 16 + (C_BEXP + j), 1)], LIMIT, ALU.add, ALU.min).then_inc(glu_ready, 1)
                v.wait_ge(glu_ready, n * DC + (j + 1))
                moe(nc.vector.tensor_scalar(lin[:, j % 2, :], lin[:, j % 2, :], -LIMIT, 1.0, ALU.max, ALU.add))
                moe(nc.vector.tensor_tensor(lin[:, j % 2, :], lin[:, j % 2, :], glu[:, j % 2, :], ALU.mult))
                v.wait_ge(esig_ready, n * DC + (j + 1))
                nc.vector.tensor_tensor(eact[:, j % 4, :], lin[:, j % 2, :], sig[:, j % 2, :], ALU.mult).then_inc(eact_ready, 1)
                if j == HALF and not last:
                    v.wait_ge(placeT_ready, n + 1)
                    find_places(e + 1)

            v.wait_ge(flags_ready, 1)
            with v.Fori(0, PASSES) as p:
                needed = v.value_load(flags[0:1, bass.ds(p, 1)], min_val=0, max_val=1)
                with v.If(needed > 0):
                    n = p * EXPERTS
                    moe.base, moe.k = p * (EXPERTS * MOE_STEPS + 1), 0
                    moe(nc.vector.tensor_scalar(rank[:, :, :], rank[:, :, :], -float(CAP), None, ALU.add))
                    find_places(0)
                    split_weights(n, 0)
                    split_tokens(n + 1)
                    split_weights(n, 1)
                    for j in range(HALF):
                        expert_step(p, 0, j)
                    with v.Fori(0, EXPERTS - 1) as e:
                        for j in range(HALF, DC):
                            expert_step(p, e, j)
                        for j in range(HALF):
                            expert_step(p, e + 1, j, after=True)
                    for j in range(HALF, DC):
                        expert_step(p, EXPERTS - 1, j, last=True)
                    for r in range(2 * TT):
                        add_output(n + (EXPERTS - 1), EXPERTS - 1, r)
            v.drain().then_inc(y_ready, 1)
            v.wait_ge(yT_ready, 1)
            for c in range(DC):
                op = add_gated(c, DOWN + c // 2, c % 2, 5)
            op.then_inc(x_ready, 1)
            norm(LAYERS, 3, cols[:, C_NF:C_NF + DC]).then_inc(h_ready, 1)

        @block.tensor
        def _(pe):
            mm_ = nc.tensor.matmul

            def sums(l, n, tiles=0):
                pe.wait_ge(sq_ready, l * NORMS + n + 1)
                for c in range(DC):
                    mm = mm_(ps[:, SSUM, 0:TOK], ones, sq[:, c, :], start=c == 0, stop=c == DC - 1)
                    if c == 0 and tiles:
                        mm.then_inc(tile_used, tiles)
                mm.then_inc(ssum_ready, 1)

            def ffn_in(l, f, t0, i, g=0):
                s = (i - 1) % 5
                t = t0 + i
                slot = ring[:, t % RING, :]
                pe.wait_ge(tile_landed[t % RING], (l * GROUPS + g + t // RING + 1) * 16)
                for half in range(2):
                    for c in range(DC):
                        b = (half * DC + c) * P
                        mm = mm_(ps[:, ff_banks[s], half * TOK:(half + 1) * TOK], slot[:, b:b + P], h[:, c, :],
                                 start=c == 0, stop=c == DC - 1)
                mm.then_inc(gu_ready, 1)

            def ffn_down(l, f, t0, i, g=0):
                s = (i - 1) % 5
                slot = ring[:, (t0 + i) % RING, :]
                pe.wait_ge(act_ready, l * (2 * FF_TILES) + g * 5 + (f * FF_TILES + i + 1))
                for m in range(DC):
                    b = (2 * DC + m) * P
                    mm = mm_(ps[:, DOWN + m // 2, m % 2 * TOK:(m % 2 + 1) * TOK], slot[:, b:b + P], act[:, s, :],
                             start=i == 0 and m % 2 == 0, stop=i == FF_TILES - 1, skip_group_check=True)
                mm.then_inc(tile_used, 1)

            def ffn(l, f, t0):
                ffn_in(l, f, t0, 0)
                ffn_in(l, f, t0, 1)
                ffn_down(l, f, t0, 0)
                with pe.Fori(0, (FF_TILES - 2) // 5) as g:
                    for s in range(5):
                        ffn_in(l, f, t0, 2 + s, g)
                        ffn_down(l, f, t0, 1 + s, g)
                ffn_down(l, f, t0, FF_TILES - 1)

            def project_t(w, bank, half, m=P):
                for c in range(DC):
                    mm = w.used(mm_(ps[0:m, bank, half * TOK:(half + 1) * TOK], w.take()[:, 0:m], h[:, c, :],
                                    start=c == 0, stop=c == DC - 1))
                return mm

            def project_tok(w, banks, n):
                for c in range(DC):
                    blk = w.take(n)
                    for t in range(TT):
                        mm = mm_(ps[:, banks[t], 0:n * P], h[:, c, t * P:(t + 1) * P], blk, start=c == 0, stop=c == DC - 1)
                        if t == TT - 1:
                            w.used(mm)
                        if c == DC - 1:
                            mm.then_inc(proj_ready, 1)

            def out_proj(w, src):
                for m in range(DC):
                    for c in range(DC):
                        mm = w.used(mm_(ps[:, DOWN + m // 2, m % 2 * TOK:(m % 2 + 1) * TOK], w.take(), src[:, c, :],
                                        start=c == 0, stop=c == DC - 1))
                    if m % 2:
                        mm.then_inc(out_ready, 1)

            pe.wait_ge(konst_landed, 16)
            pe.wait_ge(x_landed, 16)
            for i in range(OUTS):
                for c in range(2 * i, 2 * i + 2):
                    for t in range(TT):
                        mm = nc.tensor.transpose(ps[:, 4 + i, c % 2 * TOK + t * P:c % 2 * TOK + (t + 1) * P], x_tok[:, t, c * P:(c + 1) * P], ident)
                mm.then_inc(xt_ready, 1)
            pe.wait_ge(rel_landed, 2 * 16)
            for i in range(BIAS_HEADS):
                if i >= 4:
                    pe.wait_ge(vec_taken, i - 3)
                mm_(ps[:, i % 4, :], relb[0:BUCKETS + 1, i, :], onehot[0:BUCKETS + 1, min(i // DIL_SLOTS, DIL_GROUPS), :],
                    start=True, stop=True).then_inc(vec_ready, 1)
            pe.wait_ge(vec_taken, BIAS_HEADS)

            with pe.Fori(0, LAYERS) as l:
                sums(l, 0)
                pe.wait_ge(h_ready, l * NORMS + 1)
                ffn(l, 0, 0)
                sums(l, 1)
                pe.wait_ge(h_ready, l * NORMS + 2)
                w = Blocks(pe, l, MIX0)

                def free_bank(r):
                    if r >= 4:
                        pe.wait_ge(proj_taken, l * PROJ + r - 3)

                for r in range(QK_CHUNKS // 2):
                    free_bank(r)
                    project_t(w, r % 4, 0)
                    project_t(w, r % 4, 1).then_inc(proj_ready, 1)
                free_bank(8)
                project_tok(w, (7 % 4, 8 % 4), 4)
                free_bank(10)
                project_tok(w, (9 % 4, 10 % 4), 3)
                pe.wait_ge(proj_taken, l * PROJ + 11)

                def logits(u):
                    if u >= 2:
                        pe.wait_ge(scores_made, l * UNITS + u - 1)
                    b = 2 * (u % 2)
                    if u < DIL_UNITS:
                        s, qt = divmod(u, TT)
                        jobs = [(s, g, DIL_GROUPS + g) for g in range(DIL_GROUPS)]
                    else:
                        hh, qt = divmod(u - DIL_UNITS, TT)
                        jobs = [(m, 2 * DIL_GROUPS + hh, 2 * DIL_GROUPS + DIFF_HEADS + hh) for m in range(2)]
                    for i, (s, cq, ck) in enumerate(jobs):
                        rows = slice(s * DH, (s + 1) * DH)
                        col = 2 * i if u >= DIL_UNITS else i
                        mm = mm_(ps[:, b + col // 2, col % 2 * TOK:(col % 2 + 1) * TOK], qk[rows, cq, qt * P:(qt + 1) * P],
                                 qk[rows, ck, :], start=True, stop=True)
                    mm.then_inc(logits_ready, 1)

                def transposes(u):
                    pe.wait_ge(probs_ready, l * UNITS + u + 1)
                    if u >= 1:
                        pe.wait_ge(pt_taken, l * UNITS + u)
                    for i in range(6 if u < DIL_UNITS else 2):
                        mm = nc.tensor.transpose(ps[:, 4 + i // 4, i % 4 * P:(i % 4 + 1) * P], S[:, u % 2, i * P:(i + 1) * P], ident)
                    mm.then_inc(pt_ready, 1)

                def weighted_values(u):
                    pe.wait_ge(pt_taken, l * UNITS + u + 1)
                    if u < DIL_UNITS:
                        s, qt = divmod(u, TT)
                        for i in range(6):
                            hd = 2 * (i // 2) + s
                            mm = mm_(ps[s * DH:(s + 1) * DH, 6, qt * P:(qt + 1) * P], vb[:, i % 2, hd * DH:(hd + 1) * DH],
                                     PT[:, u % 2, i * P:(i + 1) * P], start=i == 0, stop=i == 5)
                        if u == DIL_UNITS - 1:
                            mm.then_inc(o_ready, 1)
                    else:
                        hh, qt = divmod(u - DIL_UNITS, TT)
                        if hh >= 1 and qt == 0:
                            pe.wait_ge(o_taken, l * 5 + hh)
                        for i in range(2):
                            mm = mm_(ps[:, 7 - hh % 2, qt * P:(qt + 1) * P], vc[:, i, hh * P:(hh + 1) * P],
                                     PT[:, u % 2, i * P:(i + 1) * P], start=i == 0, stop=i == 1)
                        if qt == 1:
                            mm.then_inc(o_ready, 1)

                for u in range(UNITS + 2):
                    if u < UNITS:
                        logits(u)
                    if 1 <= u <= UNITS:
                        transposes(u - 1)
                    if u >= 2:
                        weighted_values(u - 2)
                pe.wait_ge(scores_made, l * UNITS + UNITS)
                project_tok(w, (11 % 4, 12 % 4), 4)
                project_tok(w, (13 % 4, 14 % 4), 4)
                pe.wait_ge(osq_ready, l + 1)
                for i in range(2):
                    mm = mm_(ps[:, 6 + i, :], ones, sq[:, 2 * i:2 * i + 2, :], start=True, stop=True)
                mm.then_inc(ossum_ready, 1)
                pe.wait_ge(proj_taken, l * PROJ + PROJ)

                def dft_channels(g):
                    pe.wait_ge(dft1_taken, l * FOURIER_GROUPS + g + 1)
                    if g >= 2:
                        pe.wait_ge(dft2_taken, l * FOURIER_GROUPS + g - 1)
                    for i in range(2):
                        mm = mm_(ps[:, 2 + g % 2, 0:TOK], dch[:, i, :], dft1[:, g % 2, i * TOK:(i + 1) * TOK],
                                 start=i == 0, stop=i == 1)
                    mm.then_inc(dft2_ready, 1)

                for g in range(FOURIER_GROUPS):
                    if g >= 2:
                        pe.wait_ge(dft1_taken, l * FOURIER_GROUPS + g - 1)
                    for t in range(TT):
                        mm = mm_(ps[:, g % 2, :], a_tok[:, t, g * P:(g + 1) * P], dseq[:, t, :], start=t == 0, stop=t == TT - 1)
                    mm.then_inc(dft1_ready, 1)
                    if g >= 1:
                        dft_channels(g - 1)
                dft_channels(FOURIER_GROUPS - 1)
                pe.wait_ge(pt_taken, l * UNITS + UNITS)
                for m in range(DC):
                    b0 = 4 * (1 - m % 2)
                    if m == 1:
                        pe.wait_ge(dft2_taken, l * FOURIER_GROUPS + FOURIER_GROUPS)
                    if m >= 2:
                        pe.wait_ge(merged_ready, l * DC + m - 1)
                    for j in range(3):
                        mm = project_t(w, b0 + j // 2, j % 2)
                    mm.then_inc(gates_ready, 1)
                    if m == 0:
                        pe.wait_ge(dft2_taken, l * FOURIER_GROUPS + FOURIER_GROUPS)
                        pe.wait_ge(o_taken, l * 5 + 5)
                        pe.wait_ge(yc_ready, l + 1)
                    for c in range(FOURIER_GROUPS):
                        w.used(mm_(ps[:, b0 + 2, 0:TOK], w.take(), four[:, c, :], start=c == 0, stop=c == FOURIER_GROUPS - 1))
                    w.used(mm_(ps[:, b0 + 2, TOK:2 * TOK], w.take(), ob[:, :], start=True, stop=True))
                    for c in range(DIFF_HEADS):
                        mm = w.used(mm_(ps[:, b0 + 3, 0:TOK], w.take(), oc[:, c, :], start=c == 0, stop=c == DIFF_HEADS - 1))
                    mm.then_inc(ys_ready, 1)
                last = MIX0 + MIX_TILES
                for t in range(last, last + PAD_TILES):
                    pe.wait_ge(tile_landed[t % RING], (l * GROUPS + t // RING + 1) * 16)
                pe.wait_ge(merged_ready, l * DC + DC)
                out_proj(w, merged)
                sums(l, 2, PAD_TILES + 1)
                pe.wait_ge(h_ready, l * NORMS + 3)
                ffn(l, 1, FFN2)

            sums(LAYERS, 0)
            w = Blocks(pe, LAYERS, 0)
            pe.wait_ge(cact_ready, 1)
            for m in range(ADA):
                for c in range(DC):
                    mm = w.used(mm_(ps[:, 3, m:m + 1], w.take(), small[:, 16 + c:17 + c], start=c == 0, stop=c == DC - 1))
            mm.then_inc(ada_ready, 1)
            sums(LAYERS, 1)
            pe.wait_ge(h_ready, LAYERS * NORMS + 1)
            R0 = LAYERS * PROJ

            def free2(r):
                if r >= 4:
                    pe.wait_ge(proj_taken, R0 + r - 3)

            def project_pairs(r0, n):
                for r in range(r0, r0 + n):
                    free2(r)
                    project_t(w, r % 4, 0)
                    project_t(w, r % 4, 1).then_inc(proj_ready, 1)

            for i in range(2):
                free2(2 * i + 1)
                project_tok(w, (2 * i % 4, (2 * i + 1) % 4), 4)
            project_pairs(4, 8)
            for i in range(HEADS):
                if i >= 2:
                    pe.wait_ge(roped, i - 1)
                pe.wait_ge(proj_taken, R0 + 5 + i)
                mm_(ps[0:ROT, 4 + i % 2, :], rotT, mqk[0:ROT, 2 * i:2 * i + 2, :], start=True, stop=True).then_inc(rot_ready, 1)
            pe.wait_ge(roped, HEADS)
            U0 = LAYERS * UNITS
            for u in range(HEADS + 2):
                if u < HEADS:
                    if u >= 2:
                        pe.wait_ge(scores_made, U0 + u - 1)
                    q, k = mqk[:, u, :], mqk[:, HEADS + u, :]
                    mm_(ps[:, u % 2, 0:P], q[:, 0:P], k[:, 0:P], start=True, stop=True)
                    mm_(ps[:, u % 2, P:3 * P], q[:, P:TOK], k, start=True, stop=True).then_inc(logits_ready, 1)
                if 1 <= u <= HEADS:
                    pe.wait_ge(probs_ready, U0 + u)
                    if u >= 2:
                        pe.wait_ge(pt_taken, U0 + u - 1)
                    for i in range(3):
                        mm = nc.tensor.transpose(ps[:, 4, i * P:(i + 1) * P], mS[:, (u - 1) % 2, i * P:(i + 1) * P], ident)
                    mm.then_inc(pt_ready, 1)
                if u >= 2:
                    hd = u - 2
                    pe.wait_ge(pt_taken, U0 + hd + 1)
                    if hd >= 2:
                        pe.wait_ge(o_taken, LAYERS * 5 + hd - 1)
                    vs = [mv[:, t, hd * P:(hd + 1) * P] for t in range(TT)]
                    pt = mPT[:, hd % 2, :]
                    mm_(ps[:, 6 + hd % 2, 0:P], vs[0], pt[:, 0:P], start=True, stop=True)
                    mm_(ps[:, 6 + hd % 2, P:TOK], vs[0], pt[:, P:2 * P], start=True, stop=False)
                    mm_(ps[:, 6 + hd % 2, P:TOK], vs[1], pt[:, 2 * P:3 * P], start=False, stop=True).then_inc(o_ready, 1)
            pe.wait_ge(scores_made, U0 + HEADS)
            project_pairs(12, 4)
            free2(16)
            project_t(w, 0, 0, RANK).then_inc(proj_ready, 1)
            project_pairs(17, 4)
            free2(22)
            project_tok(w, (21 % 4, 22 % 4), 4)
            free2(24)
            project_tok(w, (23 % 4, 24 % 4), 4)
            pe.wait_ge(pt_taken, U0 + HEADS)
            pe.wait_ge(proj_taken, R0 + 17)
            for hh in range(GLA_HEADS):
                mm = mm_(ps[:, 4 + hh // 2, hh % 2 * TOK:(hh % 2 + 1) * TOK], glaw[:, hh * P:(hh + 1) * P], glow[0:RANK, :], start=True, stop=True)
            mm.then_inc(z_ready, 1)
            pe.wait_ge(proj_taken, R0 + 25)
            pe.wait_ge(k_decayed, 1)
            pe.wait_ge(qk_decayed, 1)
            for hh in range(GLA_HEADS):
                mm = mm_(ps[:, 0, hh * P:(hh + 1) * P], kd[:, hh, 0:P], qd[:, hh, P:TOK], start=True, stop=True)
            mm.then_inc(lev_ready, 1)
            for i in range(1, len(LEVELS) + 2):
                if i <= len(LEVELS):
                    pe.wait_ge(k_decayed, i + 1)
                    pe.wait_ge(qk_decayed, i + 1)
                q, k = (qd, kd) if i <= len(LEVELS) else (gqk[:, 0:GLA_HEADS], gqk[:, GLA_HEADS:])
                if i == 2:
                    pe.wait_ge(lev_taken, 1)
                if i >= 3:
                    pe.wait_ge(lev_taken, 1 + (i - 2) * TT)
                for t in range(TT):
                    for hh in range(GLA_HEADS):
                        mm = mm_(ps[:, 2 * (i % 2) + t, hh * P:(hh + 1) * P], k[:, hh, t * P:(t + 1) * P], q[:, hh, t * P:(t + 1) * P],
                                 start=True, stop=True)
                    mm.then_inc(lev_ready, 1)
            pe.wait_ge(scores_done, 1)
            for c in range(DC):
                hh = c // 2
                o = ps[:, 4 + c // 2, c % 2 * TOK:(c % 2 + 1) * TOK]
                vs = [gv[:, t, c * P:(c + 1) * P] for t in range(TT)]
                mm_(o[:, 0:P], vs[0], acc[:, 0, hh, :], start=True, stop=True)
                mm_(o[:, P:TOK], vs[0], off[:, hh, :], start=True, stop=False)
                mm = mm_(o[:, P:TOK], vs[1], acc[:, 1, hh, :], start=False, stop=True)
                if c % 2:
                    mm.then_inc(go_ready, 1)
            pe.wait_ge(osq_ready, LAYERS + 1)
            for hh in range(GLA_HEADS):
                for i in range(2):
                    mm = mm_(ps[:, hh // 2, hh % 2 * TOK:(hh % 2 + 1) * TOK], ones, sq[:, 2 * hh + i, :], start=i == 0, stop=i == 1)
            mm.then_inc(ossum_ready, 1)
            for m in range(DC):
                b0 = 2 + 2 * (m % 2)
                if m >= 2:
                    pe.wait_ge(merged_ready, LAYERS * DC + m - 1)
                project_t(w, b0, 0)
                project_t(w, b0, 1).then_inc(gates_ready, 1)
                for c in range(HEADS):
                    w.used(mm_(ps[:, b0 + 1, 0:TOK], w.take(), oa[:, c, :], start=c == 0, stop=c == DC - 1))
                if m == 0:
                    pe.wait_ge(gla_ready, 1)
                for c in range(DC):
                    mm = w.used(mm_(ps[:, b0 + 1, TOK:2 * TOK], w.take(), go[:, c, :], start=c == 0, stop=c == DC - 1))
                mm.then_inc(ys_ready, 1)
            pe.wait_ge(merged_ready, LAYERS * DC + DC)
            out_proj(w, merged2)
            sums(LAYERS, 2, 1)
            pe.wait_ge(h_ready, LAYERS * NORMS + 2)
            for t in range(TT):
                for c in range(DC):
                    mm = mm_(ps[:, 3, t * EXPERTS:(t + 1) * EXPERTS], h[:, c, t * P:(t + 1) * P], router[:, c, :], start=c == 0, stop=c == DC - 1)
            mm.then_inc(route_ready, 1)
            for i in range(2 * TT):
                for c in range(4):
                    mm = nc.tensor.transpose(ps[:, 4 + i, c * P:(c + 1) * P], h[:, i % 2 * 4 + c, i // 2 * P:(i // 2 + 1) * P], ident)
                mm.then_inc(htok_ready, 1)
            pe.wait_ge(wt_ready, 1)
            for t in range(TT):
                mm = nc.tensor.transpose(ps[0:EXPERTS, 3, t * P:(t + 1) * P], wt[:, t, :], ident)
            mm.then_inc(wtT_ready, 1)
            for t in range(TT):
                cols_t = slice(t * EXPERTS, (t + 1) * EXPERTS)
                for k in range(t):
                    mm_(ps[:, 2, cols_t], ones, sel[:, k, :], start=k == 0, stop=False)
                mm_(ps[:, 2, cols_t], before, sel[:, t, :], start=t == 0, stop=True)
            for t in range(TT):
                mm = mm_(ps[:, 2, TT * EXPERTS:(TT + 1) * EXPERTS], ones, sel[:, t, :], start=t == 0, stop=t == TT - 1)
            mm.then_inc(ranks_ready, 1)
            pe.wait_ge(wtT_taken, 1)
            for i in range(2 * TT):
                pe.wait_ge(htok_taken, i + 1)
                mm_(ps[:, 4 + i, :], wtT[0:EXPERTS, i // 2 * P:(i // 2 + 1) * P], bout[:, i % 2 * 512:i % 2 * 512 + 512], start=True,
                    stop=True).then_inc(bias_sums_ready, 1)

            def gather(n):
                pe.wait_ge(place_ready, n)
                for c in range(DC):
                    for t in range(TT):
                        mm = mm_(ps[:, 2, c * CAP:(c + 1) * CAP], h_tok[:, t, c * P:(c + 1) * P], place[:, t, :], start=t == 0, stop=t == TT - 1)
                mm.then_inc(xg_ready, 1)

            def expert_in(n, j):
                if j == 0:
                    pe.wait_ge(xg_taken, n + 1)
                for i in range(2):
                    u = 2 * j + i
                    pe.wait_ge(wlo_ready, n * UNITS_E + (u + 1))
                    for c in range(DC // 2):
                        for part in (w_hi, w_lo):
                            mm = mm_(ps[0:2 * CAP, j % 2, 0:2 * P], xg[:, i * (DC // 2) + c, :, :], part[u % W_UNITS][:, c * 2 * P:(c + 1) * 2 * P],
                                     start=i == 0 and c == 0 and part is w_hi, stop=i == 1 and c == DC // 2 - 1 and part is w_lo)
                    mm.then_inc(w_used, 1)

            def turn(n, j, first=False):
                pe.wait_ge(htok_copied, n * DC + (j + 1))
                if not first:
                    pe.wait_ge(glu_ready, n * DC + j)
                for half in range(2):
                    mm = mm_(ps[:, 3, half * CAP:(half + 1) * CAP], hid_tok[0:2 * CAP, j % 2, half * P:(half + 1) * P], fold, start=True, stop=True)
                mm.then_inc(hid_ready, 1)

            def expert_out(n, j):
                pe.wait_ge(eact_ready, n * DC + (j + 1))
                for half in range(2):
                    b = 2 * DC * P + half * 512
                    mm = mm_(ps[0:CAP, 4 + half, :], eact[:, j % 4, :], slot(j)[:, b:b + 512], start=j == 0, stop=j == DC - 1)
                    if j == DC - 1 and half == 0:
                        mm.then_inc(eout_ready, 1)
                mm.then_inc(moe_used, 1)

            def back(n, r):
                t, half = divmod(r, 2)
                if r == 0:
                    pe.wait_ge(placeT_taken, n + 1)
                    pe.wait_ge(eout_taken, n * 2 + 2)
                if t > 0:
                    pe.wait_ge(scat_added, n * (2 * TT) + (r - 1))
                mm_(ps[:, 6 + r % 2, :], placeT[0:CAP, t * P:(t + 1) * P], outd[0:CAP, half * 512:half * 512 + 512], start=True,
                    stop=True).then_inc(scat_ready, 1)

            def expert_step(n, j, after=False, last=False):
                if j + 2 < DC:
                    expert_in(n, j + 2)
                elif not last:
                    expert_in(n + 1, j + 2 - DC)
                if j == HALF + 1 and not last:
                    pe.wait_ge(placeT_taken, n + 1)
                    gather(n + 2)
                if j + 1 < DC:
                    turn(n, j + 1)
                elif not last:
                    turn(n + 1, 0)
                if j == HALF:
                    for t in range(TT):
                        mm = nc.tensor.transpose(ps[0:CAP, 2, t * P:(t + 1) * P], place[:, t, :], ident)
                    mm.then_inc(placeT_ready, 1)
                if after:
                    for r in ((0,), (1,), (2, 3), ())[j]:
                        back(n - 1, r)
                expert_out(n, j)

            pe.wait_ge(flags_ready, 1)
            with pe.Fori(0, PASSES) as p:
                needed = pe.value_load(flags[0:1, bass.ds(p, 1)], min_val=0, max_val=1)
                with pe.If(needed > 0):
                    n = p * EXPERTS
                    gather(n + 1)
                    expert_in(n, 0)
                    expert_in(n, 1)
                    turn(n, 0, True)
                    for j in range(HALF):
                        expert_step(n, j)
                    with pe.Fori(0, EXPERTS - 1) as e:
                        for j in range(HALF, DC):
                            expert_step(p * EXPERTS + e, j)
                        for j in range(HALF):
                            expert_step(p * EXPERTS + e + 1, j, after=True)
                    for j in range(HALF, DC):
                        expert_step(n + (EXPERTS - 1), j, last=True)
                    for r in range(2 * TT):
                        back(n + (EXPERTS - 1), r)
            pe.wait_ge(y_ready, 1)
            for c in range(DC):
                for t in range(TT):
                    mm = nc.tensor.transpose(ps[:, DOWN + c // 2, c % 2 * TOK + t * P:c % 2 * TOK + (t + 1) * P], y_tok[:, t, c * P:(c + 1) * P], ident)
            mm.then_inc(yT_ready, 1)
            sums(LAYERS, 3)
            pe.wait_ge(h_ready, LAYERS * NORMS + 3)
            for i in range(2 * OUTS):
                t, half = divmod(i, OUTS)
                if i >= 4:
                    pe.wait_ge(ytok_taken, i - 3)
                for c in range(2):
                    mm = nc.tensor.transpose(ps[:, i % 4, c * P:(c + 1) * P], h[:, 2 * half + c, t * P:(t + 1) * P], ident)
                mm.then_inc(ytok_ready, 1)


def constants():
    k = np.zeros((P, KONST), np.float32)
    k[:, K_ID:K_ID + P] = np.eye(P)
    k[:, K_ONES:K_ONES + TOK] = 1.0
    r = np.arange(P)
    tri = np.where(r[None, :] <= r[:, None], 0.0, NEG)
    k[:, K_CAUSAL:K_CAUSAL + 384] = np.concatenate([tri, np.zeros((P, P)), tri], 1)
    for i, s in enumerate(LEVELS):
        j, q = r[:, None], r[None, :]
        k[:, K_LEVEL + i * P:K_LEVEL + (i + 1) * P] = (j // (2 * s) == q // (2 * s)) & (j % (2 * s) < s) & (q % (2 * s) >= s)
    k[:, K_LEVEL + 7 * P:K_LEVEL + 8 * P] = np.eye(P)
    k[:, K_IOTA:K_IOTA + CAP] = np.arange(CAP)
    k[:, K_BEFORE:K_BEFORE + P] = r[:, None] < r[None, :]
    k[:, K_FOLD:K_FOLD + CAP] = r[:, None] % CAP == np.arange(CAP)
    k[:, K_EPS:K_EPS + 3] = (EPS1, EPS2, 1.0)
    ang = 2 * np.pi * np.outer(np.arange(TOK), np.arange(TOK)) / TOK
    seq = np.concatenate([np.cos(ang), np.sin(ang)], 1) / math.sqrt(TOK)
    k[:, K_DSEQ:K_DSEQ + 2 * VEC] = seq.reshape(TT, P, VEC).transpose(1, 0, 2).reshape(P, -1)
    ang = 2 * np.pi * np.outer(r, r) / P
    k[:, K_DCH:K_DCH + 2 * P] = np.concatenate([np.cos(ang), -np.sin(ang)], 1) / math.sqrt(P)
    half = ROT // 2
    freq = np.float32(500000.0) ** (-np.arange(half, dtype=np.float32) * np.float32(2.0) / np.float32(ROT))
    a = (np.arange(TOK, dtype=np.float32)[:, None] * freq[None, :]).T
    k[0:ROT, K_COS:K_COS + TOK] = np.cos(np.concatenate([a, a]))
    k[0:ROT, K_SIN:K_SIN + TOK] = np.sin(np.concatenate([a, a]))
    for i in range(half):
        k[half + i, K_ROT + i] = -1.0
        k[i, K_ROT + half + i] = 1.0
    return k


def bucket_tables():
    rel = np.arange(VEC) - (TOK - 1)
    half = BUCKETS // 2
    exact = half // 2
    n = np.abs(rel)
    nf = np.maximum(n, 1).astype(np.float32)
    large = exact + (np.log(nf / np.float32(exact)) / np.float32(math.log(MAX_DISTANCE / exact)) * np.float32(half - exact)).astype(np.int32)
    bucket = np.where(rel > 0, half, 0) + np.where(n < exact, n, np.minimum(large, half - 1))
    tables = np.zeros((BUCKETS + 1, 4, VEC), np.float32)
    for g in range(4):
        seen = np.ones(VEC, bool)
        if g < DIL_GROUPS:
            window, dil = DIL_PAIRS[g]
            seen = (n % dil == 0) & (n // dil <= window // (2 * dil))
        tables[bucket[seen], g, np.nonzero(seen)[0]] = 1.0
        tables[BUCKETS, g, ~seen] = NEG
    return tables


def by_output(w):
    k, n = w.shape
    return w.reshape(k // P, P, n // P, P).transpose(2, 0, 1, 3).reshape(-1, P, P)


def by_input(w, n):
    k, cols = w.shape
    return w.reshape(k // P, P, cols // (n * P), n, P).transpose(2, 0, 3, 1, 4).reshape(-1, P, P)


def tiles(blocks, n):
    b = np.concatenate(blocks)
    b = np.concatenate([b, np.zeros((n * TILE_BLOCKS - len(b), P, P), np.float32)])
    return b.reshape(n, TILE_BLOCKS, P, P).transpose(0, 2, 1, 3).reshape(n, P, TILE)


def ffn_tiles(gate, up, down):
    f = gate.shape[-1] // P
    t = np.empty((f, P, 3, DC, P), np.float32)
    t[:, :, 0] = gate.reshape(DC, P, f, P).transpose(2, 1, 0, 3)
    t[:, :, 1] = up.reshape(DC, P, f, P).transpose(2, 1, 0, 3)
    t[:, :, 2] = down.reshape(f, P, DC, P)
    return t.reshape(f, P, TILE)


def columns(v):
    v = np.asarray(v, np.float32).reshape(-1, P)
    return v.T


def lay_out(i):
    parts = []
    for l in range(LAYERS):
        parts.append(ffn_tiles(i["w_ffn1_gate"][l], i["w_ffn1_up"][l], i["w_ffn1_down"][l]))
        w_in = i["w_in"][l]
        qa, ka, va = (w_in[:, D + 384 * n:D + 384 * (n + 1)] for n in range(3))
        qc, kc, vcw = (w_in[:, 2176 + 512 * n:2176 + 512 * (n + 1)] for n in range(3))
        blocks = [by_output(w) for w in (qa, ka, qc, kc)] + [by_input(vcw, 4), by_input(va, 3), by_input(w_in[:, :D], 4)]
        gate = by_output(i["w_gate"][l]).reshape(3, DC, DC, P, P).transpose(1, 0, 2, 3, 4).reshape(DC, 3 * DC, P, P)
        branch = [by_output(i[n][l]).reshape(DC, -1, P, P) for n in ("w_br_a", "w_br_b", "w_br_c")]
        blocks += [np.concatenate([gate] + branch, 1).reshape(-1, P, P), by_output(i["w_out"][l])]
        parts.append(tiles(blocks, MIX_TILES + PAD_TILES))
        parts.append(ffn_tiles(i["w_ffn2_gate"][l], i["w_ffn2_up"][l], i["w_ffn2_down"][l]))
    w_in = i["w_in_2"][0]
    cut = np.cumsum([0, D, D, D, 512, 512, D, D, RANK, D, D])
    mq, mk, mvw, gq, gk, gvw, grw, low, ga, gb = (w_in[:, a:b] for a, b in zip(cut[:-1], cut[1:]))
    low = np.pad(low, ((0, 0), (0, P - RANK)))
    blocks = [by_output(i["w_ada_2"][0]), by_input(mvw, 4)] + [by_output(w) for w in (mq, mk, gq, gk, low, grw)] + [by_input(gvw, 4)]
    blocks.append(np.concatenate([by_output(w).reshape(DC, DC, P, P) for w in (ga, gb, i["w_o_moba_2"][0], i["w_o_gla_2"][0])], 1).reshape(-1, P, P))
    blocks.append(by_output(i["w_out_2"][0]))
    parts.append(tiles(blocks, SEC_TILES))
    w_exp = i["w_exp_in_2"][0]
    experts = np.empty((EXPERTS, DC, P, 3, DC, P), np.float32)
    ins = experts[:, :, :, 0:2].reshape(EXPERTS, DC, P, DC, 2, P)
    for half in range(2):
        ins[:, :, :, :, half] = w_exp[:, :, half::2].reshape(EXPERTS, DC, P, DC, P).transpose(0, 3, 2, 1, 4)
    experts[:, :, :, 0:2] = ins.reshape(EXPERTS, DC, P, 2, DC, P)
    experts[:, :, :, 2] = i["w_exp_out_2"][0].reshape(EXPERTS, DC, P, DC, P)

    layers = np.zeros((P, LAYERS, LP), np.float32)
    for l in range(LAYERS):
        lam_init = 0.8 - 0.6 * math.exp(-0.3 * l)
        layers[:, l, :LP_LAM] = np.concatenate([columns(i[n][l]) for n in ("g_ffn1", "g_mix", "g_ffn2", "b_gate", "subln_g")]
                                               + [np.full((P, 1), lam_init), np.full((P, 1), 1 - lam_init)], 1)
        layers[:, l, LP_LAM:] = np.concatenate([i[n][l] for n in ("lam_q1", "lam_k1", "lam_q2", "lam_k2")])[None]
    b_exp = i["b_exp_in_2"][0]
    b_exp = np.concatenate([b_exp[:, 0::2].reshape(EXPERTS, DC, P), b_exp[:, 1::2].reshape(EXPERTS, DC, P)], 1)
    cols = np.concatenate([columns(i[n]) for n in ("c_2", "g_final", "b_ada_2", "norm1_w_2", "gla_gate_b_2", "gla_norm_w_2", "b_merge_2",
                                                   "norm2_w_2", "final_norm_w_2")] + [columns(b_exp)], 1)
    relb = np.ones((BUCKETS + 1, BIAS_HEADS, P), np.float32)
    relb[:BUCKETS] = i["rel_bias"][:, :, None]
    return {
        "stream": np.concatenate(parts),
        "experts": experts.reshape(EXPERTS * DC, P, TILE),
        "x": i["x"].reshape(TOK, D),
        "konst": constants(),
        "layers": layers,
        "cols": cols,
        "relb": relb,
        "onehot": bucket_tables(),
        "glaw": i["gla_gate_w_2"][0],
        "router": i["w_router_2"][0].reshape(DC, P, EXPERTS).transpose(1, 0, 2),
        "brouter": np.broadcast_to(i["b_router_2"], (P, EXPERTS)),
        "bout": i["b_exp_out_2"][0],
    }


def kernel(**inputs):
    import concourse.bacc as bacc
    from concourse.bass_utils import run_bass_kernel_spmd

    arrays = {n: np.ascontiguousarray(a) for n, a in lay_out({k: np.asarray(v) for k, v in inputs.items()}).items()}
    nc = bacc.Bacc("TRN2", target_bir_lowering=False, num_devices=1)
    args = [nc.dram_tensor("in_" + n, a.shape, F32, kind="ExternalInput").ap() for n, a in arrays.items()]
    rows = nc.dram_tensor("bias_rows", (BIAS_HEADS, P, VEC), F32, kind="Internal").ap()
    out = nc.dram_tensor("out", (TOK, D), F32, kind="ExternalOutput").ap()
    build(nc, *args, rows, out)
    r = run_bass_kernel_spmd(nc, [{"in_" + n: a for n, a in arrays.items()}], core_ids=[0])
    return r.results[0]["out"].reshape(1, TOK, D)
```

```python
import math
from contextlib import ExitStack

import concourse.bass as bass
from concourse import mybir
import numpy as np

F32 = mybir.dt.float32
U32 = mybir.dt.uint32
I32 = mybir.dt.int32
F32R = mybir.dt.float32r
ALU = mybir.AluOpType
ACT = mybir.ActivationFunctionType
AX = mybir.AxisListType

P = 128
TOK = 256
TT = TOK // P
D = 1024
DC = D // P
LAYERS = 2
D_FF = 2816
FF_TILES = D_FF // P
TILE_BLOCKS = 3 * DC
TILE = TILE_BLOCKS * P
RING = 5
WORK, WORK2 = 16128, 4352

EPS1, EPS2, SUBLN_EPS = 1e-6, 1e-5, 1e-5
NEG = -1e30

DIL_PAIRS = ((128, 1), (512, 4), (2048, 16))
DIL_GROUPS, DIL_SLOTS, DH = 3, 2, 64
DIFF_HEADS = 4
BIAS_HEADS = DIL_GROUPS * DIL_SLOTS + DIFF_HEADS
BUCKETS, MAX_DISTANCE = 32, 1024
QK_CHUNKS = 2 * DIL_GROUPS + 2 * DIFF_HEADS
UNITS = DIL_SLOTS * TT + DIFF_HEADS * TT
DIL_UNITS = DIL_SLOTS * TT
FOURIER_GROUPS = 8
MERGE_BLOCKS = 3 * DC + DC + 1 + DIFF_HEADS
VEC = 2 * TOK
PROJ = QK_CHUNKS // 2 + 2 * TT + 2 * TT
MIX_BLOCKS = QK_CHUNKS * DC + 3 * DC + 4 * DC + 8 * DC + DC * MERGE_BLOCKS + DC * DC
MIX_TILES = -(-MIX_BLOCKS // TILE_BLOCKS)
LAYER_TILES = -(-(2 * FF_TILES + MIX_TILES) // RING) * RING
PAD_TILES = LAYER_TILES - 2 * FF_TILES - MIX_TILES
GROUPS = LAYER_TILES // RING
MIX0, FFN2 = FF_TILES, FF_TILES + MIX_TILES + PAD_TILES
NORMS = 3
OUTS = DC // 2

HEADS = 8
GLA_HEADS, GLA_DV = 4, 256
RANK = 16
ROT = 32
ADA = 6 * DC
ADA_TILES = ADA * DC // TILE_BLOCKS
SEC_BLOCKS = 16 * DC + 8 * DC + (4 + 4 + 8 + 1) * DC + 8 * DC + DC * 4 * DC + DC * DC
SEC_TILES = ADA_TILES + -(-SEC_BLOCKS // TILE_BLOCKS)
DENSE_TILES = LAYERS * LAYER_TILES + SEC_TILES
LEVELS = (64, 32, 16, 8, 4, 2, 1)
EXPERTS, TOPK = 32, 4
HALF = DC // 2
MOE_RING = DC
UNIT, UNITS_E, W_UNITS = DC * P, 2 * DC, 4
CAP = 64
PASSES = TOK // CAP
LAYER_STEPS, MOE_STEPS = 44, 2 * DC
ALPHA, LIMIT = 1.702, 7.0

LP_FFN1, LP_MIX, LP_FFN2, LP_BGATE, LP_SUBLN, LP_LAMI, LP_LAM = 0, 8, 16, 24, 48, 49, 51
LP = LP_LAM + 4 * DH
(C_X, C_GFIN, C_BADA, C_N1, C_GLAB, C_GLAN, C_BMERGE, C_N2, C_NF, C_BEXP) = (
    0, 8, 16, 64, 72, 76, 78, 94, 102, 110)
COLS = C_BEXP + EXPERTS * 16
K_ID, K_ONES, K_CAUSAL, K_LEVEL, K_IOTA = 0, 128, 384, 768, 768 + 8 * 128
K_BEFORE, K_FOLD, K_EPS = K_IOTA + CAP, K_IOTA + CAP + P, K_IOTA + 2 * CAP + P
K_DSEQ = K_EPS + 4
K_DCH = K_DSEQ + 2 * VEC
K_COS, K_SIN, K_ROT = K_DCH + 2 * P, K_DCH + 2 * P + TOK, K_DCH + 2 * P + 2 * TOK
KONST = K_ROT + ROT


def build(nc, stream, experts, x_in, konst_in, layer_in, cols_in, relb_in, onehot_in, glaw_in,
          router_in, brouter_in, bout_in, bias_rows, out):
    with ExitStack() as ctx:
        def sb(name, shape, dt=F32):
            return ctx.enter_context(nc.sbuf_tensor(name, shape, dt))

        def sem(name):
            return ctx.enter_context(nc.semaphore(name))

        ring = sb("ring", [P, RING, TILE])
        x = sb("x", [P, DC, TOK])
        konst = sb("konst", [P, KONST])
        lp_all = sb("lp_all", [P, LAYERS, LP])
        lp = sb("lp", [P, LP])
        cols = sb("cols", [P, COLS])
        glaw = sb("glaw", [RANK, 512])
        router = sb("router", [P, DC, EXPERTS])
        brouter = sb("brouter", [P, EXPERTS])
        bout = sb("bout", [EXPERTS, D])
        small = sb("small", [P, 64])
        mod = sb("mod", [P, ADA])
        modgain = sb("modgain", [P, 2 * DC])
        with ExitStack() as dense:
            def sb_dense(name, shape):
                return dense.enter_context(nc.sbuf_tensor(name, shape, F32))

            work = sb_dense("work", [P, WORK])
            h = sb_dense("h", [P, DC, TOK])
            sq = sb_dense("sq", [P, DC, TOK])
            std = sb_dense("std", [P, 4 * TOK])
            rstd = sb_dense("rstd", [P, 4 * TOK])
            work2 = sb_dense("work2", [P, WORK2])
        sb("under_biases", [P, BIAS_HEADS * TT * TOK])
        f_hi = [sb(f"f_hi{i}", [P, UNIT], F32R)[:, :] for i in range(3)]
        f_lo = [sb(f"f_lo{i}", [P, UNIT], F32R)[:, :] for i in range(3)]
        h_hi = sb("h_hi", [P, DC, TOK], F32R)
        h_lo = sb("h_lo", [P, DC, TOK], F32R)
        sb("rest_of_work", [P, WORK - BIAS_HEADS * TT * TOK - 6 * UNIT - 2 * DC * TOK])
        with ExitStack() as ffn_over:
            ffn_over.enter_context(nc.sbuf_tensor("under_norms", [P, 2 * DC * TOK + 8 * TOK], F32))
            act_hi = ffn_over.enter_context(nc.sbuf_tensor("act_hi", [P, 3, TOK], F32R))
            act_lo = ffn_over.enter_context(nc.sbuf_tensor("act_lo", [P, 3, TOK], F32R))
        w_hi = [sb(f"w_hi{i}", [P, UNIT], F32R)[:, :] for i in range(W_UNITS)]
        w_lo = [sb(f"w_lo{i}", [P, UNIT], F32R)[:, :] for i in range(W_UNITS)]
        xg = sb("xg", [P, DC, 2, CAP], F32R)[:, :, :, :]
        moe_work = sb("moe_work", [P, 12 * CAP + TOK + 4 * P])
        ps = ctx.enter_context(nc.psum_tensor("ps", [P, 8, 512], F32))

        def carve(at, *shape):
            n = math.prod(shape)
            v = work[:, at:at + n] if at < WORK else work2[:, at - WORK:at - WORK + n]
            if len(shape) == 2:
                v = v.rearrange("p (a b) -> p a b", b=shape[1])
            if len(shape) == 3:
                v = v.rearrange("p (a b c) -> p a b c", b=shape[1], c=shape[2])
            return v

        bias = carve(0, BIAS_HEADS, TT, TOK)
        vecs = ring[:, RING - 2:, :].rearrange("p a b -> p (a b)")[:, 0:BIAS_HEADS * VEC].rearrange("p (a b) -> p a b", b=VEC)
        relb = carve(10240, BIAS_HEADS, P)
        onehot = carve(11520, 4, VEC)
        x_tok = carve(13568, TT, D)
        silu = carve(17920, 5, TOK)
        act = carve(19200, 5, TOK)
        qk = carve(5120, QK_CHUNKS, TOK)
        vc = carve(8704, TT, 512)
        vb = carve(9728, TT, 384)
        a_tok = carve(10496, TT, D)
        four = carve(12544, FOURIER_GROUPS, TOK)
        S = [carve(at, 768) for at in (14592, 15360, 18944)]
        C_MAX, C_SUM, C_REC = (8, 10, 28), (12, 14, 30), (24, 26, 59)
        PT = carve(16128, 2, 768)
        ob = carve(17664, TOK)
        oc = carve(17920, DIFF_HEADS, TOK)
        dft1 = carve(5120, 2, VEC)
        merged = carve(10496, DC, TOK)
        sg = carve(14592, 2, 3, TOK)
        row = h[:, 0:4, :].rearrange("p (a b) c -> p a (b c)", b=2)
        mqk = carve(0, 16, TOK)
        mv = carve(4096, TT, D)
        oa = carve(6144, HEADS, TOK)
        mS = [carve(at, 384) for at in (8192, 8576, 9984)]
        mPT = carve(8960, 2, 384)
        gqk = carve(0, 2 * GLA_HEADS, TOK)
        lg = carve(2048, GLA_HEADS, TOK)
        bcum = carve(3072, GLA_HEADS * TOK)
        glow = carve(9728, TOK)
        off = carve(9984, GLA_HEADS, P)
        tmp = carve(10496, GLA_HEADS, P)
        gv = carve(11008, TT, D)
        gr = carve(13056, DC, TOK)
        expd = carve(15104, GLA_HEADS * TOK)
        qd = [carve(at, GLA_HEADS, TOK) for at in (16128, 4096)]
        kd = [carve(at, GLA_HEADS, TOK) for at in (17152, 5120)]
        acc = carve(18176, TT, GLA_HEADS, P)
        gtmp = carve(19200, GLA_HEADS * TOK)
        go = carve(4096, DC, TOK)
        merged2 = carve(0, DC, TOK)
        sg2 = carve(16128, 2, 2, TOK)
        moe_hi = carve(0, 3, TILE)
        wt = carve(9216, TT, EXPERTS)
        wtT = carve(9280, TOK)
        sel = carve(9536, TT, EXPERTS)
        rank = carve(9600, TT, EXPERTS)
        lgt = carve(9664, TT, EXPERTS)
        eqs = carve(9728, TOPK, EXPERTS)
        sels = carve(9856, TOPK, EXPERTS)
        fullest = carve(9984, 1)
        flagf = carve(9988, PASSES + 1)
        flags = carve(10000, PASSES + 1).bitcast(I32)
        outd = carve(10016, D)
        h_tok = carve(11040, TT, D)
        y_tok = carve(13088, TT, D)

        def carve_moe(at, *shape):
            v = moe_work[:, at:at + math.prod(shape)]
            return v.rearrange("p (a b) -> p a b", b=shape[-1]) if len(shape) == 2 else v

        glu = carve_moe(0, 2, CAP)
        sig = carve_moe(2 * CAP, 2, CAP)
        lin = carve_moe(4 * CAP, 2, CAP)
        eact = carve_moe(6 * CAP, 4, CAP)
        place = carve_moe(10 * CAP, TT, CAP)
        placeT = carve_moe(12 * CAP, TOK)
        hid_tok = carve_moe(12 * CAP + TOK, 2, 2 * P)
        top8 = small[:, 32:40]
        topi = small[:, 40:48].bitcast(U32)
        topf = small[:, 48:52]
        topw = small[:, 52:56]

        ident = konst[:, K_ID:K_ID + P]
        ones = konst[:, K_ONES:K_ONES + P]
        ones_tok = konst[:, K_ONES:K_ONES + TOK]
        causal = konst[:, K_CAUSAL:K_CAUSAL + 384]
        iota = konst[:, K_IOTA:K_IOTA + CAP]
        before = konst[:, K_BEFORE:K_BEFORE + P]
        fold = konst[0:2 * CAP, K_FOLD:K_FOLD + CAP]
        eps_col = {EPS1: konst[:, K_EPS:K_EPS + 1], EPS2: konst[:, K_EPS + 1:K_EPS + 2]}
        one_col = konst[:, K_EPS + 2:K_EPS + 3]
        dseq = konst[:, K_DSEQ:K_DSEQ + 2 * VEC].rearrange("p (a b) -> p a b", b=VEC)
        dch = konst[:, K_DCH:K_DCH + 2 * P].rearrange("p (a b) -> p a b", b=P)
        cosT = konst[0:ROT, K_COS:K_COS + TOK]
        sinT = konst[0:ROT, K_SIN:K_SIN + TOK]
        rotT = konst[0:ROT, K_ROT:K_ROT + ROT]

        def level_mask(i):
            return konst[:, K_LEVEL + i * P:K_LEVEL + (i + 1) * P]

        ff_banks = (0, 1, 3, 0, 1)
        SSUM, DOWN = 2, 4

        tile_landed = [sem(f"tile_landed{i}") for i in range(RING)]
        tile_used = sem("tile_used")
        moe_landed = [sem(f"moe_landed{i}") for i in range(MOE_RING)]
        moe_used = sem("moe_used")
        konst_landed, x_landed, par_landed = sem("konst_landed"), sem("x_landed"), sem("par_landed")
        rel_landed = sem("rel_landed")
        xt_ready = sem("xt_ready")
        vec_ready, vec_taken = sem("vec_ready"), sem("vec_taken")
        rows_written, bias_landed = sem("rows_written"), sem("bias_landed")
        x_ready = sem("x_ready")
        sq_ready, ssum_ready, std_ready, h_ready = (
            sem("sq_ready"), sem("ssum_ready"), sem("std_ready"), sem("h_ready"))
        gu_ready, silu_ready, act_ready = sem("gu_ready"), sem("silu_ready"), sem("act_ready")
        act_made, act_rounded = sem("act_made"), sem("act_rounded")
        h_made, h_rounded = sem("h_made"), sem("h_rounded")
        gate_done, down_done = sem("gate_done"), sem("down_done")
        f_used = (gate_done, gu_ready, down_done)
        f_rounded = [sem(f"f_rounded{i}") for i in range(3)]
        f_split = [sem(f"f_split{i}") for i in range(2)]
        proj_ready, proj_taken = sem("proj_ready"), sem("proj_taken")
        logits_ready, scores_made, max_ready = sem("logits_ready"), sem("scores_made"), sem("max_ready")
        exp_ready, probs_ready = sem("exp_ready"), sem("probs_ready")
        pt_ready, pt_taken = sem("pt_ready"), sem("pt_taken")
        o_ready, o_taken = sem("o_ready"), sem("o_taken")
        osq_ready, ossum_ready, ostd_ready, yc_ready = (
            sem("osq_ready"), sem("ossum_ready"), sem("ostd_ready"), sem("yc_ready"))
        lamdot_ready, lamexp_ready = sem("lamdot_ready"), sem("lamexp_ready")
        dft1_ready, dft1_taken = sem("dft1_ready"), sem("dft1_taken")
        dft2_ready, dft2_taken = sem("dft2_ready"), sem("dft2_taken")
        gates_ready, sig_ready, ys_ready, merged_ready = (
            sem("gates_ready"), sem("sig_ready"), sem("ys_ready"), sem("merged_ready"))
        out_ready = sem("out_ready")
        row_ready, row_taken = sem("row_ready"), sem("row_taken")
        cact_ready, ada_ready = sem("cact_ready"), sem("ada_ready")
        rot_ready, roped = sem("rot_ready"), sem("roped")
        z_ready, zb_ready, sp_ready = sem("z_ready"), sem("zb_ready"), sem("sp_ready")
        diff_ready, decay_ready, k_decayed = sem("diff_ready"), sem("decay_ready"), sem("k_decayed")
        qk_decayed = sem("qk_decayed")
        lev_ready, lev_taken, added, scores_done = (
            sem("lev_ready"), sem("lev_taken"), sem("added"), sem("scores_done"))
        go_ready, go_taken, gla_ready = sem("go_ready"), sem("go_taken"), sem("gla_ready")
        route_ready, top_ready, topexp_ready, wt_ready = (
            sem("route_ready"), sem("top_ready"), sem("topexp_ready"), sem("wt_ready"))
        wtT_ready, wtT_taken = sem("wtT_ready"), sem("wtT_taken")
        htok_ready, htok_taken = sem("htok_ready"), sem("htok_taken")
        ranks_ready, flags_ready, bias_sums_ready = sem("ranks_ready"), sem("flags_ready"), sem("bias_sums_ready")
        place_ready, xg_ready, xg_taken = sem("place_ready"), sem("xg_ready"), sem("xg_taken")
        placeT_ready, placeT_taken = sem("placeT_ready"), sem("placeT_taken")
        whi_ready, wlo_ready, xhi_ready = sem("whi_ready"), sem("wlo_ready"), sem("xhi_ready")
        w_used, htok_copied = sem("w_used"), sem("htok_copied")
        hid_ready, glu_ready, esig_ready, eact_ready = (
            sem("hid_ready"), sem("glu_ready"), sem("esig_ready"), sem("eact_ready"))
        eout_ready, eout_taken = sem("eout_ready"), sem("eout_taken")
        scat_ready, scat_added, y_ready = sem("scat_ready"), sem("scat_added"), sem("y_ready")
        yT_ready = sem("yT_ready")
        ytok_ready, ytok_taken, stored = (
            sem("ytok_ready"), sem("ytok_taken"), sem("stored"))
        act_step, dve_step, moe_step = sem("act_step"), sem("dve_step"), sem("moe_step")

        class Steps:

            def __init__(self, eng, sem):
                self.eng, self.sem, self.base, self.k = eng, sem, 0, 0

            def __call__(self, ins):
                ins.then_inc(self.sem, 1)
                self.k += 1
                self.eng.wait_ge(self.sem, self.base + self.k)

        class Blocks:

            def __init__(self, pe, l, tile):
                self.pe, self.l, self.first, self.n = pe, l, tile * TILE_BLOCKS, tile * TILE_BLOCKS
                self.taken = 0

            def take(self, k=1):
                t, b = divmod(self.n, TILE_BLOCKS)
                if b == 0:
                    self.pe.wait_ge(tile_landed[t % RING], (self.l * GROUPS + t // RING + 1) * 16)
                assert b + k <= TILE_BLOCKS
                self.n += k
                self.taken = k
                return ring[:, t % RING, b * P:(b + k) * P]

            def used(self, mm):
                start = self.n - self.taken
                if start % TILE_BLOCKS == 0 and start > self.first:
                    mm.then_inc(tile_used, 1)
                return mm

        def f_raw(t0, i, k):
            return ring[:, (t0 + i) % RING, k * UNIT:(k + 1) * UNIT]

        def f_count(l, f, i, g=0):
            return l * (2 * FF_TILES) + g * 5 + (f * FF_TILES + i + 1)

        def slot(j):
            return ring[:, j, :] if j < RING else moe_hi[:, j - RING, :]

        block = ctx.enter_context(nc.Block())

        @block.sync
        def _(sp):
            sp.dma_start(x_tok[:, :, :], x_in.rearrange("(t p) d -> p t d", p=P)).then_inc(x_landed, 16)
            sp.wait_ge(konst_landed, 16)
            sp.wait_ge(rel_landed, 2 * 16)
            for s in range(RING):
                if s == RING - 2:
                    sp.wait_ge(rows_written, 16)
                sp.dma_start(ring[:, s, :], stream[s]).then_inc(tile_landed[s], 16)
            whole = DENSE_TILES // RING
            with sp.Fori(1, whole) as g:
                for s in range(RING):
                    sp.wait_ge(tile_used, g * RING + (s + 1 - RING))
                    sp.dma_start(ring[:, s, :], stream[g * RING + s]).then_inc(tile_landed[s], 16)
            for s in range(DENSE_TILES - whole * RING):
                sp.wait_ge(tile_used, (whole - 1) * RING + s + 1)
                sp.dma_start(ring[:, s, :], stream[whole * RING + s]).then_inc(tile_landed[s], 16)

            sp.wait_ge(tile_used, DENSE_TILES)
            for j in range(MOE_RING):
                if j == RING:
                    sp.wait_ge(x_ready, 1 + LAYERS * NORMS + 2)
                sp.dma_start(slot(j), experts[j]).then_inc(moe_landed[j], 16)
            sp.wait_ge(flags_ready, 1)
            with sp.Fori(0, PASSES) as p:
                needed = sp.value_load(flags[0:1, bass.ds(p, 1)], min_val=0, max_val=1)
                with sp.If(needed > 0):
                    with sp.Fori(1, EXPERTS) as e:
                        for j in range(MOE_RING):
                            sp.wait_ge(moe_used, p * (EXPERTS * DC) + e * DC + (j + 1 - DC))
                            sp.dma_start(slot(j), experts[e * DC + j]).then_inc(moe_landed[j], 16)
                again = sp.value_load(flags[0:1, bass.ds(p + 1, 1)], min_val=0, max_val=1)
                with sp.If(again > 0):
                    for j in range(MOE_RING):
                        sp.wait_ge(moe_used, p * (EXPERTS * DC) + (EXPERTS * DC - DC + j + 1))
                        sp.dma_start(slot(j), experts[j]).then_inc(moe_landed[j], 16)
            sp.wait_ge(ytok_taken, 2 * OUTS)
            sp.dma_start(out.rearrange("(t p) d -> p t d", p=P), y_tok[:, :, :]).then_inc(stored, 16)
            sp.wait_ge(stored, 16)

        @block.gpsimd
        def _(pool):
            pool.dma_start(konst[:, :], konst_in).then_inc(konst_landed, 16)
            pool.dma_start(relb[0:BUCKETS + 1], relb_in).then_inc(rel_landed, 16)
            pool.dma_start(onehot[0:BUCKETS + 1], onehot_in).then_inc(rel_landed, 16)
            pool.dma_start(lp_all[:, :, :], layer_in).then_inc(par_landed, 16)
            pool.dma_start(cols[:, :], cols_in).then_inc(par_landed, 16)
            pool.dma_start(glaw[:, :], glaw_in).then_inc(par_landed, 16)
            pool.dma_start(router[:, :, :], router_in).then_inc(par_landed, 16)
            pool.dma_start(brouter[:, :], brouter_in).then_inc(par_landed, 16)
            pool.dma_start(bout[:, :], bout_in).then_inc(par_landed, 16)
            pool.wait_ge(vec_taken, BIAS_HEADS)
            pool.dma_start(bias_rows.rearrange("h p v -> p h v"), vecs[:, :, :]).then_inc(rows_written, 16)
            pool.wait_ge(rows_written, 16)
            for qt in range(TT):
                skew = bass.AP(bias_rows.tensor, (TOK - 1) - qt * P,
                               [[VEC - 1, P], [P * VEC, BIAS_HEADS], [1, TOK]])
                pool.dma_start(bias[:, :, qt, :], skew).then_inc(bias_landed, 16)

            for v in range(len(LEVELS) + 1):
                pool.wait_ge(decay_ready, v + 1)
                if v > 1:
                    pool.wait_ge(lev_ready, (v - 2) * TT + 1)
                pool.tensor_tensor(kd[v % 2], gqk[:, GLA_HEADS:, :],
                                   expd.rearrange("p (h t) -> p h t", t=TOK), ALU.mult).then_inc(k_decayed, 1)

        @block.scalar
        def _(a):
            step = Steps(a, act_step)

            def f_round(l, f, t0, i, k, g=0):
                if k == 0 or i == 0:
                    t = t0 + i
                    a.wait_ge(tile_landed[t % RING], (l * GROUPS + g + t // RING + 1) * 16)
                if i > 0:
                    a.wait_ge(f_used[k], f_count(l, f, i - 1, g))
                nc.scalar.activation(f_hi[k], f_raw(t0, i, k), ACT.Copy).then_inc(f_rounded[k], 1)

            def norm(l, n, eps, scale=1.0 / D, ffn_tile0=None):
                a.wait_ge(x_ready, l * NORMS + n + 1)
                for half in (slice(0, DC // 2), slice(DC // 2, DC)):
                    nc.scalar.activation(sq[:, half, :], x[:, half, :], ACT.Square).then_inc(sq_ready, 1)
                if ffn_tile0 is not None:
                    for k in range(2):
                        f_round(l, n // 2, ffn_tile0, 0, k)
                a.wait_ge(ssum_ready, l * NORMS + n + 1)
                nc.scalar.activation(std[:, 0:TOK], ps[:, SSUM, 0:TOK], ACT.Sqrt, bias=eps_col[eps],
                                     scale=scale).then_inc(std_ready, 1)

            def ffn_tile(l, f, t0, i, g=0, last=False):
                s = (i - 1) % 5
                if not last:
                    f_round(l, f, t0, i + 1, 0, g)
                a.wait_ge(gu_ready, f_count(l, f, i, g))
                nc.scalar.activation(silu[:, s, :], ps[:, ff_banks[s], 0:TOK], ACT.Silu).then_inc(silu_ready, 1)
                if not last:
                    f_round(l, f, t0, i + 1, 1, g)
                f_round(l, f, t0, i, 2, g)

            def ffn(l, f, t0):
                for i in range(2):
                    a.wait_ge(h_made, l * 4 + (2 * f + i + 1))
                    nc.scalar.activation(h_hi[:, 4 * i:4 * i + 4, :], h[:, 4 * i:4 * i + 4, :], ACT.Copy).then_inc(h_rounded, 1)
                ffn_tile(l, f, t0, 0)
                with a.Fori(0, (FF_TILES - 2) // 5) as g:
                    for s in range(5):
                        ffn_tile(l, f, t0, 1 + s, g)
                ffn_tile(l, f, t0, FF_TILES - 1, last=True)

            for i in range(BIAS_HEADS):
                a.wait_ge(vec_ready, i + 1)
                nc.scalar.activation(vecs[:, i, :], ps[:, i % 4, :], ACT.Copy).then_inc(vec_taken, 1)
            a.wait_ge(par_landed, 6 * 16)
            nc.scalar.activation(small[:, 16:24], cols[:, C_X:C_X + DC], ACT.Silu).then_inc(cact_ready, 1)

            with a.Fori(0, LAYERS) as l:
                norm(l, 0, EPS1, ffn_tile0=0)
                ffn(l, 0, 0)
                norm(l, 1, EPS1)
                a.wait_ge(lamdot_ready, l + 1)
                nc.scalar.activation(small[:, 2:4], small[:, 0:2], ACT.Exp).then_inc(lamexp_ready, 1)

                def take_proj(r):
                    a.wait_ge(proj_ready, l * PROJ + r + 1)
                    bank = ps[:, r % 4, :]
                    if r < 7:
                        dst = qk[:, 2 * r:2 * r + 2, :]
                        bank = bank.rearrange("p (a b) -> p a b", b=TOK)
                    elif r < 9:
                        dst = vc[:, r - 7, :]
                    elif r < 11:
                        dst, bank = vb[:, r - 9, :], ps[:, r % 4, 0:384]
                    else:
                        dst = a_tok[:, (r - 11) % 2, (r - 11) // 2 * 512:(r - 11) // 2 * 512 + 512]
                    nc.scalar.activation(dst, bank, ACT.Copy).then_inc(proj_taken, 1)

                for r in range(11):
                    take_proj(r)

                def exps(u):
                    a.wait_ge(max_ready, l * UNITS + u + 1)
                    cm, cs, su = C_MAX[u % 3], C_SUM[u % 3], S[u % 3]
                    if u < DIL_UNITS:
                        nc.scalar.activation(su, su, ACT.Exp, bias=small[:, cm:cm + 1], accum_out=small[:, cs:cs + 1]).then_inc(exp_ready, 1)
                    else:
                        for m in range(2):
                            half = su[:, m * TOK:(m + 1) * TOK]
                            e = nc.scalar.activation(half, half, ACT.Exp, bias=small[:, cm + m:cm + m + 1], accum_out=small[:, cs + m:cs + m + 1])
                        e.then_inc(exp_ready, 1)

                def take_pt(u):
                    a.wait_ge(pt_ready, l * UNITS + u + 1)
                    n = 768 if u < DIL_UNITS else 256
                    nc.scalar.activation(PT[:, u % 2, 0:n], ps[:, 4:6, :].rearrange("p a b -> p (a b)")[:, 0:n],
                                         ACT.Copy).then_inc(pt_taken, 1)

                def take_o(i):
                    a.wait_ge(o_ready, l * 5 + i + 1)
                    if i == 0:
                        nc.scalar.activation(ob[:, :], ps[:, 6, 0:TOK], ACT.Copy).then_inc(o_taken, 1)
                    else:
                        hh = i - 1
                        nc.scalar.activation(oc[:, hh, :], ps[:, 7 - hh % 2, 0:TOK], ACT.Copy).then_inc(o_taken, 1)

                for u in range(UNITS + 3):
                    if u < UNITS:
                        exps(u)
                    if 2 <= u < UNITS + 2:
                        take_pt(u - 2)
                    if u >= 3:
                        w = u - 3
                        if w == DIL_UNITS - 1:
                            take_o(0)
                        if w >= DIL_UNITS and w % 2 == 1:
                            take_o(1 + (w - DIL_UNITS) // 2)
                a.wait_ge(o_taken, l * 5 + 5)
                nc.scalar.activation(sq[:, 0:4, :], oc[:, :, :], ACT.Square).then_inc(osq_ready, 1)
                for r in range(11, PROJ):
                    take_proj(r)
                a.wait_ge(ossum_ready, l + 1)
                nc.scalar.activation(std[:, :], ps[:, 6:8, :].rearrange("p a b -> p (a b)"), ACT.Sqrt, bias=eps_col[SUBLN_EPS],
                                     scale=1.0 / P).then_inc(ostd_ready, 1)
                for g in range(FOURIER_GROUPS):
                    a.wait_ge(dft1_ready, l * FOURIER_GROUPS + g + 1)
                    nc.scalar.activation(dft1[:, g % 2, :], ps[:, g % 2, :], ACT.Copy).then_inc(dft1_taken, 1)
                for m in range(DC):
                    a.wait_ge(gates_ready, l * DC + m + 1)
                    if m >= 2:
                        a.wait_ge(merged_ready, l * DC + m - 1)
                    b0 = 4 * (1 - m % 2)
                    for j in range(3):
                        c = LP_BGATE + j * DC + m
                        e = nc.scalar.activation(sg[:, m % 2, j, :], ps[:, b0 + j // 2, j % 2 * TOK:(j % 2 + 1) * TOK], ACT.Sigmoid, bias=lp[:, c:c + 1])
                    e.then_inc(sig_ready, 1)
                norm(l, 2, EPS1, ffn_tile0=FFN2)
                ffn(l, 1, FFN2)

            norm(LAYERS, 0, EPS1)
            for g in range(ADA // 4):
                a.wait_ge(row_ready, g + 1)
                nc.scalar.activation(row[0:1, g % 2, :], ps[0:1, g % 2, :], ACT.Copy).then_inc(row_taken, 1)
            norm(LAYERS, 1, EPS2)

            def take_proj2(r):
                a.wait_ge(proj_ready, LAYERS * PROJ + r + 1)
                bank = ps[:, r % 4, :]
                pair = bank.rearrange("p (a b) -> p a b", b=TOK)
                if r < 4:
                    op = nc.scalar.activation(mv[:, r % 2, r // 2 * 512:r // 2 * 512 + 512], bank, ACT.Copy)
                elif r < 12:
                    op = nc.scalar.activation(mqk[:, 2 * (r - 4):2 * (r - 4) + 2, :], pair, ACT.Copy)
                elif r < 14:
                    op = nc.scalar.activation(gqk[:, 2 * (r - 12):2 * (r - 12) + 2, :], pair, ACT.Copy, scale=float(P) ** -0.5)
                elif r < 16:
                    op = nc.scalar.activation(gqk[:, 2 * (r - 12):2 * (r - 12) + 2, :], pair, ACT.Copy)
                elif r == 16:
                    op = nc.scalar.activation(glow[0:RANK, :], ps[0:RANK, r % 4, 0:TOK], ACT.Copy)
                elif r < 21:
                    op = nc.scalar.activation(gr[:, 2 * (r - 17):2 * (r - 17) + 2, :], pair, ACT.Silu)
                else:
                    op = nc.scalar.activation(gv[:, (r - 21) % 2, (r - 21) // 2 * 512:(r - 21) // 2 * 512 + 512], bank, ACT.Copy)
                op.then_inc(proj_taken, 1)

            for r in range(12):
                take_proj2(r)

            U0 = LAYERS * UNITS

            def exps2(u):
                a.wait_ge(max_ready, U0 + u + 1)
                for m, (lo, hi) in enumerate(((0, 128), (128, 384))):
                    cm, cs, part = C_MAX[u % 3] + m, C_SUM[u % 3] + m, mS[u % 3][:, lo:hi]
                    e = nc.scalar.activation(part, part, ACT.Exp, bias=small[:, cm:cm + 1], accum_out=small[:, cs:cs + 1])
                e.then_inc(exp_ready, 1)

            for u in range(HEADS + 3):
                if u < HEADS:
                    exps2(u)
                if 2 <= u < HEADS + 2:
                    a.wait_ge(pt_ready, U0 + u - 1)
                    nc.scalar.activation(mPT[:, u % 2, :], ps[:, 4, 0:384], ACT.Copy).then_inc(pt_taken, 1)
                if u >= 3:
                    a.wait_ge(o_ready, LAYERS * 5 + u - 2)
                    nc.scalar.activation(oa[:, u - 3, :], ps[:, 6 + (u - 3) % 2, 0:TOK], ACT.Copy).then_inc(o_taken, 1)
            for r in range(12, 25):
                take_proj2(r)
            a.wait_ge(zb_ready, 1)
            step(nc.scalar.activation(gtmp[:, :], lg.rearrange("p h t -> p (h t)"), ACT.Abs))
            step(nc.scalar.activation(gtmp[:, :], gtmp[:, :], ACT.Exp, scale=-1.0))
            nc.scalar.activation(gtmp[:, :], gtmp[:, :], ACT.Ln, bias=one_col).then_inc(sp_ready, 1)
            for v in range(len(LEVELS) + 1):
                a.wait_ge(diff_ready, v + 1)
                if v > 0:
                    a.wait_ge(k_decayed, v)
                    a.wait_ge(qk_decayed, v)
                nc.scalar.activation(expd[:, :], gtmp[:, :], ACT.Exp, scale=1.0 / 16).then_inc(decay_ready, 1)
            for i in range(OUTS):
                a.wait_ge(go_ready, i + 1)
                nc.scalar.activation(go[:, 2 * i:2 * i + 2, :], ps[:, 4 + i, :].rearrange("p (a b) -> p a b", b=TOK),
                                     ACT.Copy).then_inc(go_taken, 1)
            a.wait_ge(go_taken, OUTS)
            nc.scalar.activation(sq[:, :, :], go[:, :, :], ACT.Square).then_inc(osq_ready, 1)
            a.wait_ge(ossum_ready, LAYERS + 1)
            nc.scalar.activation(std[:, :], ps[:, 0:2, :].rearrange("p a b -> p (a b)"), ACT.Sqrt, bias=eps_col[EPS2],
                                 scale=1.0 / GLA_DV).then_inc(ostd_ready, 1)
            for m in range(DC):
                a.wait_ge(gates_ready, LAYERS * DC + m + 1)
                if m >= 2:
                    a.wait_ge(merged_ready, LAYERS * DC + m - 1)
                for j in range(2):
                    c = C_BMERGE + j * DC + m
                    e = nc.scalar.activation(sg2[:, m % 2, j, :], ps[:, 2 + 2 * (m % 2), j * TOK:(j + 1) * TOK], ACT.Sigmoid,
                                             bias=cols[:, c:c + 1])
                e.then_inc(sig_ready, 1)
            norm(LAYERS, 2, EPS2)
            for t in range(TT):
                a.wait_ge(top_ready, t + 1)
                nc.scalar.activation(topw, top8[:, 0:TOPK], ACT.Exp, bias=small[:, 56:57],
                                     accum_out=small[:, 57:58]).then_inc(topexp_ready, 1)
            for i in range(2 * TT):
                a.wait_ge(htok_ready, i + 1)
                nc.scalar.activation(h_tok[:, i // 2, i % 2 * 512:i % 2 * 512 + 512], ps[:, 4 + i, :], ACT.Copy).then_inc(htok_taken, 1)

            def take_tokens(n):
                a.wait_ge(xg_ready, n)
                nc.scalar.activation(xg[:, :, 0, :], ps[:, 2, 0:DC * CAP].rearrange("p (a b) -> p a b", b=CAP), ACT.Copy).then_inc(xhi_ready, 1)

            def round_weights(n, j, first=False):
                a.wait_ge(moe_landed[j], n * 16 + 16)
                for half in range(2):
                    u = 2 * j + half
                    if not first:
                        a.wait_ge(w_used, n * UNITS_E + (u + 1 - W_UNITS))
                    nc.scalar.activation(w_hi[u % W_UNITS], slot(j)[:, half * UNIT:(half + 1) * UNIT], ACT.Copy).then_inc(whi_ready, 1)

            def take_hidden(n, j):
                a.wait_ge(w_used, n * UNITS_E + 2 * (j + 1))
                nc.scalar.activation(hid_tok[0:2 * CAP, j % 2, :], ps[0:2 * CAP, j % 2, 0:2 * P], ACT.Copy).then_inc(htok_copied, 1)

            def take_places(n):
                a.wait_ge(placeT_ready, n + 1)
                nc.scalar.activation(placeT[0:CAP, :], ps[0:CAP, 2, 0:TOK], ACT.Copy).then_inc(placeT_taken, 1)

            def take_out(n):
                for half in range(2):
                    if half == 0:
                        a.wait_ge(eout_ready, n + 1)
                    else:
                        a.wait_ge(moe_used, n * DC + DC)
                    nc.scalar.activation(outd[0:CAP, half * 512:half * 512 + 512], ps[0:CAP, 4 + half, :], ACT.Copy).then_inc(eout_taken, 1)

            def expert_step(n, j, after=False, last=False):
                if j + 2 < DC:
                    round_weights(n, j + 2)
                elif not last:
                    round_weights(n + 1, j + 2 - DC)
                if j == DC - 2 and not last:
                    take_tokens(n + 2)
                if j == HALF + 1 and not last:
                    take_places(n)
                if j + 1 < DC:
                    take_hidden(n, j + 1)
                elif not last:
                    take_hidden(n + 1, 0)
                if j == 0 and after:
                    take_out(n - 1)
                a.wait_ge(glu_ready, n * DC + (j + 1))
                nc.scalar.activation(sig[:, j % 2, :], glu[:, j % 2, :], ACT.Sigmoid, scale=ALPHA).then_inc(esig_ready, 1)
                if j == HALF and last:
                    take_places(n)

            a.wait_ge(flags_ready, 1)
            with a.Fori(0, PASSES) as p:
                needed = a.value_load(flags[0:1, bass.ds(p, 1)], min_val=0, max_val=1)
                with a.If(needed > 0):
                    n = p * EXPERTS
                    round_weights(n, 0, True)
                    take_tokens(n + 1)
                    round_weights(n, 1, True)
                    take_hidden(n, 0)
                    for j in range(HALF):
                        expert_step(n, j)
                    with a.Fori(0, EXPERTS - 1) as e:
                        for j in range(HALF, DC):
                            expert_step(p * EXPERTS + e, j)
                        for j in range(HALF):
                            expert_step(p * EXPERTS + e + 1, j, after=True)
                    for j in range(HALF, DC):
                        expert_step(n + (EXPERTS - 1), j, last=True)
                    take_out(n + (EXPERTS - 1))
            norm(LAYERS, 3, EPS2)
            for i in range(2 * OUTS):
                t, half = divmod(i, OUTS)
                a.wait_ge(ytok_ready, i + 1)
                nc.scalar.activation(y_tok[:, t, half * 256:half * 256 + 256], ps[:, i % 4, 0:256],
                                     ACT.Copy).then_inc(ytok_taken, 1)

        @block.vector
        def _(v):
            step = Steps(v, dve_step)

            def add_level(i):
                for t in range(TT):
                    n = 1 + (i - 1) * TT + t
                    v.wait_ge(lev_ready, n + 1)
                    sc = ps[:, 2 * (i % 2) + t, :].rearrange("p (h t) -> p h t", t=P)
                    mask = level_mask(i - 1).unsqueeze(1).to_broadcast([P, GLA_HEADS, P])
                    dst = acc[:, t, :, :] if i == 1 else tmp[:, :, :]
                    nc.vector.tensor_tensor(dst, sc, mask, ALU.mult).then_inc(lev_taken, 1)
                    v.wait_ge(lev_taken, n + 1)
                    if i > 1:
                        op = nc.vector.tensor_tensor(acc[:, t, :, :], acc[:, t, :, :], tmp[:, :, :], ALU.add)
                        if i == len(LEVELS) + 1 and t == TT - 1:
                            op.then_inc(scores_done, 1)
                        else:
                            step(op)

            def recip_std(l, n):
                v.wait_ge(std_ready, l * NORMS + n + 1)
                step(nc.vector.reciprocal(rstd[:, 0:TOK], std[:, 0:TOK]))

            def f_sub(l, f, t0, i, k, g=0):
                v.wait_ge(f_rounded[k], f_count(l, f, i, g))
                return nc.vector.tensor_tensor(f_lo[k], f_raw(t0, i, k), f_hi[k].bitcast(F32), ALU.subtract)

            def ffn_norm(l, f, t0, gain):
                for k in range(2):
                    f_sub(l, f, t0, 0, k).then_inc(f_split[k], 1)
                recip_std(l, 2 * f)
                for c in range(DC):
                    op = nc.vector.scalar_tensor_tensor(out=h[:, c, :], in0=x[:, c, :], scalar=gain[:, c:c + 1],
                                                        in1=rstd[:, 0:TOK], op0=ALU.mult, op1=ALU.mult)
                    if c % 4 == 3:
                        op.then_inc(h_made, 1)
                for i in range(2):
                    cs = slice(4 * i, 4 * i + 4)
                    v.wait_ge(h_rounded, l * 4 + (2 * f + i + 1))
                    nc.vector.tensor_tensor(h_lo[:, cs, :], h[:, cs, :], h_hi[:, cs, :].bitcast(F32), ALU.subtract).then_inc(h_ready, 1)

            def norm(l, n, gain, out=None, half_ready=False):
                recip_std(l, n)
                for c in range(DC):
                    op = nc.vector.scalar_tensor_tensor(out=(h if out is None else out)[:, c, :], in0=x[:, c, :], scalar=gain[:, c:c + 1],
                                                        in1=rstd[:, 0:TOK], op0=ALU.mult, op1=ALU.mult)
                    if half_ready and c % (DC // 2) == DC // 2 - 1:
                        op.then_inc(h_ready, 1)
                return op

            def ffn_tile(l, f, t0, i, g=0, last=False):
                s = (i - 1) % 5
                hi, lo = act_hi[:, s % 3, :], act_lo[:, s % 3, :]
                if not last:
                    f_sub(l, f, t0, i + 1, 0, g).then_inc(f_split[0], 1)
                v.wait_ge(silu_ready, f_count(l, f, i, g))
                nc.vector.tensor_tensor(act[:, s, :], silu[:, s, :], ps[:, ff_banks[s], TOK:2 * TOK],
                                        ALU.mult).then_inc(act_made, 1)
                if not last:
                    f_sub(l, f, t0, i + 1, 1, g).then_inc(f_split[1], 1)
                v.wait_ge(act_made, f_count(l, f, i, g))
                nc.vector.tensor_copy(hi, act[:, s, :]).then_inc(act_rounded, 1)
                v.wait_ge(act_rounded, f_count(l, f, i, g))
                nc.vector.tensor_tensor(lo, act[:, s, :], hi.bitcast(F32), ALU.subtract).then_inc(act_ready, 1)
                f_sub(l, f, t0, i, 2, g).then_inc(tile_used, 1)

            def ffn(l, f, t0):
                ffn_tile(l, f, t0, 0)
                with v.Fori(0, (FF_TILES - 2) // 5) as g:
                    for s in range(5):
                        ffn_tile(l, f, t0, 1 + s, g)
                ffn_tile(l, f, t0, FF_TILES - 1, last=True)
                v.wait_ge(down_done, f_count(l, f, FF_TILES - 1))
                for b in range(OUTS):
                    xs = x[:, 2 * b:2 * b + 2, :]
                    op = nc.vector.scalar_tensor_tensor(out=xs, in0=ps[:, DOWN + b, :].rearrange("p (a b) -> p a b", b=TOK), scalar=0.5,
                                                        in1=xs, op0=ALU.mult, op1=ALU.add)
                op.then_inc(x_ready, 1)

            for i in range(OUTS):
                v.wait_ge(xt_ready, i + 1)
                op = nc.vector.tensor_copy(x[:, 2 * i:2 * i + 2, :], ps[:, 4 + i, :].rearrange("p (a b) -> p a b", b=TOK))
            op.then_inc(x_ready, 1)
            v.wait_ge(par_landed, 6 * 16)
            v.wait_ge(konst_landed, 16)

            first_k = step.k
            with v.Fori(0, LAYERS) as l:
                step.base = l * LAYER_STEPS
                step(nc.vector.tensor_copy(lp[:, :], lp_all[:, l, :]))
                for i in range(2):
                    q = lp[:, LP_LAM + i * 2 * DH:LP_LAM + i * 2 * DH + DH]
                    k = lp[:, LP_LAM + i * 2 * DH + DH:LP_LAM + (i + 1) * 2 * DH]
                    op = nc.vector.tensor_tensor_reduce(rstd[:, 512 + i * DH:512 + (i + 1) * DH], q, k, 1.0, 0.0, ALU.mult, ALU.add, small[:, i:i + 1])
                op.then_inc(lamdot_ready, 1)
                step(nc.vector.tensor_scalar(small[:, 6:7], lp[:, LP_SUBLN:LP_SUBLN + 1], lp[:, LP_LAMI + 1:LP_LAMI + 2], None, ALU.mult))
                ffn_norm(l, 0, 0, lp[:, LP_FFN1:LP_FFN1 + DC])
                ffn(l, 0, 0)
                norm(l, 1, lp[:, LP_MIX:LP_MIX + DC], half_ready=True)
                v.wait_ge(lamexp_ready, l + 1)
                step(nc.vector.tensor_scalar(small[:, 5:6], small[:, 2:3], lp[:, LP_LAMI:LP_LAMI + 1], None, ALU.add))
                step(nc.vector.tensor_tensor(small[:, 4:5], small[:, 3:4], small[:, 5:6], ALU.subtract))
                v.wait_ge(bias_landed, TT * 16)

                def scores(u):
                    v.wait_ge(logits_ready, l * UNITS + u + 1)
                    if u >= 3:
                        v.wait_ge(pt_ready, l * UNITS + u - 2)
                    b = 2 * (u % 2)
                    if u < DIL_UNITS:
                        slot, qt = divmod(u, TT)
                        lo = ps[:, b:b + 2, :].rearrange("p a b -> p (a b)")[:, 0:768].rearrange("p (a b) -> p a b", b=TOK)
                        bi = bias[:, slot:slot + 5:2, qt, :]
                        dst = S[u % 3].rearrange("p (a b) -> p a b", b=TOK)
                    else:
                        hh, qt = divmod(u - DIL_UNITS, TT)
                        lo = ps[:, b:b + 2, 0:TOK]
                        bi = bias[:, 6 + hh, qt, :].unsqueeze(1).to_broadcast([P, 2, TOK])
                        dst = S[u % 3][:, 0:512].rearrange("p (a b) -> p a b", b=TOK)
                    nc.vector.scalar_tensor_tensor(out=dst, in0=lo, scalar=DH ** -0.5, in1=bi, op0=ALU.mult,
                                                   op1=ALU.add).then_inc(scores_made, 1)
                    v.wait_ge(scores_made, l * UNITS + u + 1)
                    c = C_MAX[u % 3]
                    if u < DIL_UNITS:
                        op = nc.vector.tensor_reduce(small[:, c:c + 1], S[u % 3], AX.X, ALU.max, negate=True)
                    else:
                        op = nc.vector.tensor_reduce(small[:, c:c + 2], dst, AX.X, ALU.max, negate=True)
                    op.then_inc(max_ready, 1)

                def probs(u):
                    v.wait_ge(exp_ready, l * UNITS + u + 1)
                    cs, cr, su = C_SUM[u % 3], C_REC[u % 3], S[u % 3]
                    if u < DIL_UNITS:
                        step(nc.vector.reciprocal(small[:, cr:cr + 1], small[:, cs:cs + 1]))
                        op = nc.vector.tensor_scalar(su, su, small[:, cr:cr + 1], None, ALU.mult)
                    else:
                        step(nc.vector.reciprocal(small[:, cr:cr + 2], small[:, cs:cs + 2]))
                        step(nc.vector.tensor_scalar(su[:, TOK:512], su[:, TOK:512], small[:, cr + 1:cr + 2], small[:, 4:5], ALU.mult, ALU.mult))
                        op = nc.vector.scalar_tensor_tensor(out=su[:, 0:TOK], in0=su[:, 0:TOK], scalar=small[:, cr:cr + 1],
                                                            in1=su[:, TOK:512], op0=ALU.mult, op1=ALU.add)
                    op.then_inc(probs_ready, 1)

                for u in range(UNITS + 1):
                    if u < UNITS:
                        scores(u)
                    if u >= 1:
                        probs(u - 1)
                v.wait_ge(ostd_ready, l + 1)
                step(nc.vector.reciprocal(rstd[:, :], std[:, :]))
                for hh in range(DIFF_HEADS):
                    op = nc.vector.scalar_tensor_tensor(out=oc[:, hh, :], in0=oc[:, hh, :], scalar=small[:, 6:7],
                                                        in1=rstd[:, hh * TOK:(hh + 1) * TOK], op0=ALU.mult, op1=ALU.mult)
                op.then_inc(yc_ready, 1)
                for g in range(FOURIER_GROUPS):
                    v.wait_ge(dft2_ready, l * FOURIER_GROUPS + g + 1)
                    nc.vector.tensor_copy(four[:, g, :], ps[:, 2 + g % 2, 0:TOK]).then_inc(dft2_taken, 1)
                for m in range(DC):
                    v.wait_ge(sig_ready, l * DC + m + 1)
                    v.wait_ge(ys_ready, l * DC + m + 1)
                    b0 = 4 * (1 - m % 2) + 2
                    branches = ps[:, b0:b0 + 2, :].rearrange("p a b -> p (a b)")[:, 0:3 * TOK].rearrange("p (a b) -> p a b", b=TOK)
                    step(nc.vector.tensor_tensor(sg[:, m % 2, :, :], sg[:, m % 2, :, :], branches, ALU.mult))
                    step(nc.vector.tensor_tensor(sg[:, m % 2, 0, :], sg[:, m % 2, 0, :], sg[:, m % 2, 1, :], ALU.add))
                    nc.vector.tensor_tensor(merged[:, m, :], sg[:, m % 2, 0, :], sg[:, m % 2, 2, :], ALU.add).then_inc(merged_ready, 1)
                for b in range(OUTS):
                    v.wait_ge(out_ready, l * OUTS + b + 1)
                    xs = x[:, 2 * b:2 * b + 2, :]
                    op = nc.vector.tensor_tensor(xs, xs, ps[:, DOWN + b, :].rearrange("p (a b) -> p a b", b=TOK), ALU.add)
                op.then_inc(x_ready, 1)
                ffn_norm(l, 1, FFN2, lp[:, LP_FFN2:LP_FFN2 + DC])
                ffn(l, 1, FFN2)
            assert step.k - first_k == LAYER_STEPS, step.k - first_k
            step.base = LAYERS * LAYER_STEPS
            step.k = first_k

            norm(LAYERS, 0, cols[:, C_GFIN:C_GFIN + DC], out=x).then_inc(x_ready, 1)
            v.wait_ge(ada_ready, 1)
            step(nc.vector.tensor_tensor(mod[:, :], ps[:, 3, 0:ADA], cols[:, C_BADA:C_BADA + ADA], ALU.add))
            for n, (sc, w) in enumerate(((DC, C_N1), (4 * DC, C_N2))):
                step(nc.vector.scalar_tensor_tensor(out=modgain[:, n * DC:(n + 1) * DC], in0=mod[:, sc:sc + DC], scalar=1.0,
                                                    in1=cols[:, w:w + DC], op0=ALU.add, op1=ALU.mult))

            def mod_norm(n, i):
                step(norm(LAYERS, n, modgain[:, i * DC:(i + 1) * DC]))
                shift = mod[:, 3 * i * DC:(3 * i + 1) * DC]
                for half in (slice(0, DC // 2), slice(DC // 2, DC)):
                    nc.vector.tensor_tensor(h[:, half, :], h[:, half, :], shift[:, half].unsqueeze(2).to_broadcast([P, DC // 2, TOK]),
                                            ALU.add).then_inc(h_ready, 1)

            mod_norm(1, 0)
            for i in range(HEADS):
                v.wait_ge(rot_ready, i + 1)
                qs = mqk[0:ROT, 2 * i:2 * i + 2, :]
                rp = ps[0:ROT, 4 + i % 2, :].rearrange("p (a b) -> p a b", b=TOK)
                rt = rstd[0:ROT, 512:1024].rearrange("p (a b) -> p a b", b=TOK)
                step(nc.vector.tensor_tensor(rt, rp, sinT.unsqueeze(1).to_broadcast([ROT, 2, TOK]), ALU.mult))
                step(nc.vector.tensor_tensor(qs, qs, cosT.unsqueeze(1).to_broadcast([ROT, 2, TOK]), ALU.mult))
                nc.vector.tensor_tensor(qs, qs, rt, ALU.add).then_inc(roped, 1)
                v.wait_ge(roped, i + 1)
            U0 = LAYERS * UNITS
            for u in range(HEADS + 1):
                if u < HEADS:
                    v.wait_ge(logits_ready, U0 + u + 1)
                    if u >= 3:
                        v.wait_ge(pt_ready, U0 + u - 2)
                    nc.vector.scalar_tensor_tensor(out=mS[u % 3], in0=ps[:, u % 2, 0:384], scalar=P ** -0.5, in1=causal,
                                                   op0=ALU.mult, op1=ALU.add).then_inc(scores_made, 1)
                    v.wait_ge(scores_made, U0 + u + 1)
                    c = C_MAX[u % 3]
                    nc.vector.tensor_reduce(small[:, c:c + 1], mS[u % 3][:, 0:128], AX.X, ALU.max, negate=True)
                    nc.vector.tensor_reduce(small[:, c + 1:c + 2], mS[u % 3][:, 128:384], AX.X, ALU.max, negate=True).then_inc(max_ready, 1)
                if u >= 1:
                    w = u - 1
                    cs, cr, su = C_SUM[w % 3], C_REC[w % 3], mS[w % 3]
                    v.wait_ge(exp_ready, U0 + w + 1)
                    step(nc.vector.reciprocal(small[:, cr:cr + 2], small[:, cs:cs + 2]))
                    nc.vector.tensor_scalar(su[:, 0:128], su[:, 0:128], small[:, cr:cr + 1], None, ALU.mult)
                    nc.vector.tensor_scalar(su[:, 128:384], su[:, 128:384], small[:, cr + 1:cr + 2], None, ALU.mult).then_inc(probs_ready, 1)
            v.wait_ge(z_ready, 1)
            for hh in range(GLA_HEADS):
                op = nc.vector.tensor_scalar(lg[:, hh, :], ps[:, 4 + hh // 2, hh % 2 * TOK:(hh % 2 + 1) * TOK], cols[:, C_GLAB + hh:C_GLAB + hh + 1], None, ALU.add)
            op.then_inc(zb_ready, 1)
            v.wait_ge(sp_ready, 1)
            lgf = lg.rearrange("p h t -> p (h t)")
            step(nc.vector.scalar_tensor_tensor(out=lgf, in0=lgf, scalar=0.0, in1=gtmp[:, :], op0=ALU.min, op1=ALU.subtract))
            for hh in range(GLA_HEADS):
                op = nc.vector.tensor_tensor_scan(out=bcum[:, hh * TOK:(hh + 1) * TOK], data0=ones_tok, data1=lg[:, hh, :],
                                                  initial=0.0, op0=ALU.mult, op1=ALU.add)
            step(op)
            for i, s in enumerate((P,) + LEVELS):
                if i > 0:
                    v.wait_ge(decay_ready, i)
                bv = bcum.rearrange("p (n two s) -> p n two s", two=2, s=s)
                gv_ = gtmp.rearrange("p (n two s) -> p n two s", two=2, s=s)
                n = GLA_HEADS * TOK // (2 * s)
                ref = bv[:, :, 0, s - 1:s].to_broadcast([P, n, s])
                nc.vector.tensor_tensor(gv_[:, :, 0, :], ref, bv[:, :, 0, :], ALU.subtract)
                nc.vector.tensor_tensor(gv_[:, :, 1, :], bv[:, :, 1, :], ref, ALU.subtract).then_inc(diff_ready, 1)
                if i == 2:
                    v.wait_ge(lev_ready, 1)
                    nc.vector.tensor_copy(off[:, :, :], ps[:, 0, :].rearrange("p (h t) -> p h t", t=P)).then_inc(lev_taken, 1)
                if i >= 3:
                    add_level(i - 2)
                v.wait_ge(decay_ready, i + 1)
                if i > 1:
                    v.wait_ge(lev_ready, (i - 2) * TT + 1)
                nc.vector.tensor_tensor(qd[i % 2], gqk[:, 0:GLA_HEADS, :], expd.rearrange("p (h t) -> p h t", t=TOK), ALU.mult).then_inc(qk_decayed, 1)
            add_level(len(LEVELS) - 1)
            add_level(len(LEVELS))
            add_level(len(LEVELS) + 1)
            v.wait_ge(ostd_ready, LAYERS + 1)
            step(nc.vector.reciprocal(rstd[:, :], std[:, :]))
            for c in range(DC):
                op = nc.vector.scalar_tensor_tensor(out=go[:, c, :], in0=go[:, c, :], scalar=cols[:, C_GLAN + c % 2:C_GLAN + c % 2 + 1],
                                                    in1=rstd[:, c // 2 * TOK:(c // 2 + 1) * TOK], op0=ALU.mult, op1=ALU.mult)
            step(op)
            nc.vector.tensor_tensor(go[:, :, :], go[:, :, :], gr[:, :, :], ALU.mult).then_inc(gla_ready, 1)
            for m in range(DC):
                v.wait_ge(sig_ready, LAYERS * DC + m + 1)
                v.wait_ge(ys_ready, LAYERS * DC + m + 1)
                b0 = 2 + 2 * (m % 2)
                step(nc.vector.tensor_tensor(sg2[:, m % 2, :, :], sg2[:, m % 2, :, :], ps[:, b0 + 1, :].rearrange("p (a b) -> p a b", b=TOK), ALU.mult))
                nc.vector.tensor_tensor(merged2[:, m, :], sg2[:, m % 2, 0, :], sg2[:, m % 2, 1, :], ALU.add).then_inc(merged_ready, 1)

            def add_gated(c, bank, half, gate):
                g = mod[:, gate * DC + c:gate * DC + c + 1]
                return nc.vector.scalar_tensor_tensor(out=x[:, c, :], in0=ps[:, bank, half * TOK:(half + 1) * TOK], scalar=g,
                                                      in1=x[:, c, :], op0=ALU.mult, op1=ALU.add)

            for b in range(OUTS):
                v.wait_ge(out_ready, LAYERS * OUTS + b + 1)
                add_gated(2 * b, DOWN + b, 0, 2)
                op = add_gated(2 * b + 1, DOWN + b, 1, 2)
            op.then_inc(x_ready, 1)
            mod_norm(2, 1)
            v.wait_ge(route_ready, 1)
            for t in range(TT):
                step(nc.vector.tensor_tensor(lgt[:, t, :], ps[:, 3, t * EXPERTS:(t + 1) * EXPERTS], brouter[:, :], ALU.add))
                step(nc.vector.max(top8, lgt[:, t, :]))
                step(nc.vector.max_index(topi, top8, lgt[:, t, :]))
                step(nc.vector.tensor_copy(topf, topi[:, 0:TOPK]))
                nc.vector.tensor_scalar(small[:, 56:57], top8[:, 0:1], -1.0, None, ALU.mult).then_inc(top_ready, 1)
                v.wait_ge(topexp_ready, t + 1)
                step(nc.vector.reciprocal(small[:, 58:59], small[:, 57:58]))
                step(nc.vector.tensor_scalar(topw, topw, small[:, 58:59], None, ALU.mult))
                for k in range(TOPK):
                    nc.vector.tensor_scalar(sels[:, k, :], iota[:, 0:EXPERTS], topf[:, k:k + 1], None, ALU.is_equal)
                    op = nc.vector.tensor_scalar(eqs[:, k, :], iota[:, 0:EXPERTS], topf[:, k:k + 1], topw[:, k:k + 1], ALU.is_equal, ALU.mult)
                step(op)
                nc.vector.tensor_tensor(sels[:, 0:2, :], sels[:, 0:2, :], sels[:, 2:4, :], ALU.add)
                step(nc.vector.tensor_tensor(eqs[:, 0:2, :], eqs[:, 0:2, :], eqs[:, 2:4, :], ALU.add))
                nc.vector.tensor_tensor(sel[:, t, :], sels[:, 0, :], sels[:, 1, :], ALU.add)
                op = nc.vector.tensor_tensor(wt[:, t, :], eqs[:, 0, :], eqs[:, 1, :], ALU.add)
                if t < TT - 1:
                    step(op)
            op.then_inc(wt_ready, 1)
            v.wait_ge(ranks_ready, 1)
            rank_ps = ps[:, 2, 0:TT * EXPERTS].rearrange("p (t e) -> p t e", e=EXPERTS)
            step(nc.vector.scalar_tensor_tensor(out=rank[:, :, :], in0=rank_ps, scalar=float(CAP + 1), in1=sel[:, :, :], op0=ALU.add, op1=ALU.mult))
            nc.vector.tensor_scalar(rank[:, :, :], rank[:, :, :], -1.0, None, ALU.add)
            step(nc.vector.tensor_reduce(fullest[:, :], ps[:, 2, TT * EXPERTS:(TT + 1) * EXPERTS], AX.X, ALU.max))
            step(nc.vector.tensor_scalar(flagf[:, :], iota[:, 0:PASSES + 1], float(CAP), fullest[:, 0:1], ALU.mult, ALU.is_lt))
            nc.vector.tensor_copy(flags[:, :], flagf[:, :]).then_inc(flags_ready, 1)
            v.wait_ge(wtT_ready, 1)
            nc.vector.tensor_copy(wtT[0:EXPERTS, :], ps[0:EXPERTS, 3, 0:TOK]).then_inc(wtT_taken, 1)

            for i in range(2 * TT):
                v.wait_ge(bias_sums_ready, i + 1)
                op = nc.vector.tensor_copy(y_tok[:, i // 2, i % 2 * 512:i % 2 * 512 + 512], ps[:, 4 + i, :])
            step(op)

            moe = Steps(v, moe_step)

            def find_places(e):
                for t in range(TT):
                    op = nc.vector.tensor_scalar(place[:, t, :], iota, rank[:, t, bass.ds(e, 1)], None, ALU.is_equal)
                op.then_inc(place_ready, 1)

            def split_weights(n, j):
                for half in range(2):
                    u = 2 * j + half
                    v.wait_ge(whi_ready, n * UNITS_E + (u + 1))
                    nc.vector.tensor_tensor(w_lo[u % W_UNITS], slot(j)[:, half * UNIT:(half + 1) * UNIT], w_hi[u % W_UNITS].bitcast(F32),
                                            ALU.subtract).then_inc(wlo_ready, 1)

            def split_tokens(n):
                v.wait_ge(xhi_ready, n)
                nc.vector.tensor_tensor(xg[:, :, 1, :], ps[:, 2, 0:DC * CAP].rearrange("p (a b) -> p a b", b=CAP), xg[:, :, 0, :].bitcast(F32),
                                        ALU.subtract).then_inc(xg_taken, 1)

            def add_output(n, e, r):
                t, half = divmod(r, 2)
                v.wait_ge(scat_ready, n * (2 * TT) + (r + 1))
                ys = y_tok[:, t, half * 512:half * 512 + 512]
                nc.vector.scalar_tensor_tensor(out=ys, in0=ps[:, 6 + r % 2, :], scalar=wt[:, t, bass.ds(e, 1)], in1=ys, op0=ALU.mult,
                                               op1=ALU.add).then_inc(scat_added, 1)

            def expert_step(p, e, j, after=False, last=False):
                n = p * EXPERTS + e
                moe.base, moe.k = p * (EXPERTS * MOE_STEPS + 1) + e * MOE_STEPS + 1, 2 * j
                if j + 2 < DC:
                    split_weights(n, j + 2)
                elif not last:
                    split_weights(n + 1, j + 2 - DC)
                if j == DC - 2 and not last:
                    split_tokens(n + 2)
                if after:
                    for r in ((), (0,), (1,), (2, 3))[j]:
                        add_output(n - 1, e - 1, r)
                v.wait_ge(hid_ready, n * DC + (j + 1))
                nc.vector.tensor_scalar(lin[:, j % 2, :], ps[:, 3, CAP:2 * CAP], cols[:, bass.ds(e * 16 + (C_BEXP + DC + j), 1)], LIMIT, ALU.add, ALU.min)
                nc.vector.tensor_scalar(glu[:, j % 2, :], ps[:, 3, 0:CAP], cols[:, bass.ds(e * 16 + (C_BEXP + j), 1)], LIMIT, ALU.add, ALU.min).then_inc(glu_ready, 1)
                v.wait_ge(glu_ready, n * DC + (j + 1))
                moe(nc.vector.tensor_scalar(lin[:, j % 2, :], lin[:, j % 2, :], -LIMIT, 1.0, ALU.max, ALU.add))
                moe(nc.vector.tensor_tensor(lin[:, j % 2, :], lin[:, j % 2, :], glu[:, j % 2, :], ALU.mult))
                v.wait_ge(esig_ready, n * DC + (j + 1))
                nc.vector.tensor_tensor(eact[:, j % 4, :], lin[:, j % 2, :], sig[:, j % 2, :], ALU.mult).then_inc(eact_ready, 1)
                if j == HALF and not last:
                    v.wait_ge(placeT_ready, n + 1)
                    find_places(e + 1)

            v.wait_ge(flags_ready, 1)
            with v.Fori(0, PASSES) as p:
                needed = v.value_load(flags[0:1, bass.ds(p, 1)], min_val=0, max_val=1)
                with v.If(needed > 0):
                    n = p * EXPERTS
                    moe.base, moe.k = p * (EXPERTS * MOE_STEPS + 1), 0
                    moe(nc.vector.tensor_scalar(rank[:, :, :], rank[:, :, :], -float(CAP), None, ALU.add))
                    find_places(0)
                    split_weights(n, 0)
                    split_tokens(n + 1)
                    split_weights(n, 1)
                    for j in range(HALF):
                        expert_step(p, 0, j)
                    with v.Fori(0, EXPERTS - 1) as e:
                        for j in range(HALF, DC):
                            expert_step(p, e, j)
                        for j in range(HALF):
                            expert_step(p, e + 1, j, after=True)
                    for j in range(HALF, DC):
                        expert_step(p, EXPERTS - 1, j, last=True)
                    for r in range(2 * TT):
                        add_output(n + (EXPERTS - 1), EXPERTS - 1, r)
            v.drain().then_inc(y_ready, 1)
            v.wait_ge(yT_ready, 1)
            for c in range(DC):
                op = add_gated(c, DOWN + c // 2, c % 2, 5)
            op.then_inc(x_ready, 1)
            norm(LAYERS, 3, cols[:, C_NF:C_NF + DC], half_ready=True)

        @block.tensor
        def _(pe):
            mm_ = nc.tensor.matmul

            def sums(l, n, tiles=0):
                for c in range(DC):
                    if c % (DC // 2) == 0:
                        pe.wait_ge(sq_ready, l * (2 * NORMS) + (2 * n + c // (DC // 2) + 1))
                    mm = mm_(ps[:, SSUM, 0:TOK], ones, sq[:, c, :], start=c == 0, stop=c == DC - 1)
                    if c == 0 and tiles:
                        mm.then_inc(tile_used, tiles)
                mm.then_inc(ssum_ready, 1)

            def products(dst, hi, lo, x_hi, x_lo, first, last):
                mm_(dst, hi, x_hi, start=first, stop=False, skip_group_check=True)
                mm_(dst, hi, x_lo, start=False, stop=False, skip_group_check=True)
                return mm_(dst, lo, x_hi, start=False, stop=last, skip_group_check=True)

            def ffn_in(l, f, i, g=0):
                s = (i - 1) % 5
                for k in range(2):
                    pe.wait_ge(f_split[k], f_count(l, f, i, g))
                    for c in range(DC):
                        b = slice(c * P, (c + 1) * P)
                        if i == 0 and k == 0 and c % (DC // 2) == 0:
                            pe.wait_ge(h_ready, l * (2 * NORMS) + (4 * f + c // (DC // 2) + 1))
                        mm = products(ps[:, ff_banks[s], k * TOK:(k + 1) * TOK], f_hi[k][:, b], f_lo[k][:, b], h_hi[:, c, :], h_lo[:, c, :],
                                      c == 0, c == DC - 1)
                    mm.then_inc(f_used[k], 1)

            def ffn_down(l, f, t0, i, g=0):
                s = (i - 1) % 5
                pe.wait_ge(act_ready, f_count(l, f, i, g))
                t = t0 + i
                pe.wait_ge(tile_used, l * LAYER_TILES + g * 5 + (t + 1))
                for m in range(DC):
                    b = slice(m * P, (m + 1) * P)
                    mm = products(ps[:, DOWN + m // 2, m % 2 * TOK:(m % 2 + 1) * TOK], f_hi[2][:, b], f_lo[2][:, b], act_hi[:, s % 3, :],
                                  act_lo[:, s % 3, :], i == 0 and m % 2 == 0, i == FF_TILES - 1)
                mm.then_inc(down_done, 1)

            def ffn(l, f, t0):
                ffn_in(l, f, 0)
                ffn_in(l, f, 1)
                ffn_down(l, f, t0, 0)
                with pe.Fori(0, (FF_TILES - 2) // 5) as g:
                    for s in range(5):
                        ffn_in(l, f, 2 + s, g)
                        ffn_down(l, f, t0, 1 + s, g)
                ffn_down(l, f, t0, FF_TILES - 1)

            def project_t(w, bank, half, m=P, h_count=None):
                for c in range(DC):
                    if h_count is not None and c % (DC // 2) == 0:
                        pe.wait_ge(h_ready, h_count + c // (DC // 2))
                    mm = w.used(mm_(ps[0:m, bank, half * TOK:(half + 1) * TOK], w.take()[:, 0:m], h[:, c, :],
                                    start=c == 0, stop=c == DC - 1))
                return mm

            def project_tok(w, banks, n):
                for c in range(DC):
                    blk = w.take(n)
                    for t in range(TT):
                        mm = mm_(ps[:, banks[t], 0:n * P], h[:, c, t * P:(t + 1) * P], blk, start=c == 0, stop=c == DC - 1)
                        if t == TT - 1:
                            w.used(mm)
                        if c == DC - 1:
                            mm.then_inc(proj_ready, 1)

            def out_proj(w, src):
                for m in range(DC):
                    for c in range(DC):
                        mm = w.used(mm_(ps[:, DOWN + m // 2, m % 2 * TOK:(m % 2 + 1) * TOK], w.take(), src[:, c, :],
                                        start=c == 0, stop=c == DC - 1))
                    if m % 2:
                        mm.then_inc(out_ready, 1)

            pe.wait_ge(konst_landed, 16)
            pe.wait_ge(x_landed, 16)
            for i in range(OUTS):
                for c in range(2 * i, 2 * i + 2):
                    for t in range(TT):
                        mm = nc.tensor.transpose(ps[:, 4 + i, c % 2 * TOK + t * P:c % 2 * TOK + (t + 1) * P], x_tok[:, t, c * P:(c + 1) * P], ident)
                mm.then_inc(xt_ready, 1)
            pe.wait_ge(rel_landed, 2 * 16)
            for i in range(BIAS_HEADS):
                if i >= 4:
                    pe.wait_ge(vec_taken, i - 3)
                mm_(ps[:, i % 4, :], relb[0:BUCKETS + 1, i, :], onehot[0:BUCKETS + 1, min(i // DIL_SLOTS, DIL_GROUPS), :],
                    start=True, stop=True).then_inc(vec_ready, 1)
            pe.wait_ge(vec_taken, BIAS_HEADS)

            with pe.Fori(0, LAYERS) as l:
                sums(l, 0)
                ffn(l, 0, 0)
                sums(l, 1)
                w = Blocks(pe, l, MIX0)

                def free_bank(r):
                    if r >= 4:
                        pe.wait_ge(proj_taken, l * PROJ + r - 3)

                for r in range(QK_CHUNKS // 2):
                    free_bank(r)
                    project_t(w, r % 4, 0, h_count=l * (2 * NORMS) + 3 if r == 0 else None)
                    project_t(w, r % 4, 1).then_inc(proj_ready, 1)
                free_bank(8)
                project_tok(w, (7 % 4, 8 % 4), 4)
                free_bank(10)
                project_tok(w, (9 % 4, 10 % 4), 3)
                pe.wait_ge(proj_taken, l * PROJ + 11)

                def logits(u):
                    if u >= 2:
                        pe.wait_ge(scores_made, l * UNITS + u - 1)
                    b = 2 * (u % 2)
                    if u < DIL_UNITS:
                        s, qt = divmod(u, TT)
                        jobs = [(s, g, DIL_GROUPS + g) for g in range(DIL_GROUPS)]
                    else:
                        hh, qt = divmod(u - DIL_UNITS, TT)
                        jobs = [(m, 2 * DIL_GROUPS + hh, 2 * DIL_GROUPS + DIFF_HEADS + hh) for m in range(2)]
                    for i, (s, cq, ck) in enumerate(jobs):
                        rows = slice(s * DH, (s + 1) * DH)
                        col = 2 * i if u >= DIL_UNITS else i
                        mm = mm_(ps[:, b + col // 2, col % 2 * TOK:(col % 2 + 1) * TOK], qk[rows, cq, qt * P:(qt + 1) * P],
                                 qk[rows, ck, :], start=True, stop=True)
                    mm.then_inc(logits_ready, 1)

                def transposes(u):
                    pe.wait_ge(probs_ready, l * UNITS + u + 1)
                    if u >= 1:
                        pe.wait_ge(pt_taken, l * UNITS + u)
                    for i in range(6 if u < DIL_UNITS else 2):
                        mm = nc.tensor.transpose(ps[:, 4 + i // 4, i % 4 * P:(i % 4 + 1) * P], S[u % 3][:, i * P:(i + 1) * P], ident)
                    mm.then_inc(pt_ready, 1)

                def weighted_values(u):
                    pe.wait_ge(pt_taken, l * UNITS + u + 1)
                    if u < DIL_UNITS:
                        s, qt = divmod(u, TT)
                        for i in range(6):
                            hd = 2 * (i // 2) + s
                            mm = mm_(ps[s * DH:(s + 1) * DH, 6, qt * P:(qt + 1) * P], vb[:, i % 2, hd * DH:(hd + 1) * DH],
                                     PT[:, u % 2, i * P:(i + 1) * P], start=i == 0, stop=i == 5)
                        if u == DIL_UNITS - 1:
                            mm.then_inc(o_ready, 1)
                    else:
                        hh, qt = divmod(u - DIL_UNITS, TT)
                        if hh >= 1 and qt == 0:
                            pe.wait_ge(o_taken, l * 5 + hh)
                        for i in range(2):
                            mm = mm_(ps[:, 7 - hh % 2, qt * P:(qt + 1) * P], vc[:, i, hh * P:(hh + 1) * P],
                                     PT[:, u % 2, i * P:(i + 1) * P], start=i == 0, stop=i == 1)
                        if qt == 1:
                            mm.then_inc(o_ready, 1)

                for u in range(UNITS + 3):
                    if u < UNITS:
                        logits(u)
                    if 2 <= u < UNITS + 2:
                        transposes(u - 2)
                    if u >= 3:
                        weighted_values(u - 3)
                pe.wait_ge(scores_made, l * UNITS + UNITS)
                project_tok(w, (11 % 4, 12 % 4), 4)
                project_tok(w, (13 % 4, 14 % 4), 4)
                pe.wait_ge(osq_ready, l + 1)
                for i in range(2):
                    mm = mm_(ps[:, 6 + i, :], ones, sq[:, 2 * i:2 * i + 2, :], start=True, stop=True)
                mm.then_inc(ossum_ready, 1)
                pe.wait_ge(proj_taken, l * PROJ + PROJ)

                def dft_channels(g):
                    pe.wait_ge(dft1_taken, l * FOURIER_GROUPS + g + 1)
                    if g >= 2:
                        pe.wait_ge(dft2_taken, l * FOURIER_GROUPS + g - 1)
                    for i in range(2):
                        mm = mm_(ps[:, 2 + g % 2, 0:TOK], dch[:, i, :], dft1[:, g % 2, i * TOK:(i + 1) * TOK],
                                 start=i == 0, stop=i == 1)
                    mm.then_inc(dft2_ready, 1)

                for g in range(FOURIER_GROUPS):
                    if g >= 2:
                        pe.wait_ge(dft1_taken, l * FOURIER_GROUPS + g - 1)
                    for t in range(TT):
                        mm = mm_(ps[:, g % 2, :], a_tok[:, t, g * P:(g + 1) * P], dseq[:, t, :], start=t == 0, stop=t == TT - 1)
                    mm.then_inc(dft1_ready, 1)
                    if g >= 1:
                        dft_channels(g - 1)
                dft_channels(FOURIER_GROUPS - 1)
                pe.wait_ge(pt_taken, l * UNITS + UNITS)
                for m in range(DC):
                    b0 = 4 * (1 - m % 2)
                    if m == 1:
                        pe.wait_ge(dft2_taken, l * FOURIER_GROUPS + FOURIER_GROUPS)
                    if m >= 2:
                        pe.wait_ge(merged_ready, l * DC + m - 1)
                    for j in range(3):
                        mm = project_t(w, b0 + j // 2, j % 2)
                    mm.then_inc(gates_ready, 1)
                    if m == 0:
                        pe.wait_ge(dft2_taken, l * FOURIER_GROUPS + FOURIER_GROUPS)
                        pe.wait_ge(o_taken, l * 5 + 5)
                        pe.wait_ge(yc_ready, l + 1)
                    for c in range(FOURIER_GROUPS):
                        w.used(mm_(ps[:, b0 + 2, 0:TOK], w.take(), four[:, c, :], start=c == 0, stop=c == FOURIER_GROUPS - 1))
                    w.used(mm_(ps[:, b0 + 2, TOK:2 * TOK], w.take(), ob[:, :], start=True, stop=True))
                    for c in range(DIFF_HEADS):
                        mm = w.used(mm_(ps[:, b0 + 3, 0:TOK], w.take(), oc[:, c, :], start=c == 0, stop=c == DIFF_HEADS - 1))
                    mm.then_inc(ys_ready, 1)
                last = MIX0 + MIX_TILES
                for t in range(last, last + PAD_TILES):
                    pe.wait_ge(tile_landed[t % RING], (l * GROUPS + t // RING + 1) * 16)
                pe.wait_ge(merged_ready, l * DC + DC)
                out_proj(w, merged)
                sums(l, 2, PAD_TILES + 1)
                ffn(l, 1, FFN2)

            sums(LAYERS, 0)
            w = Blocks(pe, LAYERS, 0)
            pe.wait_ge(cact_ready, 1)
            for g in range(ADA // 4 + 1):
                if g < ADA // 4:
                    if g >= 2:
                        pe.wait_ge(row_taken, g - 1)
                    for c in range(DC):
                        mm = w.used(mm_(ps[0:1, g % 2, :], small[:, 16 + c:17 + c], w.take(4), start=c == 0, stop=c == DC - 1))
                    mm.then_inc(row_ready, 1)
                if g >= 1:
                    pe.wait_ge(row_taken, g)
                    for i in range(4):
                        m = 4 * (g - 1) + i
                        mm = mm_(ps[:, 3, m:m + 1], row[0:1, (g - 1) % 2, i * P:(i + 1) * P], ones[0:1, 0:1], start=True, stop=True)
            mm.then_inc(ada_ready, 1)
            sums(LAYERS, 1)
            pe.wait_ge(h_ready, 2 * (LAYERS * NORMS + 1))
            R0 = LAYERS * PROJ

            def free2(r):
                if r >= 4:
                    pe.wait_ge(proj_taken, R0 + r - 3)

            def project_pairs(r0, n):
                for r in range(r0, r0 + n):
                    free2(r)
                    project_t(w, r % 4, 0)
                    project_t(w, r % 4, 1).then_inc(proj_ready, 1)

            for i in range(2):
                free2(2 * i + 1)
                project_tok(w, (2 * i % 4, (2 * i + 1) % 4), 4)
            project_pairs(4, 8)
            for i in range(HEADS):
                if i >= 2:
                    pe.wait_ge(roped, i - 1)
                pe.wait_ge(proj_taken, R0 + 5 + i)
                mm_(ps[0:ROT, 4 + i % 2, :], rotT, mqk[0:ROT, 2 * i:2 * i + 2, :], start=True, stop=True).then_inc(rot_ready, 1)
            pe.wait_ge(roped, HEADS)
            U0 = LAYERS * UNITS
            for u in range(HEADS + 3):
                if u < HEADS:
                    if u >= 2:
                        pe.wait_ge(scores_made, U0 + u - 1)
                    q, k = mqk[:, u, :], mqk[:, HEADS + u, :]
                    mm_(ps[:, u % 2, 0:P], q[:, 0:P], k[:, 0:P], start=True, stop=True)
                    mm_(ps[:, u % 2, P:3 * P], q[:, P:TOK], k, start=True, stop=True).then_inc(logits_ready, 1)
                if 2 <= u < HEADS + 2:
                    pe.wait_ge(probs_ready, U0 + u - 1)
                    if u >= 3:
                        pe.wait_ge(pt_taken, U0 + u - 2)
                    for i in range(3):
                        mm = nc.tensor.transpose(ps[:, 4, i * P:(i + 1) * P], mS[(u - 2) % 3][:, i * P:(i + 1) * P], ident)
                    mm.then_inc(pt_ready, 1)
                if u >= 3:
                    hd = u - 3
                    pe.wait_ge(pt_taken, U0 + hd + 1)
                    if hd >= 2:
                        pe.wait_ge(o_taken, LAYERS * 5 + hd - 1)
                    vs = [mv[:, t, hd * P:(hd + 1) * P] for t in range(TT)]
                    pt = mPT[:, hd % 2, :]
                    mm_(ps[:, 6 + hd % 2, 0:P], vs[0], pt[:, 0:P], start=True, stop=True)
                    mm_(ps[:, 6 + hd % 2, P:TOK], vs[0], pt[:, P:2 * P], start=True, stop=False)
                    mm_(ps[:, 6 + hd % 2, P:TOK], vs[1], pt[:, 2 * P:3 * P], start=False, stop=True).then_inc(o_ready, 1)
            pe.wait_ge(scores_made, U0 + HEADS)
            project_pairs(12, 4)
            free2(16)
            project_t(w, 0, 0, RANK).then_inc(proj_ready, 1)
            project_pairs(17, 4)
            free2(22)
            project_tok(w, (21 % 4, 22 % 4), 4)
            free2(24)
            project_tok(w, (23 % 4, 24 % 4), 4)
            pe.wait_ge(pt_taken, U0 + HEADS)
            pe.wait_ge(proj_taken, R0 + 17)
            for hh in range(GLA_HEADS):
                mm = mm_(ps[:, 4 + hh // 2, hh % 2 * TOK:(hh % 2 + 1) * TOK], glaw[:, hh * P:(hh + 1) * P], glow[0:RANK, :], start=True, stop=True)
            mm.then_inc(z_ready, 1)
            pe.wait_ge(proj_taken, R0 + 25)
            pe.wait_ge(k_decayed, 1)
            pe.wait_ge(qk_decayed, 1)
            for hh in range(GLA_HEADS):
                mm = mm_(ps[:, 0, hh * P:(hh + 1) * P], kd[0][:, hh, 0:P], qd[0][:, hh, P:TOK], start=True, stop=True)
            mm.then_inc(lev_ready, 1)
            for i in range(1, len(LEVELS) + 2):
                if i <= len(LEVELS):
                    pe.wait_ge(k_decayed, i + 1)
                    pe.wait_ge(qk_decayed, i + 1)
                q, k = (qd[i % 2], kd[i % 2]) if i <= len(LEVELS) else (gqk[:, 0:GLA_HEADS], gqk[:, GLA_HEADS:])
                if i == 2:
                    pe.wait_ge(lev_taken, 1)
                if i >= 3:
                    pe.wait_ge(lev_taken, 1 + (i - 2) * TT)
                for t in range(TT):
                    for hh in range(GLA_HEADS):
                        mm = mm_(ps[:, 2 * (i % 2) + t, hh * P:(hh + 1) * P], k[:, hh, t * P:(t + 1) * P], q[:, hh, t * P:(t + 1) * P],
                                 start=True, stop=True)
                    mm.then_inc(lev_ready, 1)
            pe.wait_ge(scores_done, 1)
            for c in range(DC):
                hh = c // 2
                o = ps[:, 4 + c // 2, c % 2 * TOK:(c % 2 + 1) * TOK]
                vs = [gv[:, t, c * P:(c + 1) * P] for t in range(TT)]
                mm_(o[:, 0:P], vs[0], acc[:, 0, hh, :], start=True, stop=True)
                mm_(o[:, P:TOK], vs[0], off[:, hh, :], start=True, stop=False)
                mm = mm_(o[:, P:TOK], vs[1], acc[:, 1, hh, :], start=False, stop=True)
                if c % 2:
                    mm.then_inc(go_ready, 1)
            pe.wait_ge(osq_ready, LAYERS + 1)
            for hh in range(GLA_HEADS):
                for i in range(2):
                    mm = mm_(ps[:, hh // 2, hh % 2 * TOK:(hh % 2 + 1) * TOK], ones, sq[:, 2 * hh + i, :], start=i == 0, stop=i == 1)
            mm.then_inc(ossum_ready, 1)
            for m in range(DC):
                b0 = 2 + 2 * (m % 2)
                if m >= 2:
                    pe.wait_ge(merged_ready, LAYERS * DC + m - 1)
                project_t(w, b0, 0)
                project_t(w, b0, 1).then_inc(gates_ready, 1)
                for c in range(HEADS):
                    w.used(mm_(ps[:, b0 + 1, 0:TOK], w.take(), oa[:, c, :], start=c == 0, stop=c == DC - 1))
                if m == 0:
                    pe.wait_ge(gla_ready, 1)
                for c in range(DC):
                    mm = w.used(mm_(ps[:, b0 + 1, TOK:2 * TOK], w.take(), go[:, c, :], start=c == 0, stop=c == DC - 1))
                mm.then_inc(ys_ready, 1)
            pe.wait_ge(merged_ready, LAYERS * DC + DC)
            out_proj(w, merged2)
            sums(LAYERS, 2, 1)
            pe.wait_ge(h_ready, 2 * (LAYERS * NORMS + 2))
            for t in range(TT):
                for c in range(DC):
                    mm = mm_(ps[:, 3, t * EXPERTS:(t + 1) * EXPERTS], h[:, c, t * P:(t + 1) * P], router[:, c, :], start=c == 0, stop=c == DC - 1)
            mm.then_inc(route_ready, 1)
            for i in range(2 * TT):
                for c in range(4):
                    mm = nc.tensor.transpose(ps[:, 4 + i, c * P:(c + 1) * P], h[:, i % 2 * 4 + c, i // 2 * P:(i // 2 + 1) * P], ident)
                mm.then_inc(htok_ready, 1)
            pe.wait_ge(wt_ready, 1)
            for t in range(TT):
                mm = nc.tensor.transpose(ps[0:EXPERTS, 3, t * P:(t + 1) * P], wt[:, t, :], ident)
            mm.then_inc(wtT_ready, 1)
            for t in range(TT):
                cols_t = slice(t * EXPERTS, (t + 1) * EXPERTS)
                for k in range(t):
                    mm_(ps[:, 2, cols_t], ones, sel[:, k, :], start=k == 0, stop=False)
                mm_(ps[:, 2, cols_t], before, sel[:, t, :], start=t == 0, stop=True)
            for t in range(TT):
                mm = mm_(ps[:, 2, TT * EXPERTS:(TT + 1) * EXPERTS], ones, sel[:, t, :], start=t == 0, stop=t == TT - 1)
            mm.then_inc(ranks_ready, 1)
            pe.wait_ge(wtT_taken, 1)
            for i in range(2 * TT):
                pe.wait_ge(htok_taken, i + 1)
                mm_(ps[:, 4 + i, :], wtT[0:EXPERTS, i // 2 * P:(i // 2 + 1) * P], bout[:, i % 2 * 512:i % 2 * 512 + 512], start=True,
                    stop=True).then_inc(bias_sums_ready, 1)

            def gather(n):
                pe.wait_ge(place_ready, n)
                for c in range(DC):
                    for t in range(TT):
                        mm = mm_(ps[:, 2, c * CAP:(c + 1) * CAP], h_tok[:, t, c * P:(c + 1) * P], place[:, t, :], start=t == 0, stop=t == TT - 1)
                mm.then_inc(xg_ready, 1)

            def expert_in(n, j):
                if j == 0:
                    pe.wait_ge(xg_taken, n + 1)
                for i in range(2):
                    u = 2 * j + i
                    pe.wait_ge(wlo_ready, n * UNITS_E + (u + 1))
                    for c in range(DC // 2):
                        for part in (w_hi, w_lo):
                            mm = mm_(ps[0:2 * CAP, j % 2, 0:2 * P], xg[:, i * (DC // 2) + c, :, :], part[u % W_UNITS][:, c * 2 * P:(c + 1) * 2 * P],
                                     start=i == 0 and c == 0 and part is w_hi, stop=i == 1 and c == DC // 2 - 1 and part is w_lo)
                    mm.then_inc(w_used, 1)

            def turn(n, j, first=False):
                pe.wait_ge(htok_copied, n * DC + (j + 1))
                if not first:
                    pe.wait_ge(glu_ready, n * DC + j)
                for half in range(2):
                    mm = mm_(ps[:, 3, half * CAP:(half + 1) * CAP], hid_tok[0:2 * CAP, j % 2, half * P:(half + 1) * P], fold, start=True, stop=True)
                mm.then_inc(hid_ready, 1)

            def expert_out(n, j):
                pe.wait_ge(eact_ready, n * DC + (j + 1))
                for half in range(2):
                    b = 2 * DC * P + half * 512
                    mm = mm_(ps[0:CAP, 4 + half, :], eact[:, j % 4, :], slot(j)[:, b:b + 512], start=j == 0, stop=j == DC - 1)
                    if j == DC - 1 and half == 0:
                        mm.then_inc(eout_ready, 1)
                mm.then_inc(moe_used, 1)

            def back(n, r):
                t, half = divmod(r, 2)
                if r == 0:
                    pe.wait_ge(placeT_taken, n + 1)
                    pe.wait_ge(eout_taken, n * 2 + 2)
                if t > 0:
                    pe.wait_ge(scat_added, n * (2 * TT) + (r - 1))
                mm_(ps[:, 6 + r % 2, :], placeT[0:CAP, t * P:(t + 1) * P], outd[0:CAP, half * 512:half * 512 + 512], start=True,
                    stop=True).then_inc(scat_ready, 1)

            def expert_step(n, j, after=False, last=False):
                if j + 2 < DC:
                    expert_in(n, j + 2)
                elif not last:
                    expert_in(n + 1, j + 2 - DC)
                if j == HALF + 1 and not last:
                    pe.wait_ge(placeT_taken, n + 1)
                    gather(n + 2)
                if j + 1 < DC:
                    turn(n, j + 1)
                elif not last:
                    turn(n + 1, 0)
                if j == HALF:
                    for t in range(TT):
                        mm = nc.tensor.transpose(ps[0:CAP, 2, t * P:(t + 1) * P], place[:, t, :], ident)
                    mm.then_inc(placeT_ready, 1)
                if after:
                    for r in ((0,), (1,), (2, 3), ())[j]:
                        back(n - 1, r)
                expert_out(n, j)

            pe.wait_ge(flags_ready, 1)
            with pe.Fori(0, PASSES) as p:
                needed = pe.value_load(flags[0:1, bass.ds(p, 1)], min_val=0, max_val=1)
                with pe.If(needed > 0):
                    n = p * EXPERTS
                    gather(n + 1)
                    expert_in(n, 0)
                    expert_in(n, 1)
                    turn(n, 0, True)
                    for j in range(HALF):
                        expert_step(n, j)
                    with pe.Fori(0, EXPERTS - 1) as e:
                        for j in range(HALF, DC):
                            expert_step(p * EXPERTS + e, j)
                        for j in range(HALF):
                            expert_step(p * EXPERTS + e + 1, j, after=True)
                    for j in range(HALF, DC):
                        expert_step(n + (EXPERTS - 1), j, last=True)
                    for r in range(2 * TT):
                        back(n + (EXPERTS - 1), r)
            pe.wait_ge(y_ready, 1)
            for c in range(DC):
                for t in range(TT):
                    mm = nc.tensor.transpose(ps[:, DOWN + c // 2, c % 2 * TOK + t * P:c % 2 * TOK + (t + 1) * P], y_tok[:, t, c * P:(c + 1) * P], ident)
            mm.then_inc(yT_ready, 1)
            sums(LAYERS, 3)
            pe.wait_ge(h_ready, 2 * (LAYERS * NORMS + 3))
            for i in range(2 * OUTS):
                t, half = divmod(i, OUTS)
                if i >= 4:
                    pe.wait_ge(ytok_taken, i - 3)
                for c in range(2):
                    mm = nc.tensor.transpose(ps[:, i % 4, c * P:(c + 1) * P], h[:, 2 * half + c, t * P:(t + 1) * P], ident)
                mm.then_inc(ytok_ready, 1)


def constants():
    k = np.zeros((P, KONST), np.float32)
    k[:, K_ID:K_ID + P] = np.eye(P)
    k[:, K_ONES:K_ONES + TOK] = 1.0
    r = np.arange(P)
    tri = np.where(r[None, :] <= r[:, None], 0.0, NEG)
    k[:, K_CAUSAL:K_CAUSAL + 384] = np.concatenate([tri, np.zeros((P, P)), tri], 1)
    for i, s in enumerate(LEVELS):
        j, q = r[:, None], r[None, :]
        k[:, K_LEVEL + i * P:K_LEVEL + (i + 1) * P] = (j // (2 * s) == q // (2 * s)) & (j % (2 * s) < s) & (q % (2 * s) >= s)
    k[:, K_LEVEL + 7 * P:K_LEVEL + 8 * P] = np.eye(P)
    k[:, K_IOTA:K_IOTA + CAP] = np.arange(CAP)
    k[:, K_BEFORE:K_BEFORE + P] = r[:, None] < r[None, :]
    k[:, K_FOLD:K_FOLD + CAP] = r[:, None] % CAP == np.arange(CAP)
    k[:, K_EPS:K_EPS + 3] = (EPS1, EPS2, 1.0)
    ang = 2 * np.pi * np.outer(np.arange(TOK), np.arange(TOK)) / TOK
    seq = np.concatenate([np.cos(ang), np.sin(ang)], 1) / math.sqrt(TOK)
    k[:, K_DSEQ:K_DSEQ + 2 * VEC] = seq.reshape(TT, P, VEC).transpose(1, 0, 2).reshape(P, -1)
    ang = 2 * np.pi * np.outer(r, r) / P
    k[:, K_DCH:K_DCH + 2 * P] = np.concatenate([np.cos(ang), -np.sin(ang)], 1) / math.sqrt(P)
    half = ROT // 2
    freq = np.float32(500000.0) ** (-np.arange(half, dtype=np.float32) * np.float32(2.0) / np.float32(ROT))
    a = (np.arange(TOK, dtype=np.float32)[:, None] * freq[None, :]).T
    k[0:ROT, K_COS:K_COS + TOK] = np.cos(np.concatenate([a, a]))
    k[0:ROT, K_SIN:K_SIN + TOK] = np.sin(np.concatenate([a, a]))
    for i in range(half):
        k[half + i, K_ROT + i] = -1.0
        k[i, K_ROT + half + i] = 1.0
    return k


def bucket_tables():
    rel = np.arange(VEC) - (TOK - 1)
    half = BUCKETS // 2
    exact = half // 2
    n = np.abs(rel)
    nf = np.maximum(n, 1).astype(np.float32)
    large = exact + (np.log(nf / np.float32(exact)) / np.float32(math.log(MAX_DISTANCE / exact)) * np.float32(half - exact)).astype(np.int32)
    bucket = np.where(rel > 0, half, 0) + np.where(n < exact, n, np.minimum(large, half - 1))
    tables = np.zeros((BUCKETS + 1, 4, VEC), np.float32)
    for g in range(4):
        seen = np.ones(VEC, bool)
        if g < DIL_GROUPS:
            window, dil = DIL_PAIRS[g]
            seen = (n % dil == 0) & (n // dil <= window // (2 * dil))
        tables[bucket[seen], g, np.nonzero(seen)[0]] = 1.0
        tables[BUCKETS, g, ~seen] = NEG
    return tables


def by_output(w):
    k, n = w.shape
    return w.reshape(k // P, P, n // P, P).transpose(2, 0, 1, 3).reshape(-1, P, P)


def by_input(w, n):
    k, cols = w.shape
    return w.reshape(k // P, P, cols // (n * P), n, P).transpose(2, 0, 3, 1, 4).reshape(-1, P, P)


def tiles(blocks, n):
    b = np.concatenate(blocks)
    b = np.concatenate([b, np.zeros((n * TILE_BLOCKS - len(b), P, P), np.float32)])
    return b.reshape(n, TILE_BLOCKS, P, P).transpose(0, 2, 1, 3).reshape(n, P, TILE)


def ffn_tiles(gate, up, down):
    f = gate.shape[-1] // P
    t = np.empty((f, P, 3, DC, P), np.float32)
    t[:, :, 0] = gate.reshape(DC, P, f, P).transpose(2, 1, 0, 3)
    t[:, :, 1] = up.reshape(DC, P, f, P).transpose(2, 1, 0, 3)
    t[:, :, 2] = down.reshape(f, P, DC, P)
    return t.reshape(f, P, TILE)


def columns(v):
    v = np.asarray(v, np.float32).reshape(-1, P)
    return v.T


def lay_out(i):
    parts = []
    for l in range(LAYERS):
        parts.append(ffn_tiles(i["w_ffn1_gate"][l], i["w_ffn1_up"][l], i["w_ffn1_down"][l]))
        w_in = i["w_in"][l]
        qa, ka, va = (w_in[:, D + 384 * n:D + 384 * (n + 1)] for n in range(3))
        qc, kc, vcw = (w_in[:, 2176 + 512 * n:2176 + 512 * (n + 1)] for n in range(3))
        blocks = [by_output(w) for w in (qa, ka, qc, kc)] + [by_input(vcw, 4), by_input(va, 3), by_input(w_in[:, :D], 4)]
        gate = by_output(i["w_gate"][l]).reshape(3, DC, DC, P, P).transpose(1, 0, 2, 3, 4).reshape(DC, 3 * DC, P, P)
        branch = [by_output(i[n][l]).reshape(DC, -1, P, P) for n in ("w_br_a", "w_br_b", "w_br_c")]
        blocks += [np.concatenate([gate] + branch, 1).reshape(-1, P, P), by_output(i["w_out"][l])]
        parts.append(tiles(blocks, MIX_TILES + PAD_TILES))
        parts.append(ffn_tiles(i["w_ffn2_gate"][l], i["w_ffn2_up"][l], i["w_ffn2_down"][l]))
    w_in = i["w_in_2"][0]
    cut = np.cumsum([0, D, D, D, 512, 512, D, D, RANK, D, D])
    mq, mk, mvw, gq, gk, gvw, grw, low, ga, gb = (w_in[:, a:b] for a, b in zip(cut[:-1], cut[1:]))
    low = np.pad(low, ((0, 0), (0, P - RANK)))
    blocks = [by_input(i["w_ada_2"][0], 4), by_input(mvw, 4)] + [by_output(w) for w in (mq, mk, gq, gk, low, grw)] + [by_input(gvw, 4)]
    blocks.append(np.concatenate([by_output(w).reshape(DC, DC, P, P) for w in (ga, gb, i["w_o_moba_2"][0], i["w_o_gla_2"][0])], 1).reshape(-1, P, P))
    blocks.append(by_output(i["w_out_2"][0]))
    parts.append(tiles(blocks, SEC_TILES))
    w_exp = i["w_exp_in_2"][0]
    experts = np.empty((EXPERTS, DC, P, 3, DC, P), np.float32)
    ins = experts[:, :, :, 0:2].reshape(EXPERTS, DC, P, DC, 2, P)
    for half in range(2):
        ins[:, :, :, :, half] = w_exp[:, :, half::2].reshape(EXPERTS, DC, P, DC, P).transpose(0, 3, 2, 1, 4)
    experts[:, :, :, 0:2] = ins.reshape(EXPERTS, DC, P, 2, DC, P)
    experts[:, :, :, 2] = i["w_exp_out_2"][0].reshape(EXPERTS, DC, P, DC, P)

    layers = np.zeros((P, LAYERS, LP), np.float32)
    for l in range(LAYERS):
        lam_init = 0.8 - 0.6 * math.exp(-0.3 * l)
        layers[:, l, :LP_LAM] = np.concatenate([columns(i[n][l]) for n in ("g_ffn1", "g_mix", "g_ffn2", "b_gate", "subln_g")]
                                               + [np.full((P, 1), lam_init), np.full((P, 1), 1 - lam_init)], 1)
        layers[:, l, LP_LAM:] = np.concatenate([i[n][l] for n in ("lam_q1", "lam_k1", "lam_q2", "lam_k2")])[None]
    b_exp = i["b_exp_in_2"][0]
    b_exp = np.concatenate([b_exp[:, 0::2].reshape(EXPERTS, DC, P), b_exp[:, 1::2].reshape(EXPERTS, DC, P)], 1)
    cols = np.concatenate([columns(i[n]) for n in ("c_2", "g_final", "b_ada_2", "norm1_w_2", "gla_gate_b_2", "gla_norm_w_2", "b_merge_2",
                                                   "norm2_w_2", "final_norm_w_2")] + [columns(b_exp)], 1)
    relb = np.ones((BUCKETS + 1, BIAS_HEADS, P), np.float32)
    relb[:BUCKETS] = i["rel_bias"][:, :, None]
    return {
        "stream": np.concatenate(parts),
        "experts": experts.reshape(EXPERTS * DC, P, TILE),
        "x": i["x"].reshape(TOK, D),
        "konst": constants(),
        "layers": layers,
        "cols": cols,
        "relb": relb,
        "onehot": bucket_tables(),
        "glaw": i["gla_gate_w_2"][0],
        "router": i["w_router_2"][0].reshape(DC, P, EXPERTS).transpose(1, 0, 2),
        "brouter": np.broadcast_to(i["b_router_2"], (P, EXPERTS)),
        "bout": i["b_exp_out_2"][0],
    }


def kernel(**inputs):
    import concourse.bacc as bacc
    from concourse.bass_utils import run_bass_kernel_spmd

    arrays = {n: np.ascontiguousarray(a) for n, a in lay_out({k: np.asarray(v) for k, v in inputs.items()}).items()}
    nc = bacc.Bacc("TRN2", target_bir_lowering=False, num_devices=1)
    args = [nc.dram_tensor("in_" + n, a.shape, F32, kind="ExternalInput").ap() for n, a in arrays.items()]
    rows = nc.dram_tensor("bias_rows", (BIAS_HEADS, P, VEC), F32, kind="Internal").ap()
    out = nc.dram_tensor("out", (TOK, D), F32, kind="ExternalOutput").ap()
    build(nc, *args, rows, out)
    r = run_bass_kernel_spmd(nc, [{"in_" + n: a for n, a in arrays.items()}], core_ids=[0])
    return r.results[0]["out"].reshape(1, TOK, D)
```
